# Optimizing a Trainium2 kernel written in Bass

```python
import math
import jax, jax.numpy as jnp
from jax import lax
import numpy as np
import jax
import jax.numpy as jnp

D_MODEL = 1024
BATCH = 1
SEQ = 256
DEPTH = 2

HEAD_DIM = 64
MOBA_HEADS = D_MODEL // (2 * HEAD_DIM)
MOBA_BLOCK = 256
MOBA_TOPK = 3
NSA_HEADS = D_MODEL // (2 * HEAD_DIM)
NSA_KV_GROUPS = 2
NSA_HEADS_PER_GROUP = NSA_HEADS // NSA_KV_GROUPS
NSA_CMP_BLOCK = 32
NSA_CMP_STRIDE = 16
NSA_CMP_HIDDEN = 256
NSA_SLC_BLOCK = 64
NSA_TOPN = 16
NSA_WINDOW = 512
NSA_FORCE_SCORE = 1e6
FOX_HEADS = D_MODEL // HEAD_DIM
D_FF = 4 * D_MODEL
REL_BUCKETS = 32
REL_MAX_DISTANCE = 1024
QUERY_BLOCK = 128
SEQ_ALIGN = MOBA_BLOCK
RMS_EPS = 1e-5
NEG_INF = -1e30

MOBA_W = MOBA_HEADS * HEAD_DIM
NSA_W = NSA_HEADS * HEAD_DIM
NSA_KV_W = NSA_KV_GROUPS * HEAD_DIM
EVEN_SPLITS = (MOBA_W, MOBA_W, MOBA_W, NSA_W) + (NSA_KV_W,) * 6 + (3 * NSA_HEADS,)
EVEN_IN = sum(EVEN_SPLITS)
FOX_W = FOX_HEADS * HEAD_DIM
ODD_SPLITS = (FOX_W, FOX_W, FOX_W, FOX_HEADS)
ODD_IN = sum(ODD_SPLITS)
N_BIAS_HEADS = MOBA_HEADS + NSA_HEADS


def _split(t, sizes):
    offs = [int(o) for o in np.cumsum(sizes)[:-1]]
    return jnp.split(t, offs, axis=-1)

def rmsnorm(x, g):
    xf = x.astype(jnp.float32)
    y = xf * lax.rsqrt(jnp.mean(xf * xf, axis=-1, keepdims=True) + RMS_EPS)
    return (y * g.astype(jnp.float32)).astype(x.dtype)

def masked_softmax(logits, mask):
    logits = jnp.where(mask, logits.astype(jnp.float32), NEG_INF)
    p = jax.nn.softmax(logits, axis=-1)
    return p * jnp.any(mask, axis=-1, keepdims=True)

def rel_bucket(dist):
    n = jnp.maximum(dist, 0)
    max_exact = REL_BUCKETS // 2
    nf = jnp.maximum(n, 1).astype(jnp.float32)
    large = max_exact + (jnp.log(nf / max_exact) / math.log(REL_MAX_DISTANCE / max_exact)
                         * (REL_BUCKETS - max_exact)).astype(jnp.int32)
    large = jnp.minimum(large, REL_BUCKETS - 1)
    return jnp.where(n < max_exact, n, large)

def moba_nsa_mixer(h, w_in, w_out, rel_bias, cmp_pos_k, cmp_pos_v,
                   cmp_k_w1, cmp_k_w2, cmp_v_w1, cmp_v_w2):
    B, S, _ = h.shape
    S_pad = -(-S // SEQ_ALIGN) * SEQ_ALIGN
    hp = jnp.pad(h, ((0, 0), (0, S_pad - S), (0, 0)))
    mq, mk, mv, nq, kc, vc, ksl, vsl, kwn, vwn, gz = _split(hp @ w_in, EVEN_SPLITS)
    scale = HEAD_DIM ** -0.5
    Q = QUERY_BLOCK
    G, J = NSA_KV_GROUPS, NSA_HEADS_PER_GROUP
    n_qc = S_pad // Q
    f32 = jnp.float32

    n_mb = S_pad // MOBA_BLOCK
    k_moba = min(MOBA_TOPK, n_mb)
    mq = mq.reshape(B, S_pad, MOBA_HEADS, HEAD_DIM).transpose(0, 2, 1, 3)
    mk = mk.reshape(B, n_mb, MOBA_BLOCK, MOBA_HEADS, HEAD_DIM).transpose(0, 3, 1, 2, 4)
    mv = mv.reshape(B, n_mb, MOBA_BLOCK, MOBA_HEADS, HEAD_DIM).transpose(0, 3, 1, 2, 4)
    k_mean = jnp.mean(mk, axis=3)

    nq = nq.reshape(B, S_pad, NSA_HEADS, HEAD_DIM).transpose(0, 2, 1, 3)
    n_cmp = (S_pad - NSA_CMP_BLOCK) // NSA_CMP_STRIDE + 1
    cmp_idx = np.arange(n_cmp)[:, None] * NSA_CMP_STRIDE + np.arange(NSA_CMP_BLOCK)[None, :]
    cmp_end = jnp.asarray(cmp_idx[:, -1])

    def compress(raw, pos, w1, w2):
        blocks = raw.reshape(B, S_pad, G, HEAD_DIM)[:, cmp_idx] + pos[:, None, :]
        blocks = blocks.transpose(0, 3, 1, 2, 4).reshape(B, G, n_cmp, NSA_CMP_BLOCK * HEAD_DIM)
        return jax.nn.silu(blocks @ w1) @ w2

    k_cmp = compress(kc, cmp_pos_k, cmp_k_w1, cmp_k_w2)
    v_cmp = compress(vc, cmp_pos_v, cmp_v_w1, cmp_v_w2)
    n_sb = S_pad // NSA_SLC_BLOCK
    n_sel = min(NSA_TOPN, n_sb)
    k_slc = ksl.reshape(B, n_sb, NSA_SLC_BLOCK, G, HEAD_DIM).transpose(0, 3, 1, 2, 4)
    v_slc = vsl.reshape(B, n_sb, NSA_SLC_BLOCK, G, HEAD_DIM).transpose(0, 3, 1, 2, 4)
    pad_w = ((0, 0), (0, 0), (NSA_WINDOW, 0), (0, 0))
    k_win = jnp.pad(kwn.reshape(B, S_pad, G, HEAD_DIM).transpose(0, 2, 1, 3), pad_w)
    v_win = jnp.pad(vwn.reshape(B, S_pad, G, HEAD_DIM).transpose(0, 2, 1, 3), pad_w)
    gates = jax.nn.sigmoid(gz.reshape(B, S_pad, NSA_HEADS, 3).transpose(0, 2, 1, 3))
    ci = np.arange(n_cmp)[:, None] * NSA_CMP_STRIDE
    sj = np.arange(n_sb)[None, :] * NSA_SLC_BLOCK
    overlap = jnp.asarray(((ci < sj + NSA_SLC_BLOCK) & (ci + NSA_CMP_BLOCK > sj)).astype(np.float32))

    table = rel_bias.T
    tb_moba = table[:MOBA_HEADS]
    tb_nsa = table[MOBA_HEADS:].reshape(G, J, REL_BUCKETS)
    h_m = jnp.arange(MOBA_HEADS)[:, None, None]
    g_i = jnp.arange(G)[:, None, None]
    g5 = jnp.arange(G)[:, None, None, None, None]
    j5 = jnp.arange(J)[None, :, None, None, None]

    def query_block(bc):
        b, c = bc
        q0 = c * Q
        t = q0 + jnp.arange(Q)
        qm = lax.dynamic_slice_in_dim(mq[b], q0, Q, axis=1)
        mk_b, mv_b = mk[b], mv[b]
        blk = q0 // MOBA_BLOCK
        route = jnp.einsum('hqd,hnd->hqn', qm, k_mean[b]).astype(f32)
        route = jnp.where(jnp.arange(n_mb) < blk, route, NEG_INF)
        _, sel = lax.top_k(route, k_moba)
        sel_ok = sel < blk
        k_sel = mk_b[h_m, sel]
        v_sel = mv_b[h_m, sel]
        k_own = lax.dynamic_index_in_dim(mk_b, blk, axis=1, keepdims=False)
        v_own = lax.dynamic_index_in_dim(mv_b, blk, axis=1, keepdims=False)
        d_sel = t[:, None, None] - (sel[..., None] * MOBA_BLOCK + jnp.arange(MOBA_BLOCK))
        d_own = t[:, None] - (blk * MOBA_BLOCK + jnp.arange(MOBA_BLOCK))[None, :]
        s_sel = (jnp.einsum('hqd,hqnkd->hqnk', qm, k_sel).astype(f32) * scale
                 + tb_moba[h_m[..., None], rel_bucket(d_sel)])
        s_own = (jnp.einsum('hqd,hkd->hqk', qm, k_own).astype(f32) * scale
                 + tb_moba[:, rel_bucket(d_own)])
        n_k = k_moba * MOBA_BLOCK
        m_sel = jnp.broadcast_to(sel_ok[..., None], d_sel.shape).reshape(MOBA_HEADS, Q, n_k)
        m_own = jnp.broadcast_to((d_own >= 0)[None], s_own.shape)
        p = masked_softmax(jnp.concatenate([s_sel.reshape(MOBA_HEADS, Q, n_k), s_own], axis=-1),
                           jnp.concatenate([m_sel, m_own], axis=-1))
        o_a = (jnp.einsum('hqnk,hqnkd->hqd', p[..., :n_k].reshape(MOBA_HEADS, Q, k_moba, MOBA_BLOCK), v_sel)
               + jnp.einsum('hqk,hkd->hqd', p[..., n_k:], v_own))
        qn = lax.dynamic_slice_in_dim(nq[b], q0, Q, axis=1).reshape(G, J, Q, HEAD_DIM)
        d_cmp = t[:, None] - cmp_end[None, :]
        s_cmp = (jnp.einsum('gjqd,gnd->gjqn', qn, k_cmp[b]).astype(f32) * scale
                 + tb_nsa[:, :, rel_bucket(d_cmp)])
        p_cmp = masked_softmax(s_cmp, (d_cmp >= 0)[None, None])
        o_cmp = jnp.einsum('gjqn,gnd->gjqd', p_cmp, v_cmp[b])
        imp = jnp.einsum('gjqn,nm->gqm', p_cmp, overlap)
        s_blk = t // NSA_SLC_BLOCK
        jb = jnp.arange(n_sb)[None, :]
        forced = (jb == 0) | (jb == s_blk[:, None]) | (jb == s_blk[:, None] - 1)
        imp = jnp.where(forced, imp + NSA_FORCE_SCORE, jnp.where(jb <= s_blk[:, None], imp, NEG_INF))
        _, sidx = lax.top_k(imp, n_sel)
        k_s = k_slc[b][g_i, sidx]
        v_s = v_slc[b][g_i, sidx]
        d_s = t[:, None, None] - (sidx[..., None] * NSA_SLC_BLOCK + jnp.arange(NSA_SLC_BLOCK))
        m_s = (d_s >= 0) & (sidx <= s_blk[:, None])[..., None]
        s_s = (jnp.einsum('gjqd,gqnkd->gjqnk', qn, k_s).astype(f32) * scale
               + tb_nsa[g5, j5, rel_bucket(d_s)[:, None]])
        n_ks = n_sel * NSA_SLC_BLOCK
        p_s = masked_softmax(s_s.reshape(G, J, Q, n_ks), m_s.reshape(G, 1, Q, n_ks))
        o_slc = jnp.einsum('gjqnk,gqnkd->gjqd', p_s.reshape(G, J, Q, n_sel, NSA_SLC_BLOCK), v_s)
        k_w = lax.dynamic_slice_in_dim(k_win[b], q0, Q + NSA_WINDOW, axis=1)
        v_w = lax.dynamic_slice_in_dim(v_win[b], q0, Q + NSA_WINDOW, axis=1)
        pos_w = q0 - NSA_WINDOW + jnp.arange(Q + NSA_WINDOW)
        d_w = t[:, None] - pos_w[None, :]
        m_w = (d_w >= 0) & (d_w < NSA_WINDOW) & (pos_w >= 0)[None, :]
        s_w = (jnp.einsum('gjqd,gkd->gjqk', qn, k_w).astype(f32) * scale
               + tb_nsa[:, :, rel_bucket(d_w)])
        p_w = masked_softmax(s_w, m_w[None, None])
        o_win = jnp.einsum('gjqk,gkd->gjqd', p_w, v_w)
        g = lax.dynamic_slice_in_dim(gates[b], q0, Q, axis=1).astype(f32)
        o_b = (g[..., 0:1] * o_cmp.reshape(NSA_HEADS, Q, HEAD_DIM)
               + g[..., 1:2] * o_slc.reshape(NSA_HEADS, Q, HEAD_DIM)
               + g[..., 2:3] * o_win.reshape(NSA_HEADS, Q, HEAD_DIM))
        return jnp.concatenate([o_a.astype(f32), o_b.astype(f32)], axis=0)

    b_idx = jnp.repeat(jnp.arange(B), n_qc)
    c_idx = jnp.tile(jnp.arange(n_qc), B)
    o = lax.map(query_block, (b_idx, c_idx))
    o = o.reshape(B, n_qc, MOBA_HEADS + NSA_HEADS, Q, HEAD_DIM).transpose(0, 1, 3, 2, 4)
    o = o.reshape(B, S_pad, MOBA_W + NSA_W)[:, :S]
    return o.astype(h.dtype) @ w_out

def fox_mixer(h, w_in, b_forget, w_out):
    B, S, _ = h.shape
    Q = QUERY_BLOCK
    scale = HEAD_DIM ** -0.5
    q, k, v, fz = _split(h @ w_in, ODD_SPLITS)
    q = q.reshape(B, S, FOX_HEADS, HEAD_DIM).transpose(0, 2, 1, 3)
    k = k.reshape(B, S, FOX_HEADS, HEAD_DIM).transpose(0, 2, 1, 3)
    v = v.reshape(B, S, FOX_HEADS, HEAD_DIM).transpose(0, 2, 1, 3)
    log_f = jax.nn.log_sigmoid((fz + b_forget).astype(jnp.float32))
    cum = jnp.cumsum(log_f, axis=1).transpose(0, 2, 1)
    key_pos = jnp.arange(S)

    def block(c):
        q0 = c * Q
        qc = lax.dynamic_slice_in_dim(q, q0, Q, axis=2)
        cq = lax.dynamic_slice_in_dim(cum, q0, Q, axis=2)
        t = q0 + jnp.arange(Q)
        s = (jnp.einsum('bhqd,bhkd->bhqk', qc, k).astype(jnp.float32) * scale
             + cq[..., None] - cum[:, :, None, :])
        p = masked_softmax(s, key_pos[None, :] <= t[:, None])
        return jnp.einsum('bhqk,bhkd->bhqd', p, v).astype(jnp.float32)

    o = lax.map(block, jnp.arange(S // Q))
    o = o.transpose(1, 0, 3, 2, 4).reshape(B, S, FOX_W)
    return o.astype(h.dtype) @ w_out

def sqrelu_mlp(h, w1, w2):
    a = jax.nn.relu(h @ w1)
    return (a * a) @ w2

def first_inputs(seed: int = 0) -> dict:
    key = jax.random.key(seed)
    ks = jax.random.split(key, 20)
    f32 = jnp.float32

    def nrm(k, shape, scale):
        return jax.random.normal(k, shape, f32) * scale

    n_even = (DEPTH + 1) // 2
    n_odd = DEPTH // 2
    cmp_in = NSA_CMP_BLOCK * HEAD_DIM
    return {
        'x': nrm(ks[0], (BATCH, SEQ, D_MODEL), 1.0),
        'rel_bias': nrm(ks[1], (REL_BUCKETS, N_BIAS_HEADS), 0.5),
        'mix_norm': 1.0 + nrm(ks[2], (DEPTH, D_MODEL), 0.02),
        'mlp_norm': 1.0 + nrm(ks[3], (DEPTH, D_MODEL), 0.02),
        'even_w_in': nrm(ks[4], (n_even, D_MODEL, EVEN_IN), D_MODEL ** -0.5),
        'even_w_out': nrm(ks[5], (n_even, MOBA_W + NSA_W, D_MODEL), (MOBA_W + NSA_W) ** -0.5),
        'cmp_pos_k': nrm(ks[6], (n_even, NSA_CMP_BLOCK, HEAD_DIM), 0.2),
        'cmp_pos_v': nrm(ks[7], (n_even, NSA_CMP_BLOCK, HEAD_DIM), 0.2),
        'cmp_k_w1': nrm(ks[8], (n_even, cmp_in, NSA_CMP_HIDDEN), cmp_in ** -0.5),
        'cmp_k_w2': nrm(ks[9], (n_even, NSA_CMP_HIDDEN, HEAD_DIM), NSA_CMP_HIDDEN ** -0.5),
        'cmp_v_w1': nrm(ks[10], (n_even, cmp_in, NSA_CMP_HIDDEN), cmp_in ** -0.5),
        'cmp_v_w2': nrm(ks[11], (n_even, NSA_CMP_HIDDEN, HEAD_DIM), NSA_CMP_HIDDEN ** -0.5),
        'odd_w_in': nrm(ks[12], (n_odd, D_MODEL, ODD_IN), D_MODEL ** -0.5),
        'odd_b_forget': 3.0 + nrm(ks[13], (n_odd, FOX_HEADS), 0.5),
        'odd_w_out': nrm(ks[14], (n_odd, FOX_W, D_MODEL), FOX_W ** -0.5),
        'mlp_w1': nrm(ks[15], (DEPTH, D_MODEL, D_FF), D_MODEL ** -0.5),
        'mlp_w2': nrm(ks[16], (DEPTH, D_FF, D_MODEL), D_FF ** -0.5),
        'final_norm': 1.0 + nrm(ks[17], (D_MODEL,), 0.02),
    }

def first_block(x, rel_bias, mix_norm, mlp_norm, even_w_in, even_w_out, cmp_pos_k, cmp_pos_v,
              cmp_k_w1, cmp_k_w2, cmp_v_w1, cmp_v_w2, odd_w_in, odd_b_forget, odd_w_out,
              mlp_w1, mlp_w2, final_norm):
    h = x
    for layer in range(DEPTH):
        hn = rmsnorm(h, mix_norm[layer])
        i = layer // 2
        if layer % 2 == 0:
            h = h + moba_nsa_mixer(hn, even_w_in[i], even_w_out[i], rel_bias,
                                   cmp_pos_k[i], cmp_pos_v[i], cmp_k_w1[i], cmp_k_w2[i],
                                   cmp_v_w1[i], cmp_v_w2[i])
        else:
            h = h + fox_mixer(hn, odd_w_in[i], odd_b_forget[i], odd_w_out[i])
        h = h + sqrelu_mlp(rmsnorm(h, mlp_norm[layer]), mlp_w1[layer], mlp_w2[layer])
    return rmsnorm(h, final_norm)


DEPTH_2 = 1

D_MIX = D_MODEL
D_POOL = D_MIX // 2
D_ATTN = D_MIX - D_POOL
POOL_WINDOWS = (2, 4, 8, 16)
N_POOL_GROUPS = len(POOL_WINDOWS)
POOL_GROUP_DIM = D_POOL // N_POOL_GROUPS
N_HEADS = D_ATTN // HEAD_DIM
DILATION_PAIRS = ((128, 1), (512, 4), (2048, 16))
Q_BLOCK = 128
D_PROJ_IN = D_POOL + 3 * D_ATTN
D_FF_2 = 2816
N_MOD = 9
EPS = 1e-6


def rmsnorm_2(x, g):
    xf = x.astype(jnp.float32)
    y = xf * lax.rsqrt(jnp.mean(xf * xf, axis=-1, keepdims=True) + EPS)
    return (y * g.astype(jnp.float32)).astype(x.dtype)

def modulate(n, shift, scale):
    return n * (1 + scale) + shift

def swiglu(n, w_gate, w_up, w_down):
    return (jax.nn.silu(n @ w_gate) * (n @ w_up)) @ w_down

def alibi_slopes(n_heads):
    return jnp.exp2(-8.0 * jnp.arange(1, n_heads + 1, dtype=jnp.float32) / n_heads)

def multiscale_pool(u, w_pool, pool_scale):
    B, S, C = u.shape
    uf = u.astype(jnp.float32)
    cs0 = jnp.pad(jnp.cumsum(uf, axis=1), ((0, 0), (1, 0), (0, 0)))
    t = jnp.arange(S)
    groups = []
    for g, w in enumerate(POOL_WINDOWS):
        sl = slice(g * POOL_GROUP_DIM, (g + 1) * POOL_GROUP_DIM)
        csg = cs0[..., sl]
        lower = jnp.pad(csg[:, :S + 1 - w], ((0, 0), (w - 1, 0), (0, 0)))
        count = jnp.minimum(t + 1, w).astype(jnp.float32)[None, :, None]
        mean = (csg[:, 1:] - lower) / count
        groups.append(mean - uf[..., sl])
    pooled = jnp.stack(groups, axis=2)
    y = jnp.einsum('bsgc,gcd->bsgd', pooled, w_pool.astype(jnp.float32)).reshape(B, S, C)
    return (y * pool_scale.astype(jnp.float32)).astype(u.dtype)

def dilated_attention(q, k, v):
    B, S, H, Dh = q.shape
    n_blk = S // Q_BLOCK
    slopes = alibi_slopes(H)
    scale = Dh ** -0.5

    def block(i):
        t0 = i * Q_BLOCK
        t = t0 + jnp.arange(Q_BLOCK)
        qb = lax.dynamic_slice_in_dim(q, t0, Q_BLOCK, axis=1).astype(jnp.float32) * scale
        mxs, dens, nums = [], [], []
        for window, dil in DILATION_PAIRS:
            dist = dil * jnp.arange(window // dil + 1)
            idx = t[:, None] - dist[None, :]
            valid = idx >= 0
            idx = jnp.maximum(idx, 0)
            kg = jnp.take(k, idx, axis=1).astype(jnp.float32)
            vg = jnp.take(v, idx, axis=1).astype(jnp.float32)
            s = jnp.einsum('bqhd,bqjhd->bqhj', qb, kg)
            s = s - slopes[:, None] * dist.astype(jnp.float32)[None, :]
            s = jnp.where(valid[None, :, None, :], s, -jnp.inf)
            mx = jnp.max(s, axis=-1)
            p = jnp.exp(s - mx[..., None])
            dens.append(jnp.sum(p, axis=-1))
            nums.append(jnp.einsum('bqhj,bqjhd->bqhd', p, vg))
            mxs.append(mx)
        m_all = jnp.stack(mxs)
        w_r = jnp.exp(m_all - jnp.max(m_all, axis=0))
        num = sum(w_r[r][..., None] * nums[r] for r in range(len(DILATION_PAIRS)))
        den = sum(w_r[r] * dens[r] for r in range(len(DILATION_PAIRS)))
        return (num / den[..., None]).astype(q.dtype)

    out = lax.map(block, jnp.arange(n_blk))
    return jnp.moveaxis(out, 0, 1).reshape(B, S, H, Dh)

def hybrid_mixer(n, w_in, w_pool, pool_scale, w_out):
    B, S, _ = n.shape
    z = n @ w_in
    u, q, k, v = jnp.split(z, [D_POOL, D_POOL + D_ATTN, D_POOL + 2 * D_ATTN], axis=-1)
    y_pool = multiscale_pool(u, w_pool, pool_scale)
    hs = (B, S, N_HEADS, HEAD_DIM)
    y_attn = dilated_attention(q.reshape(hs), k.reshape(hs), v.reshape(hs)).reshape(B, S, D_ATTN)
    return jnp.concatenate([y_pool, y_attn], axis=-1) @ w_out

def second_inputs(seed: int = 0) -> dict:
    key = jax.random.key(seed)
    ks = jax.random.split(key, 20)
    f32 = jnp.float32
    L, D = DEPTH_2, D_MODEL

    def nrm(k, shape, fan_in, mult=1.0):
        return jax.random.normal(k, shape, f32) * (mult * fan_in ** -0.5)

    def gain(k, shape):
        return 1.0 + 0.05 * jax.random.normal(k, shape, f32)

    return {
        "x": jax.random.normal(ks[0], (BATCH, SEQ, D), f32),
        "c": jax.random.normal(ks[1], (BATCH, D), f32),
        "w_ada": nrm(ks[2], (L, D, N_MOD * D), D, 0.5),
        "b_ada": 0.02 * jax.random.normal(ks[3], (L, N_MOD * D), f32),
        "g_ffn1": gain(ks[4], (L, D)),
        "w1_gate": nrm(ks[5], (L, D, D_FF_2), D),
        "w1_up": nrm(ks[6], (L, D, D_FF_2), D),
        "w1_down": nrm(ks[7], (L, D_FF_2, D), D_FF_2),
        "g_mix": gain(ks[8], (L, D)),
        "w_in": nrm(ks[9], (L, D, D_PROJ_IN), D),
        "w_pool": nrm(ks[10], (L, N_POOL_GROUPS, POOL_GROUP_DIM, POOL_GROUP_DIM), POOL_GROUP_DIM),
        "pool_scale": gain(ks[11], (L, D_POOL)),
        "w_out": nrm(ks[12], (L, D_MIX, D), D_MIX),
        "g_ffn2": gain(ks[13], (L, D)),
        "w2_gate": nrm(ks[14], (L, D, D_FF_2), D),
        "w2_up": nrm(ks[15], (L, D, D_FF_2), D),
        "w2_down": nrm(ks[16], (L, D_FF_2, D), D_FF_2),
        "g_final": gain(ks[17], (D,)),
    }

def second_block(x, c, w_ada, b_ada, g_ffn1, w1_gate, w1_up, w1_down, g_mix, w_in, w_pool,
              pool_scale, w_out, g_ffn2, w2_gate, w2_up, w2_down, g_final):
    h = x
    for l in range(DEPTH_2):
        mod = (jax.nn.silu(c) @ w_ada[l] + b_ada[l])[:, None, :]
        sh1, sc1, gt1, sh2, sc2, gt2, sh3, sc3, gt3 = jnp.split(mod, N_MOD, axis=-1)
        n = modulate(rmsnorm_2(h, g_ffn1[l]), sh1, sc1)
        h = h + 0.5 * gt1 * swiglu(n, w1_gate[l], w1_up[l], w1_down[l])
        n = modulate(rmsnorm_2(h, g_mix[l]), sh2, sc2)
        h = h + gt2 * hybrid_mixer(n, w_in[l], w_pool[l], pool_scale[l], w_out[l])
        n = modulate(rmsnorm_2(h, g_ffn2[l]), sh3, sc3)
        h = h + 0.5 * gt3 * swiglu(n, w2_gate[l], w2_up[l], w2_down[l])
    return rmsnorm_2(h, g_final)


def setup_inputs(seed=0):
    out = dict(first_inputs(seed))
    for name, value in second_inputs(seed + 1).items():
        if name != "x":
            out[name + "_2"] = value
    return out


def reference(
    x, rel_bias, mix_norm, mlp_norm, even_w_in, even_w_out, cmp_pos_k, cmp_pos_v, cmp_k_w1,
    cmp_k_w2, cmp_v_w1, cmp_v_w2, odd_w_in, odd_b_forget, odd_w_out, mlp_w1, mlp_w2, final_norm,
    c_2, w_ada_2, b_ada_2, g_ffn1_2, w1_gate_2, w1_up_2, w1_down_2, g_mix_2, w_in_2, w_pool_2,
    pool_scale_2, w_out_2, g_ffn2_2, w2_gate_2, w2_up_2, w2_down_2, g_final_2,
):
    x = first_block(
        x, rel_bias, mix_norm, mlp_norm, even_w_in, even_w_out, cmp_pos_k, cmp_pos_v, cmp_k_w1,
        cmp_k_w2, cmp_v_w1, cmp_v_w2, odd_w_in, odd_b_forget, odd_w_out, mlp_w1, mlp_w2,
        final_norm,
    )
    return second_block(
        x, c_2, w_ada_2, b_ada_2, g_ffn1_2, w1_gate_2, w1_up_2, w1_down_2, g_mix_2, w_in_2,
        w_pool_2, pool_scale_2, w_out_2, g_ffn2_2, w2_gate_2, w2_up_2, w2_down_2, g_final_2,
    )


_drawn_inputs = setup_inputs


def setup_inputs(seed=0):
    import zlib

    import numpy as np

    out = dict(_drawn_inputs(seed))
    spreads = {}
    factors = {'mix_norm': 5.207,
     'cmp_pos_k': 8.0,
     'final_norm': 2.842,
     'b_ada_2': 2.908,
     'g_ffn1_2': 7.293,
     'g_mix_2': 4.866,
     'pool_scale_2': 6.509,
     'g_ffn2_2': 7.564}
    for name, (base, spread) in spreads.items():
        noise = np.random.default_rng([zlib.crc32(name.encode()), seed]).standard_normal(out[name].shape)
        drawn = base * np.exp(spread * noise) if base else spread * noise
        out[name] = jnp.asarray(drawn.astype(out[name].dtype))
    for name, factor in factors.items():
        out[name] = (out[name] * factor).astype(out[name].dtype)
    return out
```

```python
from contextlib import ExitStack

import numpy as np

import concourse.bass as bass
from concourse import mybir

F32 = mybir.dt.float32
F32R = mybir.dt.float32r
ALU = mybir.AluOpType
ACT = mybir.ActivationFunctionType
AX_X = mybir.AxisListType.X

P = 128
T = 256
TT = T // P
D = 1024
KT = D // P
HD = 64
HEADS = 8
UNIT = 2048
RING = 3
FF1 = 4096 // T
FF2 = 2816 // T
N_CMP = 15
V1W = 792
BIG = 1e30
SW = 384
REL = 2 * P + T - 1

PHASES = [
    ("qk_moba", 4), ("v_even", 4), ("q_nsa", 4), ("cmp", 4), ("out_even", 4), ("mlp0", 2 * FF1),
    ("qk_fox", 8), ("v_fox", 4), ("out_fox", 4), ("mlp1", 2 * FF1),
    ("glu0", 3 * FF2), ("qk_dil", 4), ("uv_dil", 4), ("out_dil", 4), ("glu1", 3 * FF2),
]
FIRST = {}
N_UNITS = 0
for _name, _n in PHASES:
    FIRST[_name] = N_UNITS
    N_UNITS += _n
ADA_UNITS = 36
ADA_W = 9 * D

COLS = {}
N_COLS = 0
for _name, _n in [("mix0", 8), ("mlp0", 8), ("mix1", 8), ("mlp1", 8), ("gf1", 8), ("gmix", 8), ("gf2", 8),
                  ("pool_scale", 4), ("pos", 32), ("c", 8), ("row_ok", 2), ("cmp_w2", 256),
                  ("w_pool", 512), ("w_forget", 128), ("ident", 128)]:
    COLS[_name] = N_COLS
    N_COLS += _n

ADA_SHIFT, ADA_SCALE, ADA_GATE = 0, 1, 2
SET_CMP, SET_MOBA, SET_SLC, SET_WIN, SET_FOX0, SET_FOX1, SET_DIL = range(7)


def build(nc, stream, ada, cols, x, rel_table, rel_pick, cmp_pick, fox_mask, dil_bias, pool_mat,
          b_ada, b_forget, final_norm, g_final, out):
    ctx = ExitStack()
    with ctx:
        base = [-(-nc.sbuf_base // 64) * 64]

        def place(name, shape, dt=F32, at=None):
            size = -(-int(np.prod(shape[1:])) * 4 // 64) * 64
            if at is None:
                at = base[0]
                base[0] += size
            t = nc.alloc_sbuf_tensor_at(name, list(shape), dt, offset=at)
            return t

        def sem(name):
            return ctx.enter_context(nc.semaphore(name))

        raw = place("raw", [P, RING, UNIT])
        w_hi = place("w_hi", [P, RING, UNIT], F32R)
        w_lo = place("w_lo", [P, RING, UNIT], F32R)
        a_hi = place("a_hi", [P, KT, T], F32R)
        a_lo = place("a_lo", [P, KT, T], F32R)
        turned = place("turned", [P, 2, 2 * T])
        h = place("h", [P, TT, D])
        tok_at = base[0]
        tok = place("tok", [P, TT, D])
        work = place("work", [P, 3072])
        qkv_at = base[0]
        qT = place("qT", [P, 8, T])
        kT = place("kT", [P, 8, T])
        V = place("V", [P, TT, D])
        hid_hi = place("hid_hi", [P, 3, 2 * T], F32R, at=qkv_at)
        hid_lo = place("hid_lo", [P, 3, 2 * T], F32R, at=qkv_at + 3 * 2 * T * 4)
        blk_hi = place("blk_hi", [P, 2, 16, 30], F32R, at=tok_at)
        blk_lo = place("blk_lo", [P, 2, 16, 30], F32R, at=tok_at + 4096)
        acc_ada = place("acc_ada", [P, ADA_W])
        ada_raw = place("ada_raw", [P, 2, D])
        row = place("row", [P, D])
        fmask = place("fmask", [P, T])
        par = place("par", [P, N_COLS])
        cmp_bias = place("cmp_bias", [P, 16, 16])
        kcmpT = place("kcmpT", [P, 16])
        vcmp = place("vcmp", [16, 2, HD])
        hidc = place("hidc", [P, 2, 2, 32])
        ones = place("ones", [P, P])
        low = place("low", [P, 7 * 16])
        den = place("den", [P, 7 * 16])
        wgt = place("wgt", [P, 7 * 16])
        gates = place("gates", [P, TT, 24])
        gates1 = place("gates1", [P, TT, 24])
        stat = place("stat", [P, 16, 2])
        modc = place("modc", [P, 9 * KT])
        gainc = place("gainc", [P, 3 * KT])
        silu_c = place("silu_c", [P, KT])
        wf_hi = place("wf_hi", [P, KT, 16], F32R)
        wf_lo = place("wf_lo", [P, KT, 16], F32R)
        fz = place("fz", [16, 4, T], at=tok_at)
        cum = place("cum", [16, 2, T])
        bfor = place("bfor", [16, 1])
        relt = place("relt", [33, 16])
        assert base[0] <= nc.sbuf_usable_end, (base[0], nc.sbuf_usable_end)
        rel_bias = acc_ada[:, 0:16 * T].rearrange("p (a b) -> p a b", a=16)
        dil_b = acc_ada[:, 0:2 * D].rearrange("p (a b) -> p a b", a=8)
        poolm = acc_ada[:, 3 * D:5 * D].rearrange("p (g k t) -> p g k t", g=4, k=2)
        rpick = V[0:33, 0, 0:REL]
        rrow = V[0:16, 1, 0:512]
        cpick = kT[0:33, :, :].rearrange("p a b -> p (a b)")
        cpick2 = qT[0:33, :, :].rearrange("p a b -> p (a b)")
        logit = work[:, 0:3 * SW].rearrange("p (b c) -> p b c", b=3)
        prob = work[:, 3 * SW:6 * SW].rearrange("p (b c) -> p b c", b=3)
        probT = work[:, 6 * SW:8 * SW].rearrange("p (b c) -> p b c", b=2)
        hid_act = work[:, 0:1536].rearrange("p (b c) -> p b c", b=3)
        hid_f = work[:, 1536:2048]
        pair = work[:, 0:1024].rearrange("p (v g t) -> p v g t", v=2, g=2)
        blk = work[:, 1024:1984].rearrange("p (v j n) -> p v j n", v=2, j=16)
        pcT = work[0:16, 0:2048].rearrange("p (a b) -> p a b", a=16)
        lc = work[:, 2048:2304].rearrange("p (a b) -> p a b", a=16)
        lcs = work[:, 2304:2560].rearrange("p (a b) -> p a b", a=16)
        pc = work[:, 2560:2816].rearrange("p (a b) -> p a b", a=16)

        def pc_(name, n, k=0):
            return par[:, COLS[name] + k:COLS[name] + k + n]

        ident = pc_("ident", P)
        cw2 = pc_("cmp_w2", 256).rearrange("p (v t d) -> p v t d", v=2, t=2)
        w_pool = pc_("w_pool", 512).rearrange("p (g d) -> p g d", g=4)
        wf = pc_("w_forget", 128).rearrange("p (k h) -> p k h", k=KT)

        ps = [ctx.enter_context(nc.psum_tensor(f"bank{i}", [P, 512], F32)) for i in range(8)]
        rel_dram = nc.dram_tensor("rel_scratch", (16, P, REL + 1), F32)

        par_landed = sem("par_landed")
        x_landed = sem("x_landed")
        pick_landed = sem("pick_landed")
        cpick_landed = sem("cpick_landed")
        raw_landed = [sem(f"raw_landed{i}") for i in range(RING)]
        hi_ready = sem("hi_ready")
        lo_ready = sem("lo_ready")
        unit_used = sem("unit_used")
        feat_taken = sem("feat_taken")
        acc_taken = sem("acc_taken")
        hid_ready = sem("hid_ready")
        h_ready = sem("h_ready")
        sumsq = sem("sumsq")
        rstd_guess = sem("rstd_guess")
        rows_scaled = sem("rows_scaled")
        bank_turned = sem("bank_turned")
        turned_ready = sem("turned_ready")
        act_split = sem("act_split")
        turned_free = sem("turned_free")
        dve_step = sem("dve_step")
        act_step = sem("act_step")
        pool_step = sem("pool_step")
        rel_rows = sem("rel_rows")
        rel_rows_sb = sem("rel_rows_sb")
        rel_stored = sem("rel_stored")
        rel_landed = sem("rel_landed")
        cbias_done = sem("cbias_done")
        cbias_taken = sem("cbias_taken")
        pairs_ready = sem("pairs_ready")
        blocks_ready = sem("blocks_ready")
        hidc_ready = sem("hidc_ready")
        ckv_done = sem("ckv_done")
        ckv_taken = sem("ckv_taken")
        cscores = sem("cscores")
        cshifted = sem("cshifted")
        cprobs = sem("cprobs")
        cprobsT = sem("cprobsT")
        cprobsT_sb = sem("cprobsT_sb")
        cpv = sem("cpv")
        gates_exp = sem("gates_exp")
        scores_done = sem("scores_done")
        logits_ready = sem("logits_ready")
        probs_ready = sem("probs_ready")
        probsT_done = sem("probsT_done")
        probsT_ready = sem("probsT_ready")
        pv_done = sem("pv_done")
        set_taken = sem("set_taken")
        wf_ready = sem("wf_ready")
        fz_done = sem("fz_done")
        fz_taken = sem("fz_taken")
        fz_exp = sem("fz_exp")
        cum_ready = sem("cum_ready")
        ada_landed = [sem("ada_landed0"), sem("ada_landed1")]
        bada_landed = sem("bada_landed")
        silu_ready = sem("silu_ready")
        ada_step = sem("ada_step")
        ada_done = sem("ada_done")
        mod_done = sem("mod_done")
        mod_taken = sem("mod_taken")
        gate_done = sem("gate_done")
        gate_taken = sem("gate_taken")
        gain_ready = sem("gain_ready")
        dil_landed = sem("dil_landed")
        row_landed = sem("row_landed")
        row_free = sem("row_free")
        pooled_done = sem("pooled_done")
        pooled_taken = sem("pooled_taken")
        out_ready = sem("out_ready")
        out_stored = sem("out_stored")

        heads = []
        for hh in range(HEADS):
            heads.append((SET_MOBA, hh, hh // 2, hh // 2, 64 * (hh % 2), hh * HD, rel_bias[:, hh, :]))
        for s, kt_, v0 in ((SET_SLC, 4, 512), (SET_WIN, 5, 640)):
            for hh in range(HEADS):
                g = hh // 4
                heads.append((s, hh, 4 + hh % 4, kt_, 64 * g, v0 + g * HD, rel_bias[:, 8 + hh, :]))
        for hh in range(2 * HEADS):
            heads.append((SET_FOX0 + hh // 8, hh % 8, hh // 2, hh // 2, 64 * (hh % 2), hh * HD, fmask[:, :]))
        for hh in range(HEADS):
            heads.append((SET_DIL, hh, hh // 2, hh // 2, 64 * (hh % 2), 512 + hh * HD, dil_b[:, hh, :]))
        EVEN = (0, 24)
        FOX = (24, 40)
        DIL = (40, 48)

        def set_banks(s):
            return (0, 1) if s % 2 == 0 else (2, 3)

        TURN = {n: 4 * i for i, n in enumerate(
            ["mix0", "even_out", "mlp0", "mix1", "fox_out", "mlp1", "gf1", "gmix", "dil_out", "gf2"])}
        NORM = {n: 2 * i for i, n in enumerate(
            ["mix0", "mlp0", "mix1", "mlp1", "final", "gf1", "gmix", "gf2", "last"])}
        EPS = {n: (1e-5 if n in ("mix0", "mlp0", "mix1", "mlp1", "final") else 1e-6) for n in NORM}
        N_PAR_LOADS = 6

        feat_before = {}
        n = 0
        for name, k in (("qk_moba", 4), ("q_nsa", 4), ("mlp0", FF1), ("qk_fox", 8), ("mlp1", FF1),
                        ("glu0", FF2), ("qk_dil", 4), ("glu1", FF2)):
            feat_before[name] = n
            n += k
        acc_before = {n: 4 * i for i, n in enumerate(
            ["v_even", "out_even", "mlp0", "v_fox", "out_fox", "mlp1", "glu0", "uv_dil", "out_dil", "glu1"])}
        hid_before = {"mlp0": 0, "mlp1": FF1, "glu0": 2 * FF1, "glu1": 2 * FF1 + FF2}

        block = ctx.enter_context(nc.Block())

        @block.sync
        def _(sp):
            for t in range(TT):
                sp.dma_start(h[:, t, :], x[t * P:(t + 1) * P, :]).then_inc(x_landed, 16)
            sp.dma_start(par[:, :], cols[:, :]).then_inc(par_landed, 16)
            for u in range(RING):
                sp.dma_start(raw[:, u, :], stream[u]).then_inc(raw_landed[u], 16)
            with sp.Fori(1, N_UNITS // RING) as i:
                for s in range(RING):
                    sp.wait_ge(lo_ready, i * RING + (s - RING + 1))
                    sp.dma_start(raw[:, s, :], stream[i * RING + s]).then_inc(raw_landed[s], 16)
            for u in range(N_UNITS - N_UNITS % RING, N_UNITS):
                sp.wait_ge(lo_ready, u - RING + 1)
                sp.dma_start(raw[:, u % RING, :], stream[u]).then_inc(raw_landed[u % RING], 16)
            sp.wait_ge(out_ready, 2)
            sp.dma_start(out.rearrange("(t p) d -> p t d", p=P), tok[:, :, :]).then_inc(out_stored, 16)
            sp.wait_ge(out_stored, 16)

        @block.gpsimd
        def _(pool):
            pool.memset(ones[:, :], 1.0).then_inc(pool_step, 1)
            pool.wait_ge(pool_step, 1)
            pool.memset(relt[32:33, :], 1.0).then_inc(pool_step, 1)
            pool.wait_ge(logits_ready, EVEN[1])
            pool.memset(acc_ada[:, :], 0.0).then_inc(pool_step, 1)
            for s in range(2):
                pool.dma_start(ada_raw[:, s, :], ada[s]).then_inc(ada_landed[s], 16)
            pool.wait_ge(pool_step, 3)
            pool.dma_start(acc_ada[0:1, :], b_ada).then_inc(bada_landed, 16)
            pool.wait_ge(bada_landed, 16)
            pool.wait_ge(silu_ready, 1)
            n_ada = 2 * ADA_UNITS
            for nb in range(9):
                for k in range(KT):
                    v = KT * nb + k
                    s = v % 2
                    part = ada_raw[:, s, :]
                    pool.wait_ge(ada_landed[s], 16 * (v // 2 + 1))
                    pool.tensor_scalar(part, part, silu_c[:, k:k + 1], 1.0, ALU.mult, ALU.mult).then_inc(ada_step, 1)
                    pool.wait_ge(ada_step, 2 * v + 1)
                    acc = acc_ada[:, nb * D:(nb + 1) * D]
                    pool.tensor_tensor(acc, acc, part, ALU.add).then_inc(ada_step, 1)
                    pool.wait_ge(ada_step, 2 * v + 2)
                    if v + 2 < n_ada:
                        pool.dma_start(ada_raw[:, s, :], ada[v + 2]).then_inc(ada_landed[s], 16)
            pool.memset(stat[:, 15, :], 0.0).then_inc(ada_done, 1)

        @block.scalar
        def _(act):
            steps = [0]

            def chain(ins):
                steps[0] += 1
                ins.then_inc(act_step, 1)
                act.wait_ge(act_step, steps[0])

            def round_high(u, slot, landed):
                act.wait_ge(raw_landed[slot], landed)
                if not isinstance(u, int) or u >= RING:
                    act.wait_ge(unit_used, u - (RING - 1))
                nc.scalar.activation(w_hi[:, slot, :], raw[:, slot, :], ACT.Copy).then_inc(hi_ready, 1)

            sent = [0]

            def advance(upto):
                while sent[0] < min(upto, N_UNITS):
                    u = sent[0]
                    round_high(u, u % RING, 16 * (u // RING + 1))
                    sent[0] += 1

            def round_in_loop(i, step, u0):
                round_high(i * step + u0, u0 % RING, i * (16 * step // RING) + 16 * (u0 // RING + 1))

            def norm(name):
                n = NORM[name]
                for t in range(TT):
                    if name == "mix0":
                        act.wait_ge(x_landed, 16 * TT)
                    else:
                        act.wait_ge(h_ready, n + t + 1 - 2)
                    nc.scalar.activation(tok[:, t, :], h[:, t, :], ACT.Square,
                                         accum_out=stat[:, 0, t:t + 1]).then_inc(sumsq, 1)
                act.wait_ge(sumsq, n + 2)
                nc.scalar.mul(stat[:, 1, :], stat[:, 0, :], 1.0 / D).then_inc(act_step, 1)
                steps[0] += 1
                act.wait_ge(act_step, steps[0])
                chain(nc.scalar.activation(stat[:, 2, :], stat[:, 1, :], ACT.Ln, bias=eps_col(name)))
                nc.scalar.activation(stat[:, 3, :], stat[:, 2, :], ACT.Exp, scale=-0.5).then_inc(rstd_guess, 1)

            def eps_col(name):
                return stat[:, 4, 0:1] if EPS[name] == 1e-5 else stat[:, 4, 1:2]

            def turn(name, gain=None, shift=None, first=0, upto=None):
                n = TURN[name]
                for c in range(first, 4):
                    act.wait_ge(bank_turned, n + c + 1)
                    if n + c >= 2:
                        act.wait_ge(turned_free, n + c - 1)
                    if gain is None:
                        nc.scalar.activation(turned[:, c % 2, :], ps[4 + c][:, :], ACT.Copy).then_inc(turned_ready, 1)
                    else:
                        for k in range(2):
                            kt = 2 * c + k
                            b = 0.0 if shift is None else shift[:, kt:kt + 1]
                            ins = nc.scalar.activation(turned[:, c % 2, k * T:(k + 1) * T], ps[4 + c][:, k * T:(k + 1) * T],
                                                       ACT.Identity, bias=b, scale=gain[:, kt:kt + 1])
                        ins.then_inc(turned_ready, 1)

            def features(name, dests):
                u0 = FIRST[name]
                for j, (dst, scale) in enumerate(dests):
                    advance(u0 + j + RING)
                    act.wait_ge(unit_used, u0 + j + 1)
                    nc.scalar.activation(dst, ps[4 + j % 4][:, :], ACT.Copy, scale=scale).then_inc(feat_taken, 1)

            def soft(first, last):
                for i in range(first, last):
                    s, hh = heads[i][0], heads[i][1]
                    act.wait_ge(logits_ready, i + 1)
                    if i >= 3:
                        act.wait_ge(probsT_done, i - 2)
                    for t, lo, hi in ((1, 0, 256), (0, 256, 384)):
                        k = 16 * s + 8 * t + hh
                        ins = nc.scalar.activation(prob[:, i % 3, lo:hi], logit[:, i % 3, lo:hi], ACT.Exp, scale=-1.0,
                                                   bias=low[:, k:k + 1], accum_out=den[:, k:k + 1])
                    ins.then_inc(probs_ready, 1)

            def mlp(name):
                u0 = FIRST[name]
                f0 = FIRST[name]
                advance(u0 + RING)
                act.wait_ge(unit_used, u0 + 1)
                nc.scalar.activation(hid_act[:, 0, :], ps[4][:, :], ACT.Relu).then_inc(feat_taken, 1)
                with act.Fori(0, (FF1 - 1) // 3) as i:
                    for j in range(3):
                        a = u0 + 1 + 2 * j
                        round_in_loop(i, 6, a + 2)
                        act.wait_ge(unit_used, i * 6 + (a + 1))
                        nc.scalar.activation(hid_act[:, (j + 1) % 3, :], ps[4 + (j + 1) % 3][:, :], ACT.Relu).then_inc(feat_taken, 1)
                        round_in_loop(i, 6, a + 3)
                sent[0] = u0 + 2 * FF1 - 1 + 2
                assert f0 == u0

            def glu(name):
                u0 = FIRST[name]
                last = name == "glu1"
                advance(u0 + RING)
                advance(u0 + RING + 1)
                act.wait_ge(unit_used, u0 + 2)
                nc.scalar.activation(hid_act[:, 0, :], ps[4][:, :], ACT.Silu).then_inc(feat_taken, 1)

                def block_(i, j):
                    a = u0 + 2 + 3 * j
                    if i is None:
                        advance(a + 3)
                    else:
                        round_in_loop(i, 6, a + 2)
                    slot = (j + 1) % 2
                    if i is None:
                        act.wait_ge(unit_used, a + 2)
                    else:
                        act.wait_ge(unit_used, i * 6 + (a + 1))
                    nc.scalar.activation(hid_act[:, slot, :], ps[4 + 2 * slot][:, :], ACT.Silu).then_inc(feat_taken, 1)
                    for k in (3, 4):
                        if i is None:
                            advance(a + k + 1)
                        else:
                            round_in_loop(i, 6, a + k)

                n_loop = (FF2 - 1) // 2 - (1 if last else 0)
                with act.Fori(0, n_loop) as i:
                    block_(i, 0)
                    block_(i, 1)
                sent[0] = u0 + 2 + 6 * n_loop + 2
                if last:
                    block_(None, 2 * n_loop)
                    block_(None, 2 * n_loop + 1)

            for k, (dst, src) in enumerate([(relt[0:32, :], rel_table), (bfor[:, :], b_forget), (fmask[:, :], fox_mask),
                                            (rpick, rel_pick), (cpick, cmp_pick[:, 0:2048]), (cpick2[:, 0:N_CMP * 2 * P - 2048], cmp_pick[:, 2048:N_CMP * 2 * P])]):
                act.dma_start(dst, src).then_inc(pick_landed, 16)
            act.dma_start(row[:, :], final_norm.partition_broadcast(P)).then_inc(row_landed, 16)
            advance(2)
            act.wait_ge(par_landed, 16)
            act.wait_ge(dve_step, 1)
            nc.scalar.activation(silu_c[:, :], pc_("c", KT), ACT.Silu).then_inc(silu_ready, 1)
            norm("mix0")
            turn("mix0", gain=pc_("mix0", KT))
            act.wait_ge(rel_rows, 1)
            nc.scalar.activation(rrow[:, 0:REL], ps[0][0:16, 0:REL], ACT.Copy).then_inc(rel_rows_sb, 1)
            act.wait_ge(rel_rows_sb, 1)
            act.dma_start(rel_dram[:, :, 0:REL], rrow[:, 0:REL].unsqueeze(1).to_broadcast([16, P, REL])).then_inc(rel_stored, 16)
            features("qk_moba", [(qT[:, 0:2, :], -0.125), (qT[:, 2:4, :], -0.125), (kT[:, 0:2, :], 1.0), (kT[:, 2:4, :], 1.0)])
            act.wait_ge(rel_stored, 16)
            for hh in range(16):
                band = bass.AP(rel_dram, hh * P * (REL + 1) + P - 1, [[REL, P], [1, T]])
                act.dma_start(rel_bias[:, hh, :], band).then_inc(rel_landed, 16)
            u = FIRST["v_even"]
            advance(u + 4 + 2)
            for t in range(TT):
                for n in range(2):
                    w = 512 if n == 0 else V1W - 512
                    act.wait_ge(unit_used, u + 4)
                    if t == 0 and n == 0:
                        act.wait_ge(rel_stored, 16)
                    nc.scalar.activation(V[:, t, 512 * n:512 * n + w], ps[2 * t + n][:, 0:w], ACT.Copy).then_inc(acc_taken, 1)
            act.wait_ge(acc_taken, acc_before["v_even"] + 4)
            nc.scalar.activation(gates1[:, :, :], V[:, :, 768:792], ACT.Exp, scale=-1.0).then_inc(gates_exp, 1)
            u0 = FIRST["q_nsa"]
            for j in range(3):
                advance(u0 + j + RING)
                act.wait_ge(unit_used, u0 + j + 1)
                dst = qT[:, 4 + 2 * j:6 + 2 * j, :] if j < 2 else kT[:, 4:6, :]
                nc.scalar.activation(dst, ps[4 + j][:, :], ACT.Copy, scale=-0.125 if j < 2 else 1.0).then_inc(feat_taken, 1)
            advance(u0 + 3 + RING)
            act.wait_ge(unit_used, u0 + 4)
            for v in range(2):
                for g in range(2):
                    src = ps[7][64 * g:64 * g + 64, v * T:(v + 1) * T]
                    nc.scalar.activation(pair[0:64, v, g, :], src, ACT.Copy)
                    ins = nc.scalar.activation(pair[64:128, v, g, 0:T - 1], src[:, 1:T], ACT.Copy)
            ins.then_inc(feat_taken, 1)
            advance(FIRST["cmp"] + 4 + 2)
            for v in range(2):
                for ht in range(2):
                    act.wait_ge(unit_used, FIRST["cmp"] + 2 * v + 2)
                    ins = nc.scalar.activation(hidc[:, v, ht, 0:30], ps[4 + 2 * v + ht][:, 0:30], ACT.Silu)
                    ins.then_inc(hidc_ready, 1)
            act.wait_ge(ckv_done, 1)
            nc.scalar.activation(kcmpT[:, 0:15], ps[4][:, 0:15], ACT.Copy).then_inc(ckv_taken, 1)
            nc.scalar.activation(vcmp[0:15, :, :], ps[5][0:15, 0:128], ACT.Copy).then_inc(ckv_taken, 1)
            act.wait_ge(cshifted, 1)
            nc.scalar.activation(pc[:, :, 0:15], lcs[:, :, 0:15], ACT.Exp, scale=-1.0).then_inc(cprobs, 1)
            for c in range(4):
                act.wait_ge(cprobsT, c + 1)
                nc.scalar.activation(pcT[0:15, 4 * c:4 * c + 4, :], ps[4 + c][0:15, :], ACT.Copy).then_inc(cprobsT_sb, 1)
            soft(*EVEN)
            turn("even_out")
            advance(FIRST["out_even"] + 4 + 2)
            norm("mlp0")
            turn("mlp0", gain=pc_("mlp0", KT))
            mlp("mlp0")
            advance(FIRST["mlp0"] + 2 * FF1 + 2)
            norm("mix1")
            turn("mix1", gain=pc_("mix1", KT))
            act.wait_ge(fz_taken, 1)
            chain(nc.scalar.activation(fz[:, 2, :], fz[:, 1, :], ACT.Exp))
            nc.scalar.activation(fz[:, 3, :], fz[:, 2, :], ACT.Ln, bias=1.0).then_inc(fz_exp, 1)
            features("qk_fox", [(qT[:, 2 * j:2 * j + 2, :], -0.125) for j in range(4)]
                     + [(kT[:, 2 * j:2 * j + 2, :], 1.0) for j in range(4)])
            advance(FIRST["v_fox"] + 4 + 2)
            for t in range(TT):
                for n in range(2):
                    act.wait_ge(unit_used, FIRST["v_fox"] + 4)
                    nc.scalar.activation(V[:, t, 512 * n:512 * n + 512], ps[2 * t + n][:, :], ACT.Copy).then_inc(acc_taken, 1)
            soft(*FOX)
            turn("fox_out")
            advance(FIRST["out_fox"] + 4 + 2)
            norm("mlp1")
            turn("mlp1", gain=pc_("mlp1", KT))
            mlp("mlp1")
            advance(FIRST["mlp1"] + 2 * FF1 + 2)
            norm("final")
            for j, v in enumerate((2, 5, 8)):
                for n in range(2):
                    act.wait_ge(gate_done, 2 * j + n + 1)
                    nc.scalar.activation(acc_ada[:, v * D + 512 * n:v * D + 512 * n + 512], ps[2 * (j % 2) + n][:, :],
                                         ACT.Copy, scale=(1.0 if v == 5 else 0.5)).then_inc(gate_taken, 1)
            act.wait_ge(mod_taken, 1)
            act.dma_start(dil_b, dil_bias).then_inc(dil_landed, 16)
            act.dma_start(poolm, pool_mat).then_inc(dil_landed, 16)
            norm("gf1")
            act.wait_ge(gain_ready, 1)
            turn("gf1", gain=gainc[:, 0:KT], shift=modc[:, 0:KT])
            act.dma_start(row[:, :], g_final.partition_broadcast(P)).then_inc(row_landed, 16)
            glu("glu0")
            advance(FIRST["glu0"] + 3 * FF2 + 2)
            norm("gmix")
            turn("gmix", gain=gainc[:, KT:2 * KT], shift=modc[:, 3 * KT:4 * KT])
            features("qk_dil", [(qT[:, 0:2, :], -0.125), (qT[:, 2:4, :], -0.125), (kT[:, 0:2, :], 1.0), (kT[:, 2:4, :], 1.0)])
            advance(FIRST["uv_dil"] + 4 + 2)
            for t in range(TT):
                for n in range(2):
                    act.wait_ge(unit_used, FIRST["uv_dil"] + 4)
                    nc.scalar.activation(V[:, t, 512 * n:512 * n + 512], ps[2 * t + n][:, :], ACT.Copy).then_inc(acc_taken, 1)
            for c in range(2):
                act.wait_ge(pooled_done, c + 1)
                nc.scalar.activation(qT[:, 4 + 2 * c:6 + 2 * c, :], ps[6 + c][:, :], ACT.Copy).then_inc(pooled_taken, 1)
            n = TURN["dil_out"]
            for c in range(2):
                act.wait_ge(bank_turned, n + c + 1)
                act.wait_ge(turned_free, n + c - 1)
                for k in range(2):
                    ins = nc.scalar.activation(turned[:, c % 2, k * T:(k + 1) * T], ps[4 + c][:, k * T:(k + 1) * T],
                                               ACT.Identity, scale=pc_("pool_scale", 1, 2 * c + k))
                ins.then_inc(turned_ready, 1)
            soft(*DIL)
            turn("dil_out", first=2)
            advance(FIRST["out_dil"] + 4 + 2)
            norm("gf2")
            turn("gf2", gain=gainc[:, 2 * KT:3 * KT], shift=modc[:, 6 * KT:7 * KT])
            glu("glu1")
            norm("last")

        @block.vector
        def _(dve):
            steps = [0]

            def chain(ins):
                steps[0] += 1
                ins.then_inc(dve_step, 1)
                dve.wait_ge(dve_step, steps[0])

            def take_rest(u, slot):
                dve.wait_ge(hi_ready, u + 1)
                nc.vector.tensor_tensor(w_lo[:, slot, :], raw[:, slot, :], w_hi[:, slot, :].bitcast(F32),
                                        ALU.subtract).then_inc(lo_ready, 1)

            sent = [0]

            def advance(upto):
                while sent[0] < min(upto, N_UNITS):
                    take_rest(sent[0], sent[0] % RING)
                    sent[0] += 1

            def norm_scale(name):
                n = NORM[name]
                dve.wait_ge(rstd_guess, n // 2 + 1)
                v, y, a = stat[:, 5, :], stat[:, 3, :], stat[:, 6, :]
                chain(nc.vector.tensor_scalar(v, stat[:, 1, :], EPS[name], None, ALU.add))
                chain(nc.vector.tensor_tensor(a, y, y, ALU.mult))
                chain(nc.vector.tensor_tensor(a, a, v, ALU.mult))
                chain(nc.vector.tensor_scalar(a, a, -0.5, 1.5, ALU.mult, ALU.add))
                chain(nc.vector.tensor_tensor(stat[:, 7, :], a, y, ALU.mult))

            def norm(name):
                norm_scale(name)
                for t in range(TT):
                    nc.vector.tensor_scalar(tok[:, t, :], h[:, t, :], stat[:, 7, t:t + 1], None, ALU.mult).then_inc(rows_scaled, 1)

            def turn(name, first=0, upto=4):
                n = TURN[name]
                for c in range(first, upto):
                    dve.wait_ge(turned_ready, n + c + 1)
                    src = turned[:, c % 2, :].rearrange("p (a b) -> p a b", a=2)
                    chain(nc.vector.tensor_copy(a_hi[:, 2 * c:2 * c + 2, :], src))
                    nc.vector.tensor_tensor(a_lo[:, 2 * c:2 * c + 2, :], src, a_hi[:, 2 * c:2 * c + 2, :].bitcast(F32),
                                            ALU.subtract).then_inc(act_split, 1)
                    dve.wait_ge(act_split, n + c + 1)
                    nc.vector.tensor_copy(stat[:, 14, :], stat[:, 13, :]).then_inc(turned_free, 1)

            def residual(name, last_unit, gate=None):
                for t in range(TT):
                    for n in range(2):
                        dve.wait_ge(unit_used, last_unit)
                        dst = h[:, t, 512 * n:512 * n + 512]
                        if gate is None:
                            ins = nc.vector.tensor_tensor(dst, ps[2 * t + n][:, :], dst, ALU.add)
                            ins.then_inc(acc_taken, 1)
                        else:
                            tmp = tok[:, t, 512 * n:512 * n + 512]
                            nc.vector.tensor_tensor(tmp, ps[2 * t + n][:, :], gate[:, 512 * n:512 * n + 512],
                                                    ALU.mult).then_inc(acc_taken, 1)
                            dve.wait_ge(acc_taken, acc_before[name] + 2 * t + n + 1)
                            chain(nc.vector.tensor_tensor(dst, dst, tmp, ALU.add))
                    if gate is None:
                        dve.wait_ge(acc_taken, acc_before[name] + 2 * t + 2)
                    nc.vector.tensor_copy(stat[:, 12, t:t + 1], stat[:, 13, 0:1]).then_inc(h_ready, 1)

            def heads_(first, last, norms):
                for i in range(first, last + 3):
                    if i < last:
                        s, hh = heads[i][0], heads[i][1]
                        bias = heads[i][6]
                        dve.wait_ge(scores_done, i + 1)
                        if i >= 3:
                            dve.wait_ge(probs_ready, i - 2)
                        for t, lo, hi in ((1, 0, 256), (0, 256, 384)):
                            k = 16 * s + 8 * t + hh
                            ins = nc.vector.tensor_tensor_reduce(
                                logit[:, i % 3, lo:hi], ps[6 + i % 2][:, lo:hi], bias[:, 256 - (hi - lo):256],
                                1.0, 4 * BIG, ALU.add, ALU.min, low[:, k:k + 1])
                        ins.then_inc(logits_ready, 1)
                    j = i - 2
                    if first <= j < last:
                        dve.wait_ge(probsT_done, j + 1)
                        if j >= 2:
                            dve.wait_ge(pv_done, j - 1)
                        nc.vector.tensor_copy(probT[:, j % 2, :], ps[4 + j % 2][:, 0:SW]).then_inc(probsT_ready, 1)
                    j = i - 3
                    if j >= first and heads[j][1] == HEADS - 1:
                        dve.wait_ge(pv_done, j + 1)
                        norms(heads[j][0])

            def weights(s, gate=None, rows=None):
                w = wgt[:, 16 * s:16 * s + 16]
                chain(nc.vector.reciprocal(w, den[:, 16 * s:16 * s + 16]))
                w3 = w.rearrange("p (t h) -> p t h", t=2)
                if gate is not None:
                    g3 = gates[:, :, :].rearrange("p t (h b) -> p t h b", b=3)[:, :, :, gate]
                    chain(nc.vector.tensor_tensor(w3, w3, g3, ALU.mult))
                if rows is not None:
                    for t in range(TT):
                        chain(nc.vector.tensor_scalar(w3[:, t, :], w3[:, t, :], rows[:, t:t + 1], None, ALU.mult))
                return w3

            def store_set(s, col, add=False, gate=None, rows=None):
                w3 = weights(s, gate, rows)
                for t in range(TT):
                    o3 = ps[set_banks(s)[t]][:, :].rearrange("p (h d) -> p h d", h=HEADS)
                    dst = tok[:, t, col:col + 512].rearrange("p (h d) -> p h d", h=HEADS)
                    ww = w3[:, t, :].unsqueeze(2).to_broadcast([P, HEADS, HD])
                    if add:
                        tmp = h_tmp(t)
                        chain(nc.vector.tensor_tensor(tmp, o3, ww, ALU.mult))
                        chain(nc.vector.tensor_tensor(dst, dst, tmp, ALU.add))
                    else:
                        chain(nc.vector.tensor_tensor(dst, o3, ww, ALU.mult))
                nc.vector.tensor_copy(stat[:, 11, :], stat[:, 13, :]).then_inc(set_taken, 1)

            def h_tmp(t):
                return turned[:, t, :].rearrange("p (h d) -> p h d", h=HEADS)

            def mlp(name):
                u0 = FIRST[name]
                f0, x0 = feat_before[name], hid_before[name]
                advance(u0 + RING)

                def hidden(slot, f, x):
                    dve.wait_ge(feat_taken, f + 1)
                    if not isinstance(x, int) or x > 0:
                        dve.wait_ge(hid_ready, x * 3)
                    src = hid_act[:, slot, :]
                    nc.vector.tensor_tensor(hid_f, src, src, ALU.mult).then_inc(hid_ready, 1)
                    dve.wait_ge(hid_ready, x * 3 + 1)
                    nc.vector.tensor_copy(hid_hi[:, slot, :], hid_f).then_inc(hid_ready, 1)
                    dve.wait_ge(hid_ready, x * 3 + 2)
                    nc.vector.tensor_tensor(hid_lo[:, slot, :], hid_f, hid_hi[:, slot, :].bitcast(F32),
                                            ALU.subtract).then_inc(hid_ready, 1)

                hidden(0, f0, x0)
                with dve.Fori(0, (FF1 - 1) // 3) as i:
                    for j in range(3):
                        a = u0 + 1 + 2 * j
                        take_rest(i * 6 + (a + 2), (a + 2) % RING)
                        hidden((j + 1) % 3, i * 3 + (f0 + j + 1), i * 3 + (x0 + j + 1))
                        take_rest(i * 6 + (a + 3), (a + 3) % RING)
                sent[0] = u0 + 2 * FF1 - 1 + 2

            def glu(name):
                u0 = FIRST[name]
                f0, x0 = feat_before[name], hid_before[name]
                last = name == "glu1"
                advance(u0 + RING + 1)

                def hidden(slot, f, x, u):
                    dve.wait_ge(unit_used, u + 1)
                    dve.wait_ge(feat_taken, f + 1)
                    dve.wait_ge(hid_ready, x * 3)
                    nc.vector.tensor_tensor(hid_f, hid_act[:, slot, :], ps[5 + 2 * slot][:, :], ALU.mult).then_inc(hid_ready, 1)
                    dve.wait_ge(hid_ready, x * 3 + 1)
                    nc.vector.tensor_copy(hid_hi[:, slot, :], hid_f).then_inc(hid_ready, 1)
                    dve.wait_ge(hid_ready, x * 3 + 2)
                    nc.vector.tensor_tensor(hid_lo[:, slot, :], hid_f, hid_hi[:, slot, :].bitcast(F32),
                                            ALU.subtract).then_inc(hid_ready, 1)

                hidden(0, f0, x0, u0 + 1)

                def block_(i, j):
                    a = u0 + 2 + 3 * j
                    if i is None:
                        advance(a + 3)
                        hidden((j + 1) % 2, f0 + j + 1, x0 + j + 1, a + 1)
                        advance(a + 5)
                    else:
                        take_rest(i * 6 + (a + 2), (a + 2) % RING)
                        hidden((j + 1) % 2, i * 2 + (f0 + j + 1), i * 2 + (x0 + j + 1), i * 6 + (a + 1))
                        take_rest(i * 6 + (a + 3), (a + 3) % RING)
                        take_rest(i * 6 + (a + 4), (a + 4) % RING)

                n_loop = (FF2 - 1) // 2 - (1 if last else 0)
                with dve.Fori(0, n_loop) as i:
                    block_(i, 0)
                    block_(i, 1)
                sent[0] = u0 + 2 + 6 * n_loop + 2
                if last:
                    block_(None, 2 * n_loop)
                    block_(None, 2 * n_loop + 1)

            nc.vector.memset(stat[:, 4, 0:1], 1e-5)
            nc.vector.memset(stat[:, 13, :], 0.0)
            chain(nc.vector.memset(stat[:, 4, 1:2], 1e-6))
            advance(2)
            norm("mix0")
            turn("mix0")
            dve.wait_ge(cbias_done, 1)
            nc.vector.tensor_copy(cmp_bias[:, :, 0:15], ps[2][:, 0:240].rearrange("p (n c) -> p c n", n=15)).then_inc(cbias_taken, 1)
            dve.wait_ge(cbias_taken, 1)
            advance(FIRST["v_even"] + 4 + 2)
            dve.wait_ge(gates_exp, 1)
            chain(nc.vector.tensor_scalar(gates1[:, :, :], gates1[:, :, :], 1.0, None, ALU.add))
            chain(nc.vector.reciprocal(gates[:, :, :], gates1[:, :, :]))
            advance(FIRST["q_nsa"] + 3 + RING)
            dve.wait_ge(feat_taken, feat_before["q_nsa"] + 4)
            for v in range(2):
                pos = pc_("pos", 16, 16 * v)
                for g in range(2):
                    src = bass.AP(work, v * 512 + g * T, [list(pair[:, v, g, :].ap[0]), [2, 16], [16, 15]])
                    dst = blk[:, v, :, 15 * g:15 * g + 15]
                    chain(nc.vector.tensor_tensor(dst, src, pos.unsqueeze(2).to_broadcast([P, 16, 15]), ALU.add))
                chain(nc.vector.tensor_copy(blk_hi[:, v], blk[:, v]))
                nc.vector.tensor_tensor(blk_lo[:, v], blk[:, v], blk_hi[:, v].bitcast(F32), ALU.subtract).then_inc(blocks_ready, 1)
            advance(FIRST["cmp"] + 4 + 2)
            dve.wait_ge(cscores, 1)
            for g in range(2):
                for t in range(TT):
                    s3 = ps[6 + g][:, 64 * t:64 * t + 64].rearrange("p (a b) -> p a b", a=4)[:, :, 0:15]
                    k = 8 * t + 4 * g
                    chain(nc.vector.tensor_tensor(lc[:, k:k + 4, 0:15], s3, cmp_bias[:, k:k + 4, 0:15], ALU.add))
            chain(nc.vector.tensor_reduce(low[:, 0:16], lc[:, :, 0:15], AX_X, ALU.min))
            nc.vector.tensor_tensor(lcs[:, :, 0:15], lc[:, :, 0:15], low[:, 0:16].unsqueeze(2).to_broadcast([P, 16, 15]),
                                    ALU.subtract).then_inc(cshifted, 1)
            dve.wait_ge(cprobs, 1)
            chain(nc.vector.tensor_reduce(den[:, 0:16], pc[:, :, 0:15], AX_X, ALU.add))
            dve.wait_ge(cpv, 1)
            store_set(SET_CMP, 512, gate=0, rows=pc_("row_ok", 2))

            def even_norms(s):
                if s == SET_MOBA:
                    store_set(s, 0)
                else:
                    store_set(s, 512, add=True, gate=1 if s == SET_SLC else 2)

            dve.wait_ge(rel_landed, 16 * 16)
            heads_(*EVEN, even_norms)
            turn("even_out")
            advance(FIRST["out_even"] + 4 + 2)
            residual("out_even", FIRST["out_even"] + 4)
            norm("mlp0")
            turn("mlp0")
            mlp("mlp0")
            advance(FIRST["mlp0"] + 2 * FF1 + 2)
            residual("mlp0", FIRST["mlp0"] + 2 * FF1)
            nc.vector.tensor_copy(wf_hi[:, :, :], wf).then_inc(wf_ready, 1)
            dve.wait_ge(wf_ready, 1)
            nc.vector.tensor_tensor(wf_lo[:, :, :], wf, wf_hi[:, :, :].bitcast(F32), ALU.subtract).then_inc(wf_ready, 1)
            norm("mix1")
            turn("mix1")
            dve.wait_ge(fz_done, 1)
            chain(nc.vector.tensor_scalar(fz[:, 0, :], ps[0][0:16, 0:T], bfor[:, 0:1], None, ALU.add))
            chain(nc.vector.tensor_scalar(fz[:, 1, :], fz[:, 0, :], -1.0, None, ALU.mult))
            nc.vector.tensor_tensor(fz[:, 1, :], fz[:, 1, :], fz[:, 0, :], ALU.min).then_inc(fz_taken, 1)
            dve.wait_ge(fz_exp, 1)
            chain(nc.vector.tensor_scalar(fz[:, 0, :], fz[:, 0, :], 0.0, None, ALU.min))
            chain(nc.vector.tensor_tensor(fz[:, 0, :], fz[:, 0, :], fz[:, 3, :], ALU.subtract))
            chain(nc.vector.memset(fz[:, 1, :], 1.0))
            chain(nc.vector.tensor_tensor_scan(cum[:, 0, :], fz[:, 1, :], fz[:, 0, :], 0.0, ALU.mult, ALU.add))
            nc.vector.tensor_scalar(cum[:, 1, :], cum[:, 0, :], -1.0, None, ALU.mult).then_inc(cum_ready, 1)
            advance(FIRST["v_fox"] + 4 + 2)
            heads_(*FOX, lambda s: store_set(s, 0 if s == SET_FOX0 else 512))
            turn("fox_out")
            advance(FIRST["out_fox"] + 4 + 2)
            residual("out_fox", FIRST["out_fox"] + 4)
            norm("mlp1")
            turn("mlp1")
            mlp("mlp1")
            advance(FIRST["mlp1"] + 2 * FF1 + 2)
            residual("mlp1", FIRST["mlp1"] + 2 * FF1)
            norm_scale("final")
            dve.wait_ge(row_landed, 16)
            for t in range(TT):
                nc.vector.scalar_tensor_tensor(out=h[:, t, :], in0=h[:, t, :], scalar=stat[:, 7, t:t + 1], in1=row[:, :],
                                               op0=ALU.mult, op1=ALU.mult).then_inc(h_ready, 1)
            dve.wait_ge(mod_done, 1)
            nc.vector.tensor_copy(modc[:, :], ps[7][:, 0:72]).then_inc(mod_taken, 1)
            dve.wait_ge(mod_taken, 1)
            for j, name in enumerate(("gf1", "gmix", "gf2")):
                g = gainc[:, KT * j:KT * j + KT]
                k = (3 * j + ADA_SCALE) * KT
                chain(nc.vector.tensor_scalar(g, modc[:, k:k + KT], 1.0, None, ALU.add))
                chain(nc.vector.tensor_tensor(g, g, pc_(name, KT), ALU.mult))
            nc.vector.tensor_copy(stat[:, 10, :], stat[:, 13, :]).then_inc(gain_ready, 1)
            norm("gf1")
            turn("gf1")
            glu("glu0")
            advance(FIRST["glu0"] + 3 * FF2 + 2)
            dve.wait_ge(gate_taken, 6)
            residual("glu0", FIRST["glu0"] + 3 * FF2, gate=acc_ada[:, 2 * D:3 * D])
            norm("gmix")
            turn("gmix")
            advance(FIRST["uv_dil"] + 4 + 2)
            turn("dil_out", upto=2)
            dve.wait_ge(dil_landed, 32)
            heads_(*DIL, lambda s: store_set(s, 512))
            turn("dil_out", first=2)
            advance(FIRST["out_dil"] + 4 + 2)
            residual("out_dil", FIRST["out_dil"] + 4, gate=acc_ada[:, 5 * D:6 * D])
            norm("gf2")
            turn("gf2")
            glu("glu1")
            residual("glu1", FIRST["glu1"] + 3 * FF2, gate=acc_ada[:, 8 * D:9 * D])
            norm_scale("last")
            dve.wait_ge(row_landed, 32)
            for t in range(TT):
                nc.vector.scalar_tensor_tensor(out=tok[:, t, :], in0=h[:, t, :], scalar=stat[:, 7, t:t + 1], in1=row[:, :],
                                               op0=ALU.mult, op1=ALU.mult).then_inc(out_ready, 1)

        @block.tensor
        def _(pe):
            def three(dst, l_hi, l_lo, r_hi, r_lo, start, stop):
                nc.tensor.matmul(dst, l_hi, r_lo, start=start, stop=False)
                nc.tensor.matmul(dst, l_lo, r_hi, start=False, stop=False)
                return nc.tensor.matmul(dst, l_hi, r_hi, start=False, stop=stop)

            def feature_unit(u, slot, bank, wait_split=None):
                pe.wait_ge(lo_ready, u + 1)
                wh = w_hi[:, slot, :].rearrange("p (k c) -> p k c", k=KT)
                wl = w_lo[:, slot, :].rearrange("p (k c) -> p k c", k=KT)
                for nt in range(2):
                    for k in range(KT):
                        if wait_split is not None and nt == 0 and k % 2 == 0:
                            pe.wait_ge(act_split, wait_split + k // 2 + 1)
                        cols_ = slice(nt * P, nt * P + P)
                        ins = three(ps[bank][:, nt * T:(nt + 1) * T], wh[:, k, cols_], wl[:, k, cols_],
                                    a_hi[:, k, :], a_lo[:, k, :], k == 0, k == KT - 1)
                ins.then_inc(unit_used, 1)

            def row_unit(u, slot, l_hi, l_lo, width, start, stop):
                pe.wait_ge(lo_ready, u + 1)
                wh = w_hi[:, slot, 0:2 * width].rearrange("p (k c) -> p k c", k=2)
                wl = w_lo[:, slot, 0:2 * width].rearrange("p (k c) -> p k c", k=2)
                for k in range(2):
                    for t in range(TT):
                        for n in range(2):
                            w = min(512, width - 512 * n)
                            sl = slice(512 * n, 512 * n + w)
                            ins = three(ps[2 * t + n][:, 0:w], l_hi(k)[:, t * P:(t + 1) * P], l_lo(k)[:, t * P:(t + 1) * P],
                                        wh[:, k, sl], wl[:, k, sl], start and k == 0, stop and k == 1)
                ins.then_inc(unit_used, 1)

            def rows_phase(name, width=D, wait_split=None):
                u0 = FIRST[name]
                for j in range(4):
                    if wait_split is not None:
                        pe.wait_ge(act_split, wait_split + j + 1)
                    row_unit(u0 + j, (u0 + j) % RING, lambda k: a_hi[:, 2 * j + k, :], lambda k: a_lo[:, 2 * j + k, :],
                             width, j == 0, j == 3)

            def features_phase(name, n, wait_split=None):
                u0, f0 = FIRST[name], feat_before[name]
                for j in range(n):
                    if j >= 4:
                        pe.wait_ge(feat_taken, f0 + j - 3)
                    feature_unit(u0 + j, (u0 + j) % RING, 4 + j % 4, wait_split if j == 0 else None)

            def turn(name, first=0):
                n = TURN[name]
                for c in range(first, 4):
                    for k in range(2):
                        for t in range(TT):
                            kt = 2 * c + k
                            ins = nc.tensor.transpose(ps[4 + c][:, (2 * k + t) * P:(2 * k + t + 1) * P],
                                                      tok[:, t, kt * P:(kt + 1) * P], ident)
                    ins.then_inc(bank_turned, 1)
                assert n >= 0

            def norm_turn(name):
                pe.wait_ge(rows_scaled, NORM_SCALED[name])
                turn(name)

            def attend(first, last, fox=False):
                for i in range(first, last + 3):
                    if i < last:
                        s, hh, qt_, kt_, p0, v0, _ = heads[i]
                        if i >= 2:
                            pe.wait_ge(logits_ready, i - 1)
                        bank = ps[6 + i % 2]
                        for t, lo, w in ((1, 0, 256), (0, 256, 128)):
                            nc_ = nc.tensor.matmul(bank[:, lo:lo + w], qT[p0:p0 + 64, qt_, t * P:(t + 1) * P],
                                                   kT[p0:p0 + 64, kt_, 0:w], start=True, stop=not fox)
                            if fox:
                                hf = 8 * (s - SET_FOX0) + hh
                                pick = ident[0:16, hf:hf + 1]
                                nc.tensor.matmul(bank[:, lo:lo + w], pick.to_broadcast([16, P]), cum[:, 0, 0:w],
                                                 start=False, stop=False)
                                nc_ = nc.tensor.matmul(bank[:, lo:lo + w], cum[:, 1, t * P:(t + 1) * P],
                                                       pick.to_broadcast([16, w]), start=False, stop=True)
                        nc_.then_inc(scores_done, 1)
                    j = i - 2
                    if first <= j < last:
                        pe.wait_ge(probs_ready, j + 1)
                        if j >= 2:
                            pe.wait_ge(probsT_ready, j - 1)
                        for c in range(3):
                            ins = nc.tensor.transpose(ps[4 + j % 2][:, c * P:(c + 1) * P], prob[:, j % 3, c * P:(c + 1) * P], ident)
                        ins.then_inc(probsT_done, 1)
                    j = i - 3
                    if j >= first:
                        s, hh, _, _, _, v0, _ = heads[j]
                        pe.wait_ge(probsT_ready, j + 1)
                        if hh == 0 and s >= 2:
                            pe.wait_ge(set_taken, s - 1)
                        b0, b1 = set_banks(s)
                        dst = slice(hh * HD, hh * HD + HD)
                        nc.tensor.matmul(ps[b0][:, dst], probT[:, j % 2, 256:384], V[:, 0, v0:v0 + HD], start=True, stop=True)
                        nc.tensor.matmul(ps[b1][:, dst], probT[:, j % 2, 0:128], V[:, 0, v0:v0 + HD], start=True, stop=False)
                        nc.tensor.matmul(ps[b1][:, dst], probT[:, j % 2, 128:256], V[:, 1, v0:v0 + HD],
                                         start=False, stop=True).then_inc(pv_done, 1)

            NORM_SCALED = {n: 2 * i + 2 for i, n in enumerate(["mix0", "mlp0", "mix1", "mlp1", "gf1", "gmix", "gf2"])}

            pe.wait_ge(par_landed, 16)
            pe.wait_ge(pick_landed, 16 * N_PAR_LOADS)
            pe.wait_ge(pool_step, 2)
            nc.tensor.matmul(ps[0][0:16, 0:REL], relt[:, :], rpick, start=True, stop=True).then_inc(rel_rows, 1)
            for n in range(N_CMP):
                for t in range(TT):
                    k = (2 * n + t) * P
                    pick = cpick[:, k:k + P] if k < 2048 else cpick2[:, k - 2048:k - 2048 + P]
                    ins = nc.tensor.matmul(ps[2][:, 16 * n + 8 * t:16 * n + 8 * t + 8], pick, relt[:, 8:16], start=True, stop=True)
            ins.then_inc(cbias_done, 1)
            norm_turn("mix0")
            features_phase("qk_moba", 4, TURN["mix0"])
            pe.wait_ge(rel_rows_sb, 1)
            pe.wait_ge(cbias_taken, 1)
            rows_phase("v_even", V1W)
            pe.wait_ge(feat_taken, 4)
            features_phase("q_nsa", 4)
            u0 = FIRST["cmp"]
            for j in range(4):
                v, half = j // 2, j % 2
                u = u0 + j
                pe.wait_ge(lo_ready, u + 1)
                pe.wait_ge(blocks_ready, v + 1)
                pe.wait_ge(feat_taken, 8)
                wh = w_hi[:, u % RING, :].rearrange("p (k c) -> p k c", k=8)
                wl = w_lo[:, u % RING, :].rearrange("p (k c) -> p k c", k=8)
                for k in range(8):
                    for ht in range(2):
                        c_ = slice(ht * P, ht * P + P)
                        ins = three(ps[4 + 2 * v + ht][:, 0:30], wh[:, k, c_], wl[:, k, c_],
                                    blk_hi[:, v, 8 * half + k, :], blk_lo[:, v, 8 * half + k, :],
                                    half == 0 and k == 0, half == 1 and k == 7)
                ins.then_inc(unit_used, 1)
            pe.wait_ge(hidc_ready, 4)
            for g in range(2):
                for ht in range(2):
                    nc.tensor.matmul(ps[4][64 * g:64 * g + 64, 0:15], cw2[:, 0, ht, :], hidc[:, 0, ht, 15 * g:15 * g + 15],
                                     start=(ht == 0), stop=(ht == 1))
            for g in range(2):
                for ht in range(2):
                    ins = nc.tensor.matmul(ps[5][0:15, 64 * g:64 * g + 64], hidc[:, 1, ht, 15 * g:15 * g + 15], cw2[:, 1, ht, :],
                                           start=(ht == 0), stop=(ht == 1))
            ins.then_inc(ckv_done, 1)
            pe.wait_ge(ckv_taken, 2)
            for t in range(TT):
                for hh in range(HEADS):
                    g = hh // 4
                    ins = nc.tensor.matmul(ps[6 + g][:, 16 * (4 * t + hh % 4):16 * (4 * t + hh % 4) + 15],
                                           qT[64 * g:64 * g + 64, 4 + hh % 4, t * P:(t + 1) * P],
                                           kcmpT[64 * g:64 * g + 64, 0:15], start=True, stop=True)
            ins.then_inc(cscores, 1)
            pe.wait_ge(cprobs, 1)
            for c in range(4):
                for k in range(4):
                    ins = nc.tensor.transpose(ps[4 + c][0:15, k * P:(k + 1) * P], pc[:, 4 * c + k, 0:15], ident)
                ins.then_inc(cprobsT, 1)
            pe.wait_ge(cprobsT_sb, 4)
            pe.wait_ge(acc_taken, 4)
            for t in range(TT):
                for hh in range(HEADS):
                    ins = nc.tensor.matmul(ps[t][:, hh * HD:(hh + 1) * HD], pcT[0:15, 8 * t + hh, :], vcmp[0:15, hh // 4, :],
                                           start=True, stop=True)
            ins.then_inc(cpv, 1)
            attend(*EVEN)
            pe.wait_ge(set_taken, 4)
            turn("even_out")
            rows_phase("out_even", wait_split=TURN["even_out"])

            def mlp(name):
                u0, f0, x0 = FIRST[name], feat_before[name], hid_before[name]
                pe.wait_ge(acc_taken, acc_before[name])
                feature_unit(u0, u0 % RING, 4, TURN[name])

                def down(u, slot, hs, x, start, stop):
                    pe.wait_ge(hid_ready, x * 3 + 3)
                    row_unit(u, slot, lambda k: hid_hi[:, hs, k * T:(k + 1) * T], lambda k: hid_lo[:, hs, k * T:(k + 1) * T],
                             D, start, stop)

                def pair_(i, j, start):
                    a = u0 + 1 + 2 * j
                    e = (lambda k, c: c) if i is None else (lambda k, c: i * k + c)
                    feature_unit(e(6, a), a % RING, 4 + (j + 1) % 3)
                    down(e(6, a + 1), (a + 1) % RING, j % 3, e(3, x0 + j), start, False)

                for j in range(3):
                    pair_(None, j, j == 0)
                with pe.Fori(1, (FF1 - 1) // 3) as i:
                    for j in range(3):
                        pair_(i, j, False)
                u = u0 + 2 * FF1 - 1
                down(u, u % RING, (FF1 - 1) % 3, x0 + FF1 - 1, False, True)

            def glu(name):
                u0, f0, x0 = FIRST[name], feat_before[name], hid_before[name]
                pe.wait_ge(acc_taken, acc_before[name])
                feature_unit(u0, u0 % RING, 4, TURN["gf1" if name == "glu0" else "gf2"])
                feature_unit(u0 + 1, (u0 + 1) % RING, 5)

                def down(u, slot, hs, x, start, stop):
                    pe.wait_ge(hid_ready, x * 3 + 3)
                    row_unit(u, slot, lambda k: hid_hi[:, hs, k * T:(k + 1) * T], lambda k: hid_lo[:, hs, k * T:(k + 1) * T],
                             D, start, stop)

                def triple(i, j, start):
                    a = u0 + 2 + 3 * j
                    e = (lambda k, c: c) if i is None else (lambda k, c: i * k + c)
                    b = 4 + 2 * ((j + 1) % 2)
                    feature_unit(e(6, a), a % RING, b)
                    feature_unit(e(6, a + 1), (a + 1) % RING, b + 1)
                    down(e(6, a + 2), (a + 2) % RING, j % 2, e(2, x0 + j), start, False)

                for j in range(2):
                    triple(None, j, j == 0)
                with pe.Fori(1, (FF2 - 1) // 2) as i:
                    for j in range(2):
                        triple(i, j, False)
                u = u0 + 3 * FF2 - 1
                down(u, u % RING, (FF2 - 1) % 2, x0 + FF2 - 1, False, True)

            norm_turn("mlp0")
            mlp("mlp0")
            norm_turn("mix1")
            pe.wait_ge(act_split, TURN["mix1"] + 4)
            pe.wait_ge(wf_ready, 2)
            pe.wait_ge(acc_taken, acc_before["v_fox"])
            for k in range(KT):
                ins = three(ps[0][0:16, 0:T], wf_hi[:, k, :], wf_lo[:, k, :], a_hi[:, k, :], a_lo[:, k, :], k == 0, k == KT - 1)
            ins.then_inc(fz_done, 1)
            features_phase("qk_fox", 8)
            pe.wait_ge(fz_taken, 1)
            rows_phase("v_fox")
            pe.wait_ge(acc_taken, acc_before["v_fox"] + 4)
            pe.wait_ge(feat_taken, feat_before["qk_fox"] + 8)
            pe.wait_ge(cum_ready, 1)
            attend(*FOX, fox=True)
            pe.wait_ge(set_taken, 6)
            turn("fox_out")
            rows_phase("out_fox", wait_split=TURN["fox_out"])
            norm_turn("mlp1")
            mlp("mlp1")
            pe.wait_ge(acc_taken, acc_before["glu0"])
            pe.wait_ge(ada_done, 1)
            for k in range(9 * KT):
                ins = nc.tensor.matmul(ps[7][:, k:k + 1], acc_ada[:, k * P:(k + 1) * P], ones[:, 0:1], start=True, stop=True)
            ins.then_inc(mod_done, 1)
            for j, v in enumerate((2, 5, 8)):
                for n in range(2):
                    if j == 2:
                        pe.wait_ge(gate_taken, n + 1)
                    nc.tensor.matmul(ps[2 * (j % 2) + n][:, :], ones[:, :], acc_ada[:, v * D + 512 * n:v * D + 512 * n + 512],
                                     start=True, stop=True).then_inc(gate_done, 1)
            pe.wait_ge(gate_taken, 6)
            pe.wait_ge(mod_taken, 1)
            norm_turn("gf1")
            glu("glu0")
            norm_turn("gmix")
            features_phase("qk_dil", 4, TURN["gmix"])
            pe.wait_ge(acc_taken, acc_before["uv_dil"])
            rows_phase("uv_dil")
            pe.wait_ge(acc_taken, acc_before["uv_dil"] + 4)
            pe.wait_ge(feat_taken, feat_before["qk_dil"] + 4)
            pe.wait_ge(dil_landed, 32)
            for g in range(4):
                for k in range(TT):
                    ins = nc.tensor.matmul(ps[6 + g // 2][:, (g % 2) * T:(g % 2 + 1) * T], V[:, k, g * P:(g + 1) * P],
                                           poolm[:, g, k, :], start=(k == 0), stop=(k == 1))
                if g % 2:
                    ins.then_inc(pooled_done, 1)
            for g in range(4):
                pe.wait_ge(pooled_taken, g // 2 + 1)
                ins = nc.tensor.matmul(ps[4 + g // 2][:, (g % 2) * T:(g % 2 + 1) * T], w_pool[:, g, :], qT[:, 4 + g, :],
                                       start=True, stop=True)
                if g % 2:
                    ins.then_inc(bank_turned, 1)
            pe.wait_ge(turned_ready, TURN["dil_out"] + 2)
            attend(*DIL)
            pe.wait_ge(set_taken, 7)
            turn("dil_out", first=2)
            rows_phase("out_dil", wait_split=TURN["dil_out"])
            norm_turn("gf2")
            glu("glu1")


        assert qkv_at and row_free and pairs_ready


def rel_buckets(d):
    n = np.maximum(d, 0)
    nf = np.maximum(n, 1).astype(np.float32)
    large = 16 + (np.log(nf / np.float32(16)) / np.float32(np.log(64.0)) * np.float32(16)).astype(np.int32)
    return np.where(n < 16, n, np.minimum(large, 31))


def shape_constants():
    f = np.float32

    def pick(d):
        m = np.zeros((33, d.size), f)
        b = rel_buckets(d)
        m[b, np.arange(d.size)] = -1.0
        m[0:32, d < 0] = 0.0
        m[32, d < 0] = BIG
        return m

    rel_pick = pick(255 - np.arange(REL))
    q = np.arange(P)
    cmp_pick = np.concatenate(
        [pick(t * P + q - (16 * n + 31)) for n in range(N_CMP) for t in range(TT)], axis=1)
    dist = P + q[:, None] - np.arange(T)[None, :]
    fox_mask = np.where(dist < 0, BIG, 0.0).astype(f)
    count = (dist <= 128).astype(f) + (dist % 4 == 0) + (dist % 16 == 0)
    ok = (dist >= 0) & (count > 0)
    logs = np.log(np.where(ok, count, 1.0))
    dil = np.stack([np.where(ok, dist * 2.0 ** -(hh + 1) - logs, BIG) for hh in range(HEADS)], axis=1).astype(f)
    tt = np.arange(T)
    pool = np.zeros((P, 4, TT, T), f)
    for g, w in enumerate((2, 4, 8, 16)):
        m = ((tt[:, None] <= tt[None, :]) & (tt[:, None] > tt[None, :] - w)) / np.minimum(tt[None, :] + 1, w)
        m = (m - np.eye(T)).astype(f)
        pool[:, g] = m.reshape(TT, P, T).transpose(1, 0, 2)
    row_ok = (np.arange(T) >= 31).astype(f).reshape(TT, P).T
    return rel_pick, cmp_pick, fox_mask, dil, pool, row_ok


def lay_out(a):
    def feats(w):
        n = w.shape[1] // T
        return w.reshape(KT, P, n, T).transpose(2, 1, 0, 3).reshape(n, P, UNIT)

    def rows(w):
        n, width = w.shape[0] // T, w.shape[1]
        u = w.reshape(n, 2, P, width).transpose(0, 2, 1, 3).reshape(n, P, 2 * width)
        if 2 * width < UNIT:
            u = np.concatenate([u, np.zeros((n, P, UNIT - 2 * width), u.dtype)], axis=2)
        return u

    def mlp(w1, w2):
        first, second = feats(w1), rows(w2)
        order = [first[0:1]]
        for j in range(FF1 - 1):
            order += [first[j + 1:j + 2], second[j:j + 1]]
        return order + [second[FF1 - 1:]]

    def glu(wg, wu, wd):
        g, u, d = feats(wg), feats(wu), rows(wd)
        order = [g[0:1], u[0:1]]
        for j in range(FF2 - 1):
            order += [g[j + 1:j + 2], u[j + 1:j + 2], d[j:j + 1]]
        return order + [d[FF2 - 1:]]

    w = a["even_w_in"][0]
    nq = w[:, 1536:2048].reshape(D, 2, 4, HD).transpose(0, 2, 1, 3).reshape(D, 512)
    c = {n: w[:, 2048 + 128 * i:2176 + 128 * i] for i, n in enumerate(("kc", "vc", "ks", "vs", "kw", "vw"))}
    parts = [feats(w[:, 0:1024])]
    parts += [rows(np.concatenate([w[:, 1024:1536], c["vs"], c["vw"], w[:, 2816:2840]], axis=1))]
    parts += [feats(np.concatenate([nq, c["ks"], c["kw"], c["kc"], c["vc"]], axis=1))]
    parts += [feats(a[n][0].reshape(2, 1024, 256).transpose(1, 0, 2).reshape(1024, 512)) for n in ("cmp_k_w1", "cmp_v_w1")]
    parts += [rows(a["even_w_out"][0])]
    parts += mlp(a["mlp_w1"][0], a["mlp_w2"][0])
    wo = a["odd_w_in"][0]
    parts += [feats(wo[:, 0:2048]), rows(wo[:, 2048:3072]), rows(a["odd_w_out"][0])]
    parts += mlp(a["mlp_w1"][1], a["mlp_w2"][1])
    parts += glu(a["w1_gate_2"][0], a["w1_up_2"][0], a["w1_down_2"][0])
    w2 = a["w_in_2"][0]
    parts += [feats(w2[:, 512:1536]), rows(np.concatenate([w2[:, 0:512], w2[:, 1536:2048]], axis=1)), rows(a["w_out_2"][0])]
    parts += glu(a["w2_gate_2"][0], a["w2_up_2"][0], a["w2_down_2"][0])
    stream = np.concatenate(parts, axis=0)
    assert stream.shape == (N_UNITS, P, UNIT)
    ada = np.ascontiguousarray(a["w_ada_2"][0].reshape(KT, P, 9, D).transpose(2, 0, 1, 3)).reshape(9 * KT, P, D)

    def col(v):
        return v.reshape(-1, P).T

    rel_pick, cmp_pick, fox_mask, dil, pool, row_ok = shape_constants()
    w2s = np.stack([a[n][0].reshape(2, P, HD) for n in ("cmp_k_w2", "cmp_v_w2")]).transpose(2, 0, 1, 3).reshape(P, 256)
    cols = np.concatenate([
        col(a["mix_norm"][0]), col(a["mlp_norm"][0]), col(a["mix_norm"][1]), col(a["mlp_norm"][1]),
        col(a["g_ffn1_2"][0]), col(a["g_mix_2"][0]), col(a["g_ffn2_2"][0]), col(a["pool_scale_2"][0]),
        col(a["cmp_pos_k"][0].reshape(-1)), col(a["cmp_pos_v"][0].reshape(-1)), col(a["c_2"][0]), row_ok, w2s,
        a["w_pool_2"][0].transpose(1, 0, 2).reshape(P, 512),
        wo[:, 3072:3088].reshape(KT, P, 16).transpose(1, 0, 2).reshape(P, 128), np.eye(P, dtype=np.float32)], axis=1)
    assert cols.shape == (P, N_COLS)
    return {
        "stream": stream, "ada": ada, "cols": cols, "x": a["x"][0], "rel_table": a["rel_bias"],
        "rel_pick": rel_pick, "cmp_pick": cmp_pick, "fox_mask": fox_mask, "dil_bias": dil, "pool_mat": pool,
        "b_ada": a["b_ada_2"], "b_forget": a["odd_b_forget"][0].reshape(16, 1),
        "final_norm": a["final_norm"], "g_final": a["g_final_2"],
    }


def kernel(**inputs):
    import concourse.bacc as bacc
    from concourse.bass_utils import run_bass_kernel_spmd

    arrays = {k: np.ascontiguousarray(v) for k, v in lay_out({k: np.asarray(v) for k, v in inputs.items()}).items()}
    nc = bacc.Bacc("TRN2", target_bir_lowering=False, num_devices=1)
    args = {k: nc.dram_tensor("in_" + k, v.shape, mybir.dt.from_np(v.dtype), kind="ExternalInput").ap() for k, v in arrays.items()}
    out = nc.dram_tensor("out", (T, D), F32, kind="ExternalOutput").ap()
    build(nc, out=out, **args)
    r = run_bass_kernel_spmd(nc, [{"in_" + k: v for k, v in arrays.items()}], core_ids=[0])
    return r.results[0]["out"].reshape(1, T, D)
```

```python
from contextlib import ExitStack

import numpy as np

import concourse.bass as bass
from concourse import mybir

F32 = mybir.dt.float32
F32R = mybir.dt.float32r
ALU = mybir.AluOpType
ACT = mybir.ActivationFunctionType
AX_X = mybir.AxisListType.X

P = 128
T = 256
TT = T // P
D = 1024
KT = D // P
HD = 64
HEADS = 8
UNIT = 2048
RING = 3
FF1 = 4096 // T
FF2 = 2816 // T
N_CMP = 15
V1W = 792
BIG = 1e30
SW = 384
REL = 2 * P + T - 1

PHASES = [
    ("qk_moba", 4), ("q_nsa", 4), ("v_even", 4), ("cmp", 4), ("out_even", 4), ("mlp0", 2 * FF1),
    ("qk_fox", 8), ("v_fox", 4), ("out_fox", 4), ("mlp1", 2 * FF1),
    ("glu0", 3 * FF2), ("qk_dil", 4), ("uv_dil", 4), ("out_dil", 4), ("glu1", 3 * FF2),
]
FIRST = {}
N_UNITS = 0
for _name, _n in PHASES:
    FIRST[_name] = N_UNITS
    N_UNITS += _n
ADA_PIECE = 512
ADA_W = 9 * D

COLS = {}
N_COLS = 0
for _name, _n in [("cmp_w2", 256), ("mix0", 8), ("mlp0", 8), ("mix1", 8), ("mlp1", 8), ("gf1", 8), ("gmix", 8), ("gf2", 8),
                  ("pool_scale", 4), ("pos", 32), ("c", 8), ("row_ok", 2),
                  ("w_pool", 512), ("w_forget", 128), ("ident", 128)]:
    COLS[_name] = N_COLS
    N_COLS += _n

PAIR = 3 * HD
NSA_V = 4 * PAIR
VW = {"even": NSA_V + HD + 4 * 2 * HD, "fox": 8 * PAIR, "dil": 4 * PAIR}

ADA_SHIFT, ADA_SCALE, ADA_GATE = 0, 1, 2
SET_CMP, SET_MOBA, SET_SLC, SET_WIN, SET_FOX0, SET_FOX1, SET_DIL = range(7)


def build(nc, stream, ada, cols, x, rel_table, rel_pick, cmp_pick, fox_mask, dil_bias, pool_mat,
          b_ada, b_forget, final_norm, g_final, out):
    ctx = ExitStack()
    with ctx:
        base = [-(-nc.sbuf_base // 64) * 64]

        def place(name, shape, dt=F32, at=None):
            size = -(-int(np.prod(shape[1:])) * 4 // 64) * 64
            if at is None:
                at = base[0]
                base[0] += size
            t = nc.alloc_sbuf_tensor_at(name, list(shape), dt, offset=at)
            return t

        def sem(name):
            return ctx.enter_context(nc.semaphore(name))

        raw = place("raw", [P, RING, UNIT])
        w_hi = place("w_hi", [P, RING, UNIT], F32R)
        w_lo = place("w_lo", [P, RING, UNIT], F32R)
        V_at = base[0]
        a_hi = place("a_hi", [P, KT, T], F32R)
        a_lo = place("a_lo", [P, KT, T], F32R)
        tok_at = base[0]
        tok = place("tok", [P, TT, D])
        V_all = place("V_all", [P, 2 * TT * VW["fox"]], F32R, at=V_at)

        h = place("h", [P, TT, D])
        work_at = base[0]
        work = place("work", [P, 3072])
        probT_hi = place("probT_hi", [P, 2, SW], F32R, at=work_at + 6 * SW * 4)
        probT_lo_at = base[0]
        probT_lo = place("probT_lo", [P, 2, SW], F32R)
        qkv_at = base[0]
        q_two = place("q_two", [P, 8, 2, T], F32R)
        k_two = place("k_two", [P, 8, 2, T], F32R)
        k_lo = place("k_lo", [P, 8, T], F32R)
        pooled_y = place("pooled_y", [P, 2, 2 * T], at=qkv_at + 4 * 2 * T * 4)
        hid_hi = place("hid_hi", [P, 3, 2 * T], F32R, at=qkv_at)
        hid_lo = place("hid_lo", [P, 3, 2 * T], F32R, at=qkv_at + 3 * 2 * T * 4)
        blk_hi = place("blk_hi", [P, 2, 16, 30], F32R, at=work_at + 2048 * 4)
        blk_lo = place("blk_lo", [P, 2, 16, 30], F32R, at=qkv_at + (8 + 6) * 2 * T * 4)
        acc_ada = place("acc_ada", [P, ADA_W])
        ada_at = base[0]
        ada_raw = place("ada_raw", [P, 2, ADA_PIECE])
        row = place("row", [P, D], at=ada_at)
        fmask_at = base[0]
        fmask = place("fmask", [P, T])
        par_at = base[0]
        par = place("par", [P, N_COLS])
        cmp_bias = place("cmp_bias", [P, 16, 16], at=fmask_at)
        kc_hi = place("kc_hi", [P, 2, 16], F32R)
        kc_lo = place("kc_lo", [P, 2, 16], F32R)
        vcmp = place("vcmp", [16, 2, HD], at=V_at + 4 * VW["even"] * 4)
        hidc = place("hidc", [P, 2, 2, 32], at=probT_lo_at)
        ones = place("ones", [P, P])
        low = place("low", [P, 7 * 16])
        den = place("den", [P, 7 * 16])
        wgt = place("wgt", [P, 7 * 16])
        gates_at = base[0]
        inv_gates = place("inv_gates", [P, TT, 24])
        gates_e = place("gates_e", [P, TT, 24], at=probT_lo_at + 512)
        stat = place("stat", [P, 16, 2])
        modc = place("modc", [P, 9 * KT])
        gainc = place("gainc", [P, 3 * KT])
        silu_c = place("silu_c", [P, KT])
        wf_hi = place("wf_hi", [P, KT, 16], F32R, at=probT_lo_at)
        wf_lo = place("wf_lo", [P, KT, 16], F32R, at=probT_lo_at + KT * 16 * 4)
        fz = place("fz", [16, 4, T], at=tok_at)
        cum = place("cum", [16, T], at=tok_at + 4 * T * 4)
        cum_r = place("cum_r", [112, T], F32R, at=par_at + COLS["cmp_w2"] * 4)
        pick_r = place("pick_r", [112, 2, 16], F32R, at=gates_at)
        bfor = stat[0:16, 8, 0:1]
        relt = place("relt", [33, 16], at=qkv_at + (8 + 7) * 2 * T * 4)
        assert base[0] <= nc.sbuf_usable_end, (base[0], nc.sbuf_usable_end)
        rel_bias = acc_ada[:, 0:16 * T].rearrange("p (a b) -> p a b", a=16)
        dil_b = acc_ada[:, 0:2 * D].rearrange("p (a b) -> p a b", a=8)
        poolm = acc_ada[:, 3 * D:5 * D].rearrange("p (g k t) -> p g k t", g=4, k=2)
        rpick = work[0:33, 0:REL]
        rrow = work[0:16, 1024:1024 + REL]
        cpick = acc_ada[0:33, 16 * T:16 * T + N_CMP * 2 * P]
        u_rows = work[:, 0:1024].rearrange("p (t c) -> p t c", t=TT)
        pooledT = work[:, 1024:2048].rearrange("p (g t) -> p g t", g=4)
        logit = work[:, 0:2 * SW].rearrange("p (b c) -> p b c", b=2)
        prob = work[:, 2 * SW:6 * SW].rearrange("p (b c) -> p b c", b=4)
        hid_act = work[:, 0:1536].rearrange("p (b c) -> p b c", b=3)
        hid_f = work[:, 1536:2048]
        shifted = work[:, 0:1024].rearrange("p (b c) -> p b c", b=2)
        pair = work[:, 0:1024].rearrange("p (v g t) -> p v g t", v=2, g=2)
        blk = work[:, 1024:1984].rearrange("p (v j n) -> p v j n", v=2, j=16)
        hid30 = place("hid30", [30, 2, 256], at=qkv_at + (8 + 6) * 2 * T * 4)
        pcT = [place(f"pcT{c}", [16, 2, T], at=at_) for c, at_ in enumerate((
            qkv_at + (8 + 6) * 2 * T * 4, qkv_at + (8 + 7) * 2 * T * 4, qkv_at + (16 * 2 + 6) * T * 4,
            V_at + 4 * VW["even"] * 4 + 2 * HD * 4))]
        assert 4 * VW["even"] + 2 * HD + 2 * T <= 3 * TT * D
        pc = cmp_bias

        def pc_(name, n, k=0):
            return par[:, COLS[name] + k:COLS[name] + k + n]

        ident = pc_("ident", P)
        cw2 = pc_("cmp_w2", 256).rearrange("p (v t d) -> p v t d", v=2, t=2)
        w_pool = pc_("w_pool", 512).rearrange("p (g d) -> p g d", g=4)
        wf = pc_("w_forget", 128).rearrange("p (k h) -> p k h", k=KT)

        ps = [ctx.enter_context(nc.psum_tensor(f"bank{i}", [P, 512], F32)) for i in range(8)]
        rel_dram = nc.dram_tensor("rel_scratch", (16, P, REL + 1), F32)

        par_landed = sem("par_landed")
        x_landed = sem("x_landed")
        pick_landed = sem("pick_landed")
        mask_landed = sem("mask_landed")
        feat_hi = sem("feat_hi")
        val_hi = sem("val_hi")
        probsT_hi = sem("probsT_hi")
        raw_landed = [sem(f"raw_landed{i}") for i in range(RING)]
        hi_ready = sem("hi_ready")
        lo_ready = sem("lo_ready")
        unit_used = sem("unit_used")
        feat_taken = sem("feat_taken")
        values_taken = sem("values_taken")
        hid_ready = sem("hid_ready")
        h_ready = sem("h_ready")
        sumsq = sem("sumsq")
        rstd_guess = sem("rstd_guess")
        rows_scaled = sem("rows_scaled")
        bank_turned = sem("bank_turned")
        act_high = sem("act_high")
        act_split = sem("act_split")
        dve_step = sem("dve_step")
        act_step = sem("act_step")
        pool_step = sem("pool_step")
        rel_rows = sem("rel_rows")
        rel_rows_sb = sem("rel_rows_sb")
        rel_stored = sem("rel_stored")
        rel_landed = sem("rel_landed")
        cbias_done = sem("cbias_done")
        cbias_taken = sem("cbias_taken")
        blocks_ready = sem("blocks_ready")
        hidden_rows = sem("hidden_rows")
        hidden_turned = sem("hidden_turned")
        hidc_ready = sem("hidc_ready")
        ckv_done = sem("ckv_done")
        ckv_taken = sem("ckv_taken")
        cscores = sem("cscores")
        cshifted = sem("cshifted")
        cprobs = sem("cprobs")
        cscaled = sem("cscaled")
        cprobsT = sem("cprobsT")
        cprobsT_sb = sem("cprobsT_sb")
        gates_exp = sem("gates_exp")
        scores_done = sem("scores_done")
        logits_ready = sem("logits_ready")
        probs_ready = sem("probs_ready")
        probsT_done = sem("probsT_done")
        probsT_ready = sem("probsT_ready")
        weight_ready = sem("weight_ready")
        probs_scaled = sem("probs_scaled")
        pv_done = sem("pv_done")
        wf_ready = sem("wf_ready")
        fz_done = sem("fz_done")
        fz_taken = sem("fz_taken")
        fz_exp = sem("fz_exp")
        cum_ready = sem("cum_ready")
        ada_landed = [sem("ada_landed0"), sem("ada_landed1")]
        bada_landed = sem("bada_landed")
        silu_ready = sem("silu_ready")
        ada_step = sem("ada_step")
        ADA_STEPS = 2 * KT * (ADA_W // ADA_PIECE)
        mod_done = sem("mod_done")
        mod_taken = sem("mod_taken")
        gate_done = sem("gate_done")
        gate_taken = sem("gate_taken")
        gain_ready = sem("gain_ready")
        dil_landed = sem("dil_landed")
        row_landed = sem("row_landed")
        pooled_done = sem("pooled_done")
        pooled_taken = sem("pooled_taken")
        out_ready = sem("out_ready")
        out_stored = sem("out_stored")

        heads = []

        def head(s, hh, qt, kt, b, v0, bias, gate, feat, opens):
            heads.append((16 * s + hh, qt, kt, b, v0, bias, gate, feat, hh % 2, opens))

        def pair_col(hh):
            return PAIR * (hh // 2) + HD * (hh % 2)

        def v_cols(kind, part, t, c0, counts):
            at = (part * TT + t) * VW[kind] + c0
            return bass.AP(V_all, at, [list(V_all[:, 0:1].ap[0])] + [list(c) for c in counts])

        def value_moves(kind):
            moves = []
            for t in range(TT):
                if kind != "dil":
                    moves.append((t, 2 * t, 512, 0, [[PAIR, 4], [2 * HD, 2], [1, HD]], "p (a b c) -> p a b c", dict(b=2, c=HD)))
                if kind == "even":
                    moves.append((t, 2 * t + 1, 256, NSA_V + HD, [[2 * HD, 4], [1, HD]], "p (a c) -> p a c", dict(c=HD)))
                else:
                    moves.append((t, 2 * t + 1, 512, 0 if kind == "dil" else 4 * PAIR, [[PAIR, 4], [2 * HD, 2], [1, HD]],
                                  "p (a b c) -> p a b c", dict(b=2, c=HD)))
            return moves

        for hh in range(HEADS):
            head(SET_MOBA, hh, hh // 2, hh // 2, hh % 2, pair_col(hh), rel_bias[:, hh, :], None, hh // 2, hh % 2 == 0)
        for hh in range(HEADS):
            g = hh // 4
            for s, kt_, v, br in ((SET_SLC, 4, g, 1), (SET_WIN, 5, 2 + g, 2)):
                head(s, hh, 4 + hh % 4, kt_, g, NSA_V + HD + 2 * HD * v - HD * (hh % 2), rel_bias[:, 8 + hh, :], inv_gates[:, :, 3 * hh + br],
                     4 + hh // 2, False)
        for hh in range(2 * HEADS):
            head(SET_FOX0 + hh // 8, hh % 8, hh // 2, hh // 2, hh % 2, pair_col(hh), fmask[:, :], None, hh // 2, hh % 2 == 0)
        for hh in range(HEADS):
            head(SET_DIL, hh, hh // 2, hh // 2, hh % 2, pair_col(hh), dil_b[:, hh, :], None, 4 + hh // 2, hh % 2 == 0)
        EVEN = (0, 24)
        FOX = (24, 40)
        DIL = (40, 48)
        SCALE_LAG, TURN_LAG, ROUND_LAG, PV_LAG = 1, 3, 4, 5

        TURN = {n: 4 * i for i, n in enumerate(
            ["mix0", "even_out", "mlp0", "mix1", "fox_out", "mlp1", "gf1", "gmix", "dil_out", "gf2"])}
        BANK = {"mix0": 0, "mlp0": 4, "mix1": 8, "mlp1": 12, "gf1": 16, "gmix": 20, "pooled": 24, "gf2": 26}
        NORM = {n: 2 * i for i, n in enumerate(
            ["mix0", "mlp0", "mix1", "mlp1", "final", "gf1", "gmix", "gf2", "last"])}
        EPS = {n: (1e-5 if n in ("mix0", "mlp0", "mix1", "mlp1", "final") else 1e-6) for n in NORM}
        N_PAR_LOADS = 4

        feat_before = {}
        n = 0
        for name, k in (("qk_moba", 4), ("q_nsa", 4), ("mlp0", FF1), ("qk_fox", 8), ("mlp1", FF1),
                        ("glu0", FF2), ("qk_dil", 4), ("glu1", FF2)):
            feat_before[name] = n
            n += k
        V_PHASE = {"even": "v_even", "fox": "v_fox", "dil": "uv_dil"}
        V_BEFORE = {"even": 0, "fox": 4, "dil": 8}
        hid_before = {"mlp0": 0, "mlp1": FF1, "glu0": 2 * FF1, "glu1": 2 * FF1 + FF2}

        block = ctx.enter_context(nc.Block())

        @block.sync
        def _(sp):
            for t in range(TT):
                sp.dma_start(h[:, t, :], x[t * P:(t + 1) * P, :]).then_inc(x_landed, 16)
            sp.dma_start(par[:, :], cols[:, :]).then_inc(par_landed, 16)
            for u in range(RING):
                sp.dma_start(raw[:, u, :], stream[u]).then_inc(raw_landed[u], 16)
            with sp.Fori(1, N_UNITS // RING) as i:
                for s in range(RING):
                    sp.wait_ge(lo_ready, i * RING + (s - RING + 1))
                    sp.dma_start(raw[:, s, :], stream[i * RING + s]).then_inc(raw_landed[s], 16)
            for u in range(N_UNITS - N_UNITS % RING, N_UNITS):
                sp.wait_ge(lo_ready, u - RING + 1)
                sp.dma_start(raw[:, u % RING, :], stream[u]).then_inc(raw_landed[u % RING], 16)
            sp.wait_ge(out_ready, 2)
            sp.dma_start(out.rearrange("(t p) d -> p t d", p=P), tok[:, :, :]).then_inc(out_stored, 16)
            sp.wait_ge(out_stored, 16)

        @block.gpsimd
        def _(pool):
            pool.memset(ones[:, :], 1.0).then_inc(pool_step, 1)
            pool.wait_ge(pool_step, 1)
            pool.memset(relt[32:33, :], 1.0).then_inc(pool_step, 1)
            for s in range(2):
                pool.dma_start(ada_raw[:, s, :], ada[s]).then_inc(ada_landed[s], 16)
            pool.wait_ge(cbias_taken, 1)
            pool.wait_ge(pool_step, 2)
            pool.memset(acc_ada[:, 4 * D:9 * D], 0.0).then_inc(pool_step, 1)
            pool.wait_ge(pool_step, 3)
            pool.dma_start(acc_ada[0:1, 4 * D:9 * D], b_ada[:, 4 * D:9 * D]).then_inc(bada_landed, 16)
            pool.wait_ge(bada_landed, 16)
            pool.wait_ge(silu_ready, 1)
            n_ada = ADA_W // ADA_PIECE * KT
            for nb in range(ADA_W // ADA_PIECE):
                c0 = ADA_W - ADA_PIECE * (nb + 1)
                if c0 == 4 * D - ADA_PIECE:
                    pool.wait_ge(logits_ready, EVEN[1])
                    pool.memset(acc_ada[:, 0:4 * D], 0.0).then_inc(pool_step, 1)
                    pool.wait_ge(pool_step, 4)
                    pool.dma_start(acc_ada[0:1, 0:4 * D], b_ada[:, 0:4 * D]).then_inc(bada_landed, 16)
                    pool.wait_ge(bada_landed, 32)
                for k in range(KT):
                    v = KT * nb + k
                    s = v % 2
                    part = ada_raw[:, s, :]
                    pool.wait_ge(ada_landed[s], 16 * (v // 2 + 1))
                    pool.tensor_scalar(part, part, silu_c[:, k:k + 1], 1.0, ALU.mult, ALU.mult).then_inc(ada_step, 1)
                    pool.wait_ge(ada_step, 2 * v + 1)
                    acc = acc_ada[:, c0:c0 + ADA_PIECE]
                    pool.tensor_tensor(acc, acc, part, ALU.add).then_inc(ada_step, 1)
                    pool.wait_ge(ada_step, 2 * v + 2)
                    if v + 2 < n_ada:
                        pool.dma_start(ada_raw[:, s, :], ada[v + 2]).then_inc(ada_landed[s], 16)

        @block.scalar
        def _(act):
            steps = [0]

            def chain(ins):
                steps[0] += 1
                ins.then_inc(act_step, 1)
                act.wait_ge(act_step, steps[0])

            def round_high(u, slot, landed):
                act.wait_ge(raw_landed[slot], landed)
                if not isinstance(u, int) or u >= RING:
                    act.wait_ge(unit_used, u - (RING - 1))
                nc.scalar.activation(w_hi[:, slot, :], raw[:, slot, :], ACT.Copy).then_inc(hi_ready, 1)

            sent = [0]

            def advance(upto):
                while sent[0] < min(upto, N_UNITS):
                    u = sent[0]
                    round_high(u, u % RING, 16 * (u // RING + 1))
                    sent[0] += 1

            def round_in_loop(i, step, u0):
                round_high(i * step + u0, u0 % RING, i * (16 * step // RING) + 16 * (u0 // RING + 1))

            def norm(name):
                n = NORM[name]
                for t in range(TT):
                    if name == "mix0":
                        act.wait_ge(x_landed, 16 * TT)
                    else:
                        act.wait_ge(h_ready, 2 * (n - 2) + 2 * t + 2)
                    nc.scalar.activation(tok[:, t, :], h[:, t, :], ACT.Square,
                                         accum_out=stat[:, 0, t:t + 1]).then_inc(sumsq, 1)
                act.wait_ge(sumsq, n + 2)
                nc.scalar.mul(stat[:, 1, :], stat[:, 0, :], 1.0 / D).then_inc(act_step, 1)
                steps[0] += 1
                act.wait_ge(act_step, steps[0])
                chain(nc.scalar.activation(stat[:, 2, :], stat[:, 1, :], ACT.Ln, bias=eps_col(name)))
                nc.scalar.activation(stat[:, 3, :], stat[:, 2, :], ACT.Exp, scale=-0.5).then_inc(rstd_guess, 1)

            def eps_col(name):
                return stat[:, 4, 0:1] if EPS[name] == 1e-5 else stat[:, 4, 1:2]

            def turn(name, gain, shift=None):
                n = BANK[name]
                for c in range(4):
                    act.wait_ge(bank_turned, n + c + 1)
                    for k in range(2):
                        kt = 2 * c + k
                        b = 0.0 if shift is None else shift[:, kt:kt + 1]
                        ins = nc.scalar.activation(a_hi[:, kt, :], ps[4 + c][:, k * T:(k + 1) * T],
                                                   ACT.Identity, bias=b, scale=gain[:, kt:kt + 1])
                    ins.then_inc(act_high, 1)

            def outputs(n_heads, pooled=False):
                act.wait_ge(pv_done, n_heads)
                for c in range(4):
                    src = pooled_y[:, c, :] if pooled and c < 2 else ps[c][:, :]
                    nc.scalar.activation(a_hi[:, 2 * c:2 * c + 2, :], src, ACT.Copy).then_inc(act_high, 1)

            def stack(j, tile, scale, keys):
                for b in range(2):
                    src = ps[4 + j % 4][64 * b:64 * b + 64, :].rearrange("p (a b) -> p a b", a=2)
                    two = k_two if keys else q_two
                    for half in ((b, 1 - b) if keys else (b,)):
                        ins = nc.scalar.activation(two[64 * half:64 * half + 64, tile:tile + 2, b, :], src, ACT.Copy, scale=scale)
                ins.then_inc(feat_hi, 1)

            def features(name, n):
                u0 = FIRST[name]
                for j in range(2 * n):
                    advance(u0 + j + RING)
                    act.wait_ge(unit_used, u0 + j + 1)
                    stack(j, 2 * (j % n), -0.125 if j < n else 1.0, j >= n)

            def values(kind):
                last = FIRST[V_PHASE[kind]] + 4
                advance(last + 2)
                for t, bank, w, c0, counts, form, sizes in value_moves(kind):
                    act.wait_ge(unit_used, last)
                    nc.scalar.activation(v_cols(kind, 0, t, c0, counts), ps[bank][:, 0:w].rearrange(form, **sizes),
                                         ACT.Copy).then_inc(val_hi, 1)

            def soft(first, last, between=None):
                for i in range(first, last + ROUND_LAG):
                    j = i - ROUND_LAG
                    if j >= first:
                        act.wait_ge(probsT_done, j + 1)
                        if j >= 2:
                            act.wait_ge(pv_done, j - 1)
                        nc.scalar.activation(probT_hi[:, j % 2, :], ps[4 + j % 2][:, 0:SW], ACT.Copy).then_inc(probsT_hi, 1)
                    if i < last:
                        k = heads[i][0]
                        act.wait_ge(logits_ready, i + 1)
                        if i >= 4:
                            act.wait_ge(probsT_done, i - 3)
                        for t, lo, hi in ((1, 0, 256), (0, 256, 384)):
                            kk = k + 8 * t
                            ins = nc.scalar.activation(prob[:, i % 4, lo:hi], logit[:, i % 2, lo:hi], ACT.Exp, scale=-1.0,
                                                       bias=low[:, kk:kk + 1], accum_out=den[:, kk:kk + 1])
                        ins.then_inc(probs_ready, 1)
                    if between:
                        between(i)
            def mlp(name):
                u0 = FIRST[name]
                f0 = FIRST[name]
                advance(u0 + RING)
                act.wait_ge(unit_used, u0 + 1)
                nc.scalar.activation(hid_act[:, 0, :], ps[4][:, :], ACT.Relu).then_inc(feat_taken, 1)
                with act.Fori(0, (FF1 - 1) // 3) as i:
                    for j in range(3):
                        a = u0 + 1 + 2 * j
                        round_in_loop(i, 6, a + 2)
                        act.wait_ge(unit_used, i * 6 + (a + 1))
                        nc.scalar.activation(hid_act[:, (j + 1) % 3, :], ps[4 + (j + 1) % 3][:, :], ACT.Relu).then_inc(feat_taken, 1)
                        round_in_loop(i, 6, a + 3)
                sent[0] = u0 + 2 * FF1 - 1 + 2
                assert f0 == u0

            def glu(name):
                u0 = FIRST[name]
                last = name == "glu1"
                advance(u0 + RING)
                advance(u0 + RING + 1)
                act.wait_ge(unit_used, u0 + 2)
                nc.scalar.activation(hid_act[:, 0, :], ps[4][:, :], ACT.Silu).then_inc(feat_taken, 1)

                def block_(i, j):
                    a = u0 + 2 + 3 * j
                    if i is None:
                        advance(a + 3)
                    else:
                        round_in_loop(i, 6, a + 2)
                    slot = (j + 1) % 2
                    if i is None:
                        act.wait_ge(unit_used, a + 2)
                    else:
                        act.wait_ge(unit_used, i * 6 + (a + 1))
                    nc.scalar.activation(hid_act[:, slot, :], ps[4 + 2 * slot][:, :], ACT.Silu).then_inc(feat_taken, 1)
                    for k in (3, 4):
                        if i is None:
                            advance(a + k + 1)
                        else:
                            round_in_loop(i, 6, a + k)

                n_loop = (FF2 - 1) // 2 - (1 if last else 0)
                with act.Fori(0, n_loop) as i:
                    block_(i, 0)
                    block_(i, 1)
                sent[0] = u0 + 2 + 6 * n_loop + 2
                if last:
                    block_(None, 2 * n_loop)
                    block_(None, 2 * n_loop + 1)

            for dst, src in ((relt[0:32, :], rel_table), (bfor[:, :], b_forget), (rpick, rel_pick), (cpick, cmp_pick)):
                act.dma_start(dst, src).then_inc(pick_landed, 16)
            advance(2)
            act.wait_ge(par_landed, 16)
            act.wait_ge(dve_step, 1)
            nc.scalar.activation(silu_c[:, :], pc_("c", KT), ACT.Silu).then_inc(silu_ready, 1)
            norm("mix0")
            act.wait_ge(rel_rows, 1)
            nc.scalar.activation(rrow, ps[0][0:16, 0:REL], ACT.Copy).then_inc(rel_rows_sb, 1)
            act.wait_ge(rel_rows_sb, 1)
            act.dma_start(rel_dram[:, :, 0:REL], rrow.unsqueeze(1).to_broadcast([16, P, REL])).then_inc(rel_stored, 16)
            turn("mix0", gain=pc_("mix0", KT))
            features("qk_moba", 2)
            act.wait_ge(rel_stored, 16)
            for hh in range(16):
                band = bass.AP(rel_dram, hh * P * (REL + 1) + P - 1, [[REL, P], [1, T]])
                act.dma_start(rel_bias[:, hh, :], band).then_inc(rel_landed, 16)
            u0 = FIRST["q_nsa"]
            for j in range(3):
                advance(u0 + j + RING)
                act.wait_ge(unit_used, u0 + j + 1)
                stack(j, 4 + 2 * (j % 2), -0.125 if j < 2 else 1.0, j == 2)
            advance(u0 + 3 + RING)
            act.wait_ge(unit_used, u0 + 4)
            for v in range(2):
                for g in range(2):
                    src = ps[7][64 * g:64 * g + 64, v * T:(v + 1) * T]
                    nc.scalar.activation(pair[0:64, v, g, :], src, ACT.Copy)
                    ins = nc.scalar.activation(pair[64:128, v, g, 0:T - 1], src[:, 1:T], ACT.Copy)
            ins.then_inc(feat_taken, 1)
            advance(FIRST["v_even"] + 4 + 2)
            act.wait_ge(unit_used, FIRST["v_even"] + 4)
            for t in range(TT):
                ins = nc.scalar.activation(gates_e[:, t, :], ps[2 * t + 1][:, 256:280], ACT.Exp, scale=-1.0)
            ins.then_inc(gates_exp, 1)
            values("even")
            advance(FIRST["cmp"] + 4 + 2)
            for v in range(2):
                act.wait_ge(unit_used, FIRST["cmp"] + 2 * v + 2)
                nc.scalar.activation(hid30[0:30, v, :], ps[4 + v][0:30, 0:256], ACT.Silu).then_inc(hidden_rows, 1)
            act.wait_ge(hidden_turned, 1)
            nc.scalar.activation(hidc[:, :, :, 0:30], ps[6][:, 0:128].rearrange("p (v h n) -> p v h n", v=2, h=2)[:, :, :, 0:30],
                                 ACT.Copy).then_inc(hidc_ready, 1)

            def compressed(i):
                if i == 0:
                    act.wait_ge(ckv_done, 1)
                    nc.scalar.activation(kc_hi[:, :, 0:15], ps[2][:, 0:32].rearrange("p (g n) -> p g n", g=2)[:, :, 0:15],
                                         ACT.Copy).then_inc(ckv_taken, 1)
                    nc.scalar.activation(vcmp[0:15, :, :], ps[3][0:15, 0:128], ACT.Copy).then_inc(ckv_taken, 1)
                if i == 2:
                    act.wait_ge(cshifted, 1)
                    nc.scalar.activation(pc[:, :, 0:15], pc[:, :, 0:15], ACT.Exp, scale=-1.0).then_inc(cprobs, 1)
                if 4 <= i < 8:
                    c = i - 4
                    act.wait_ge(cprobsT, c + 1)
                    nc.scalar.activation(pcT[c][0:15, :, :], ps[2 + c % 2][0:15, :].rearrange("p (a b) -> p a b", a=2),
                                         ACT.Copy).then_inc(cprobsT_sb, 1)

            soft(*EVEN, between=compressed)
            act.dma_start(fmask[:, :], fox_mask).then_inc(mask_landed, 16)
            outputs(EVEN[1])
            advance(FIRST["out_even"] + 4 + 2)
            norm("mlp0")
            turn("mlp0", gain=pc_("mlp0", KT))
            mlp("mlp0")
            advance(FIRST["mlp0"] + 2 * FF1 + 2)
            norm("mix1")
            turn("mix1", gain=pc_("mix1", KT))
            act.wait_ge(fz_taken, 1)
            chain(nc.scalar.activation(fz[:, 2, :], fz[:, 1, :], ACT.Exp))
            nc.scalar.activation(fz[:, 3, :], fz[:, 2, :], ACT.Ln, bias=1.0).then_inc(fz_exp, 1)
            features("qk_fox", 4)
            values("fox")
            soft(*FOX)
            outputs(FOX[1])
            advance(FIRST["out_fox"] + 4 + 2)
            norm("mlp1")
            turn("mlp1", gain=pc_("mlp1", KT))
            mlp("mlp1")
            advance(FIRST["mlp1"] + 2 * FF1 + 2)
            act.wait_ge(ada_step, ADA_STEPS)
            act.dma_start(row[:, :], final_norm.partition_broadcast(P)).then_inc(row_landed, 16)
            norm("final")
            for j, v in enumerate((2, 5, 8)):
                for n in range(2):
                    act.wait_ge(gate_done, 2 * j + n + 1)
                    nc.scalar.activation(acc_ada[:, v * D + 512 * n:v * D + 512 * n + 512], ps[4 + 2 * (j % 2) + n][:, :],
                                         ACT.Copy, scale=(1.0 if v == 5 else 0.5)).then_inc(gate_taken, 1)
            act.dma_start(dil_b, dil_bias).then_inc(dil_landed, 16)
            act.dma_start(poolm, pool_mat).then_inc(dil_landed, 16)
            norm("gf1")
            act.wait_ge(gain_ready, 3)
            turn("gf1", gain=gainc[:, 0:KT], shift=modc[:, 0:KT])
            act.dma_start(row[:, :], g_final.partition_broadcast(P)).then_inc(row_landed, 16)
            glu("glu0")
            advance(FIRST["glu0"] + 3 * FF2 + 2)
            norm("gmix")
            turn("gmix", gain=gainc[:, KT:2 * KT], shift=modc[:, 3 * KT:4 * KT])
            features("qk_dil", 2)
            advance(FIRST["uv_dil"] + 4 + 2)
            for t in range(TT):
                act.wait_ge(unit_used, FIRST["uv_dil"] + 4)
                nc.scalar.activation(u_rows[:, t, :], ps[2 * t][:, :], ACT.Copy).then_inc(pooled_taken, 1)
            values("dil")
            for c in range(2):
                act.wait_ge(pooled_done, c + 1)
                nc.scalar.activation(pooledT[:, 2 * c:2 * c + 2, :], ps[6 + c][:, :], ACT.Copy).then_inc(pooled_taken, 1)
            for c in range(2):
                act.wait_ge(bank_turned, BANK["pooled"] + c + 1)
                for k in range(2):
                    ins = nc.scalar.activation(pooled_y[:, c, k * T:(k + 1) * T], ps[4 + c][:, k * T:(k + 1) * T],
                                               ACT.Identity, scale=pc_("pool_scale", 1, 2 * c + k))
                ins.then_inc(pooled_taken, 1)
            soft(*DIL)
            act.wait_ge(pooled_taken, 6)
            outputs(DIL[1], pooled=True)
            advance(FIRST["out_dil"] + 4 + 2)
            norm("gf2")
            turn("gf2", gain=gainc[:, 2 * KT:3 * KT], shift=modc[:, 6 * KT:7 * KT])
            glu("glu1")
            norm("last")

        @block.vector
        def _(dve):
            steps = [0]

            def chain(ins):
                steps[0] += 1
                ins.then_inc(dve_step, 1)
                dve.wait_ge(dve_step, steps[0])

            def take_rest(u, slot):
                dve.wait_ge(hi_ready, u + 1)
                nc.vector.tensor_tensor(w_lo[:, slot, :], raw[:, slot, :], w_hi[:, slot, :].bitcast(F32),
                                        ALU.subtract).then_inc(lo_ready, 1)

            sent = [0]

            def advance(upto):
                while sent[0] < min(upto, N_UNITS):
                    take_rest(sent[0], sent[0] % RING)
                    sent[0] += 1

            def norm_scale(name):
                n = NORM[name]
                dve.wait_ge(rstd_guess, n // 2 + 1)
                v, y, a = stat[:, 5, :], stat[:, 3, :], stat[:, 6, :]
                chain(nc.vector.tensor_scalar(v, stat[:, 1, :], EPS[name], None, ALU.add))
                chain(nc.vector.tensor_tensor(a, y, y, ALU.mult))
                chain(nc.vector.tensor_tensor(a, a, v, ALU.mult))
                chain(nc.vector.tensor_scalar(a, a, -0.5, 1.5, ALU.mult, ALU.add))
                chain(nc.vector.tensor_tensor(stat[:, 7, :], a, y, ALU.mult))

            def norm(name):
                norm_scale(name)
                if NORM[name]:
                    dve.wait_ge(h_ready, 2 * NORM[name])
                for t in range(TT):
                    nc.vector.tensor_scalar(tok[:, t, :], h[:, t, :], stat[:, 7, t:t + 1], None, ALU.mult).then_inc(rows_scaled, 1)

            def turn(name, gain, shift=None):
                n = TURN[name]
                for c in range(4):
                    dve.wait_ge(act_high, n + c + 1)
                    for k in range(2):
                        kt = 2 * c + k
                        src, g = ps[4 + c][:, k * T:(k + 1) * T], gain[:, kt:kt + 1]
                        if shift is not None:
                            tmp = shifted[:, c % 2, k * T:(k + 1) * T]
                            nc.vector.tensor_scalar(tmp, src, g, shift[:, kt:kt + 1], ALU.mult, ALU.add).then_inc(dve_step, 1)
                            steps[0] += 1
                        else:
                            ins = nc.vector.scalar_tensor_tensor(out=a_lo[:, kt, :], in0=src, scalar=g, in1=a_hi[:, kt, :].bitcast(F32),
                                                                 op0=ALU.mult, op1=ALU.subtract)
                    if shift is not None:
                        dve.wait_ge(dve_step, steps[0])
                        ins = nc.vector.tensor_tensor(a_lo[:, 2 * c:2 * c + 2, :], shifted[:, c % 2, :].rearrange("p (a b) -> p a b", a=2),
                                                      a_hi[:, 2 * c:2 * c + 2, :].bitcast(F32), ALU.subtract)
                    ins.then_inc(act_split, 1)

            def outputs(name, pooled=False):
                n = TURN[name]
                for c in range(4):
                    dve.wait_ge(act_high, n + c + 1)
                    src = pooled_y[:, c, :] if pooled and c < 2 else ps[c][:, :]
                    nc.vector.tensor_tensor(a_lo[:, 2 * c:2 * c + 2, :], src.rearrange("p (a b) -> p a b", a=2),
                                            a_hi[:, 2 * c:2 * c + 2, :].bitcast(F32), ALU.subtract).then_inc(act_split, 1)

            def residual(last_unit, gate=None):
                dve.wait_ge(unit_used, last_unit)
                for t in range(TT):
                    for n in range(2):
                        dst = h[:, t, 512 * n:512 * n + 512]
                        if gate is None:
                            nc.vector.tensor_tensor(dst, ps[2 * t + n][:, :], dst, ALU.add).then_inc(h_ready, 1)
                        else:
                            tmp = tok[:, t, 512 * n:512 * n + 512]
                            chain(nc.vector.tensor_tensor(tmp, ps[2 * t + n][:, :], gate[:, 512 * n:512 * n + 512], ALU.mult))
                            nc.vector.tensor_tensor(dst, dst, tmp, ALU.add).then_inc(h_ready, 1)

            def stack(j, tile, scale, keys):
                for b in range(2):
                    rows_ = slice(64 * b, 64 * b + 64)
                    src = ps[4 + j % 4][rows_, :].rearrange("p (a b) -> p a b", a=2)
                    hi = (k_two if keys else q_two)[rows_, tile:tile + 2, b, :]
                    dst = k_lo[rows_, tile:tile + 2, :] if keys else q_two[64 * (1 - b):64 * (1 - b) + 64, tile:tile + 2, b, :]
                    ins = nc.vector.scalar_tensor_tensor(out=dst, in0=src, scalar=scale, in1=hi.bitcast(F32),
                                                         op0=ALU.mult, op1=ALU.subtract)
                ins.then_inc(feat_taken, 1)

            def features(name, n):
                u0 = FIRST[name]
                for j in range(2 * n):
                    advance(u0 + j + RING)
                    dve.wait_ge(feat_hi, f_hi[name] + j + 1)
                    stack(j, 2 * (j % n), -0.125 if j < n else 1.0, j >= n)

            f_hi = {"qk_moba": 0, "q_nsa": 4, "qk_fox": 7, "qk_dil": 15}

            def values(kind):
                last = FIRST[V_PHASE[kind]] + 4
                advance(last + 2)
                dve.wait_ge(unit_used, last)
                for part in range(2):
                    for t in range(TT):
                        nc.vector.memset(v_cols(kind, part, t, HD, [[PAIR, 8 if kind == "fox" else 4], [1, HD]]).bitcast(F32), 0.0)
                        if kind == "even":
                            nc.vector.memset(v_cols(kind, part, t, NSA_V, [[2 * HD, 5], [1, HD]]).bitcast(F32), 0.0)
                for k, (t, bank, w, c0, counts, form, sizes) in enumerate(value_moves(kind)):
                    dve.wait_ge(val_hi, V_BEFORE[kind] + k + 1)
                    nc.vector.tensor_tensor(v_cols(kind, 1, t, c0, counts), ps[bank][:, 0:w].rearrange(form, **sizes),
                                            v_cols(kind, 0, t, c0, counts).bitcast(F32), ALU.subtract).then_inc(values_taken, 1)

            def heads_(first, last, between=None):
                for i in range(first, last + ROUND_LAG):
                    if i < last:
                        k, bias = heads[i][0], heads[i][5]
                        dve.wait_ge(scores_done, i + 1)
                        if i >= 2:
                            dve.wait_ge(probs_ready, i - 1)
                        for t, lo, hi in ((1, 0, 256), (0, 256, 384)):
                            kk = k + 8 * t
                            ins = nc.vector.tensor_tensor_reduce(
                                logit[:, i % 2, lo:hi], ps[6 + i % 2][:, lo:hi], bias[:, 256 - (hi - lo):256],
                                1.0, 4 * BIG, ALU.add, ALU.min, low[:, kk:kk + 1])
                        ins.then_inc(logits_ready, 1)
                    j = i - SCALE_LAG
                    if first <= j < last:
                        k, gate = heads[j][0], heads[j][6]
                        w, d = wgt[:, k:k + 9:8], den[:, k:k + 9:8]
                        dve.wait_ge(probs_ready, j + 1)
                        if gate is None:
                            nc.vector.reciprocal(w, d).then_inc(weight_ready, 1)
                        else:
                            chain(nc.vector.tensor_tensor(w, gate, d, ALU.mult))
                            nc.vector.reciprocal(w, w).then_inc(weight_ready, 1)
                    m = i - ROUND_LAG
                    if m >= first:
                        dve.wait_ge(probsT_hi, m + 1)
                        nc.vector.tensor_tensor(probT_lo[:, m % 2, :], ps[4 + m % 2][:, 0:SW], probT_hi[:, m % 2, :].bitcast(F32),
                                                ALU.subtract).then_inc(probsT_ready, 1)
                    if first <= j < last:
                        dve.wait_ge(weight_ready, j + 1)
                        for t, lo, hi in ((1, 0, 256), (0, 256, 384)):
                            kk = heads[j][0] + 8 * t
                            p_ = prob[:, j % 4, lo:hi]
                            ins = nc.vector.tensor_scalar(p_, p_, wgt[:, kk:kk + 1], None, ALU.mult)
                        ins.then_inc(probs_scaled, 1)
                    if between:
                        between(i)

            def mlp(name):
                u0 = FIRST[name]
                f0, x0 = feat_before[name], hid_before[name]
                advance(u0 + RING)

                def hidden(slot, f, x):
                    dve.wait_ge(feat_taken, f + 1)
                    if not isinstance(x, int) or x > 0:
                        dve.wait_ge(hid_ready, x * 3)
                    src = hid_act[:, slot, :]
                    nc.vector.tensor_tensor(hid_f, src, src, ALU.mult).then_inc(hid_ready, 1)
                    dve.wait_ge(hid_ready, x * 3 + 1)
                    nc.vector.tensor_copy(hid_hi[:, slot, :], hid_f).then_inc(hid_ready, 1)
                    dve.wait_ge(hid_ready, x * 3 + 2)
                    nc.vector.tensor_tensor(hid_lo[:, slot, :], hid_f, hid_hi[:, slot, :].bitcast(F32),
                                            ALU.subtract).then_inc(hid_ready, 1)

                hidden(0, f0, x0)
                with dve.Fori(0, (FF1 - 1) // 3) as i:
                    for j in range(3):
                        a = u0 + 1 + 2 * j
                        take_rest(i * 6 + (a + 2), (a + 2) % RING)
                        hidden((j + 1) % 3, i * 3 + (f0 + j + 1), i * 3 + (x0 + j + 1))
                        take_rest(i * 6 + (a + 3), (a + 3) % RING)
                sent[0] = u0 + 2 * FF1 - 1 + 2

            def glu(name):
                u0 = FIRST[name]
                f0, x0 = feat_before[name], hid_before[name]
                last = name == "glu1"
                advance(u0 + RING + 1)

                def hidden(slot, f, x, u):
                    dve.wait_ge(unit_used, u + 1)
                    dve.wait_ge(feat_taken, f + 1)
                    dve.wait_ge(hid_ready, x * 3)
                    nc.vector.tensor_tensor(hid_f, hid_act[:, slot, :], ps[5 + 2 * slot][:, :], ALU.mult).then_inc(hid_ready, 1)
                    dve.wait_ge(hid_ready, x * 3 + 1)
                    nc.vector.tensor_copy(hid_hi[:, slot, :], hid_f).then_inc(hid_ready, 1)
                    dve.wait_ge(hid_ready, x * 3 + 2)
                    nc.vector.tensor_tensor(hid_lo[:, slot, :], hid_f, hid_hi[:, slot, :].bitcast(F32),
                                            ALU.subtract).then_inc(hid_ready, 1)

                hidden(0, f0, x0, u0 + 1)

                def block_(i, j):
                    a = u0 + 2 + 3 * j
                    if i is None:
                        advance(a + 3)
                        hidden((j + 1) % 2, f0 + j + 1, x0 + j + 1, a + 1)
                        advance(a + 5)
                    else:
                        take_rest(i * 6 + (a + 2), (a + 2) % RING)
                        hidden((j + 1) % 2, i * 2 + (f0 + j + 1), i * 2 + (x0 + j + 1), i * 6 + (a + 1))
                        take_rest(i * 6 + (a + 3), (a + 3) % RING)
                        take_rest(i * 6 + (a + 4), (a + 4) % RING)

                n_loop = (FF2 - 1) // 2 - (1 if last else 0)
                with dve.Fori(0, n_loop) as i:
                    block_(i, 0)
                    block_(i, 1)
                sent[0] = u0 + 2 + 6 * n_loop + 2
                if last:
                    block_(None, 2 * n_loop)
                    block_(None, 2 * n_loop + 1)

            nc.vector.memset(stat[:, 4, 0:1], 1e-5)
            nc.vector.memset(kc_hi[:, :, 15:16].bitcast(F32), 0.0)
            nc.vector.memset(kc_lo[:, :, 15:16].bitcast(F32), 0.0)
            chain(nc.vector.memset(stat[:, 4, 1:2], 1e-6))
            advance(2)
            norm("mix0")
            dve.wait_ge(cbias_done, 1)
            nc.vector.tensor_copy(cmp_bias[:, :, 0:15], ps[2][:, 0:240].rearrange("p (n c) -> p c n", n=15)).then_inc(cbias_taken, 1)
            turn("mix0", gain=pc_("mix0", KT))
            features("qk_moba", 2)
            for j in range(3):
                advance(FIRST["q_nsa"] + j + RING)
                dve.wait_ge(feat_hi, f_hi["q_nsa"] + j + 1)
                stack(j, 4 + 2 * (j % 2), -0.125 if j < 2 else 1.0, j == 2)
            advance(FIRST["q_nsa"] + 3 + RING)
            dve.wait_ge(feat_taken, feat_before["q_nsa"] + 4)
            for v in range(2):
                pos = pc_("pos", 16, 16 * v)
                for g in range(2):
                    src = bass.AP(work, v * 512 + g * T, [list(pair[:, v, g, :].ap[0]), [2, 16], [16, 15]])
                    dst = blk[:, v, :, 15 * g:15 * g + 15]
                    chain(nc.vector.tensor_tensor(dst, src, pos.unsqueeze(2).to_broadcast([P, 16, 15]), ALU.add))
                chain(nc.vector.tensor_copy(blk_hi[:, v], blk[:, v]))
                nc.vector.tensor_tensor(blk_lo[:, v], blk[:, v], blk_hi[:, v].bitcast(F32), ALU.subtract).then_inc(blocks_ready, 1)
            values("even")
            dve.wait_ge(gates_exp, 1)
            nc.vector.tensor_scalar(inv_gates[:, :, :], gates_e[:, :, :], 1.0, None, ALU.add).then_inc(dve_step, 1)
            steps[0] += 1
            advance(FIRST["cmp"] + 4 + 2)

            def compressed(i):
                if i == 0:
                    dve.wait_ge(ckv_taken, 2)
                    nc.vector.tensor_tensor(kc_lo[:, :, 0:15], ps[2][:, 0:32].rearrange("p (g n) -> p g n", g=2)[:, :, 0:15],
                                            kc_hi[:, :, 0:15].bitcast(F32), ALU.subtract).then_inc(ckv_taken, 1)
                if i == 1:
                    dve.wait_ge(cscores, 1)
                    s3 = ps[2][:, 0:256].rearrange("p (a b) -> p a b", a=16)[:, :, 0:15]
                    chain(nc.vector.tensor_tensor(pc[:, :, 0:15], s3, pc[:, :, 0:15], ALU.add))
                    chain(nc.vector.tensor_reduce(low[:, 0:16], pc[:, :, 0:15], AX_X, ALU.min))
                    nc.vector.tensor_tensor(pc[:, :, 0:15], pc[:, :, 0:15], low[:, 0:16].unsqueeze(2).to_broadcast([P, 16, 15]),
                                            ALU.subtract).then_inc(cshifted, 1)
                if i == 3:
                    dve.wait_ge(cprobs, 1)
                    chain(nc.vector.tensor_reduce(den[:, 0:16], pc[:, :, 0:15], AX_X, ALU.add))
                    w0 = wgt[:, 0:16].rearrange("p (t h) -> p t h", t=2)
                    d0 = den[:, 0:16].rearrange("p (t h) -> p t h", t=2)
                    chain(nc.vector.tensor_tensor(w0, inv_gates[:, :, :].rearrange("p t (h b) -> p t h b", b=3)[:, :, :, 0], d0, ALU.mult))
                    chain(nc.vector.reciprocal(w0, w0))
                    for t in range(TT):
                        nc.vector.tensor_scalar(w0[:, t, :], w0[:, t, :], pc_("row_ok", 1, t), None, ALU.mult).then_inc(dve_step, 1)
                    steps[0] += 2
                    dve.wait_ge(dve_step, steps[0])
                    nc.vector.tensor_tensor(pc[:, :, 0:15], pc[:, :, 0:15], wgt[:, 0:16].unsqueeze(2).to_broadcast([P, 16, 15]),
                                            ALU.mult).then_inc(cscaled, 1)

            dve.wait_ge(rel_landed, 16 * 16)
            heads_(*EVEN, between=compressed)
            outputs("even_out")
            advance(FIRST["out_even"] + 4 + 2)
            residual(FIRST["out_even"] + 4)
            norm("mlp0")
            turn("mlp0", gain=pc_("mlp0", KT))
            mlp("mlp0")
            advance(FIRST["mlp0"] + 2 * FF1 + 2)
            residual(FIRST["mlp0"] + 2 * FF1)
            nc.vector.tensor_copy(wf_hi[:, :, :], wf).then_inc(wf_ready, 1)
            dve.wait_ge(wf_ready, 1)
            nc.vector.tensor_tensor(wf_lo[:, :, :], wf, wf_hi[:, :, :].bitcast(F32), ALU.subtract).then_inc(wf_ready, 1)
            norm("mix1")
            turn("mix1", gain=pc_("mix1", KT))
            dve.wait_ge(fz_done, 1)
            chain(nc.vector.tensor_scalar(fz[:, 0, :], ps[0][0:16, 0:T], bfor[:, 0:1], None, ALU.add))
            chain(nc.vector.tensor_scalar(fz[:, 1, :], fz[:, 0, :], -1.0, None, ALU.mult))
            nc.vector.tensor_tensor(fz[:, 1, :], fz[:, 1, :], fz[:, 0, :], ALU.min).then_inc(fz_taken, 1)
            dve.wait_ge(fz_exp, 1)
            chain(nc.vector.tensor_scalar(fz[:, 0, :], fz[:, 0, :], 0.0, None, ALU.min))
            chain(nc.vector.tensor_tensor(fz[:, 0, :], fz[:, 0, :], fz[:, 3, :], ALU.subtract))
            chain(nc.vector.memset(fz[:, 1, :], 1.0))
            chain(nc.vector.tensor_tensor_scan(cum[:, :], fz[:, 1, :], fz[:, 0, :], 0.0, ALU.mult, ALU.add))
            chain(nc.vector.memset(cum_r[:, :].bitcast(F32), 0.0))
            chain(nc.vector.memset(pick_r[:, :, :].bitcast(F32), 0.0))
            for r in (0, 64):
                chain(nc.vector.tensor_copy(cum_r[r:r + 16, :], cum[:, :]))
                nc.vector.tensor_tensor(cum_r[r + 32:r + 48, :], cum[:, :], cum_r[0:16, :].bitcast(F32), ALU.subtract).then_inc(cum_ready, 1)
                for part in (0, 32):
                    for k, sign in enumerate((1.0, -1.0)):
                        nc.vector.tensor_scalar(pick_r[r + part:r + part + 16, k, :], ident[0:16, 0:16], sign, None,
                                                ALU.mult).then_inc(cum_ready, 1)
            features("qk_fox", 4)
            values("fox")
            dve.wait_ge(mask_landed, 16)
            heads_(*FOX)
            outputs("fox_out")
            advance(FIRST["out_fox"] + 4 + 2)
            residual(FIRST["out_fox"] + 4)
            norm("mlp1")
            dve.wait_ge(mod_done, 1)
            nc.vector.tensor_copy(modc[:, :], ps[7][:, 0:72]).then_inc(mod_taken, 1)
            dve.wait_ge(mod_taken, 1)
            for j, name in enumerate(("gf1", "gmix", "gf2")):
                g = gainc[:, KT * j:KT * j + KT]
                k = (3 * j + ADA_SCALE) * KT
                chain(nc.vector.tensor_scalar(g, modc[:, k:k + KT], 1.0, None, ALU.add))
                nc.vector.tensor_tensor(g, g, pc_(name, KT), ALU.mult).then_inc(gain_ready, 1)
            turn("mlp1", gain=pc_("mlp1", KT))
            mlp("mlp1")
            advance(FIRST["mlp1"] + 2 * FF1 + 2)
            residual(FIRST["mlp1"] + 2 * FF1)
            norm_scale("final")
            dve.wait_ge(h_ready, 2 * NORM["final"])
            dve.wait_ge(row_landed, 16)
            for t in range(TT):
                nc.vector.scalar_tensor_tensor(out=h[:, t, :], in0=h[:, t, :], scalar=stat[:, 7, t:t + 1], in1=row[:, :],
                                               op0=ALU.mult, op1=ALU.mult).then_inc(h_ready, 2)
            norm("gf1")
            turn("gf1", gain=gainc[:, 0:KT], shift=modc[:, 0:KT])
            glu("glu0")
            advance(FIRST["glu0"] + 3 * FF2 + 2)
            dve.wait_ge(gate_taken, 6)
            residual(FIRST["glu0"] + 3 * FF2, gate=acc_ada[:, 2 * D:3 * D])
            norm("gmix")
            turn("gmix", gain=gainc[:, KT:2 * KT], shift=modc[:, 3 * KT:4 * KT])
            features("qk_dil", 2)
            values("dil")
            dve.wait_ge(dil_landed, 32)
            heads_(*DIL)
            outputs("dil_out", pooled=True)
            advance(FIRST["out_dil"] + 4 + 2)
            residual(FIRST["out_dil"] + 4, gate=acc_ada[:, 5 * D:6 * D])
            norm("gf2")
            turn("gf2", gain=gainc[:, 2 * KT:3 * KT], shift=modc[:, 6 * KT:7 * KT])
            glu("glu1")
            residual(FIRST["glu1"] + 3 * FF2, gate=acc_ada[:, 8 * D:9 * D])
            norm_scale("last")
            dve.wait_ge(h_ready, 2 * NORM["last"])
            dve.wait_ge(row_landed, 32)
            for t in range(TT):
                nc.vector.scalar_tensor_tensor(out=tok[:, t, :], in0=h[:, t, :], scalar=stat[:, 7, t:t + 1], in1=row[:, :],
                                               op0=ALU.mult, op1=ALU.mult).then_inc(out_ready, 1)

        @block.tensor
        def _(pe):
            def three(dst, l_hi, l_lo, r_hi, r_lo, start, stop):
                nc.tensor.matmul(dst, l_hi, r_lo, start=start, stop=False)
                nc.tensor.matmul(dst, l_lo, r_hi, start=False, stop=False)
                return nc.tensor.matmul(dst, l_hi, r_hi, start=False, stop=stop)

            def feature_unit(u, slot, bank, wait_split=None):
                pe.wait_ge(lo_ready, u + 1)
                wh = w_hi[:, slot, :].rearrange("p (k c) -> p k c", k=KT)
                wl = w_lo[:, slot, :].rearrange("p (k c) -> p k c", k=KT)
                for nt in range(2):
                    for k in range(KT):
                        if wait_split is not None and nt == 0 and k % 2 == 0:
                            pe.wait_ge(act_split, wait_split + k // 2 + 1)
                        cols_ = slice(nt * P, nt * P + P)
                        ins = three(ps[bank][:, nt * T:(nt + 1) * T], wh[:, k, cols_], wl[:, k, cols_],
                                    a_hi[:, k, :], a_lo[:, k, :], k == 0, k == KT - 1)
                ins.then_inc(unit_used, 1)

            def row_unit(u, slot, l_hi, l_lo, width, start, stop):
                pe.wait_ge(lo_ready, u + 1)
                wh = w_hi[:, slot, 0:2 * width].rearrange("p (k c) -> p k c", k=2)
                wl = w_lo[:, slot, 0:2 * width].rearrange("p (k c) -> p k c", k=2)
                for k in range(2):
                    for t in range(TT):
                        for n in range(2):
                            w = min(512, width - 512 * n)
                            sl = slice(512 * n, 512 * n + w)
                            ins = three(ps[2 * t + n][:, 0:w], l_hi(k)[:, t * P:(t + 1) * P], l_lo(k)[:, t * P:(t + 1) * P],
                                        wh[:, k, sl], wl[:, k, sl], start and k == 0, stop and k == 1)
                ins.then_inc(unit_used, 1)

            def rows_phase(name, width=D, wait_split=None):
                u0 = FIRST[name]
                for j in range(4):
                    if wait_split is not None and j == 0:
                        pe.wait_ge(act_split, wait_split + 4)
                    row_unit(u0 + j, (u0 + j) % RING, lambda k: a_hi[:, 2 * j + k, :], lambda k: a_lo[:, 2 * j + k, :],
                             width, j == 0, j == 3)

            def features_phase(name, n, wait_split=None):
                u0, f0 = FIRST[name], feat_before[name]
                for j in range(n):
                    if j >= 4 or name == "q_nsa":
                        pe.wait_ge(feat_taken, f0 + j - 3)
                    feature_unit(u0 + j, (u0 + j) % RING, 4 + j % 4, wait_split if j == 0 else None)

            def turn():
                for c in range(4):
                    for k in range(2):
                        for t in range(TT):
                            kt = 2 * c + k
                            ins = nc.tensor.transpose(ps[4 + c][:, (2 * k + t) * P:(2 * k + t + 1) * P],
                                                      tok[:, t, kt * P:(kt + 1) * P], ident)
                    ins.then_inc(bank_turned, 1)

            def norm_turn(name):
                pe.wait_ge(rows_scaled, NORM_SCALED[name])
                turn()

            def standing(kind, part, t, v0):
                return v_cols(kind, part, t, v0, [[1, P]])

            WARM = (20, 20)

            def keep_clock(n):
                for _ in range(n):
                    nc.tensor.matmul(ps[5][:, 0:T], q_two[:, 0, 0, 0:P], k_two[:, 0, 0, :], start=True, stop=True)

            def attend(first, last, values, kind, between=None):
                fox = kind == "fox"
                for i in range(first, last + PV_LAG):
                    if i < last:
                        _, qt_, kt_, b = heads[i][:4]
                        if first + 1 <= i < first + TURN_LAG:
                            keep_clock(WARM[i - first - 1])
                        if i >= 2:
                            pe.wait_ge(logits_ready, i - 1)
                        bank = ps[6 + i % 2]
                        half = slice(64 * b, 64 * b + 64)
                        for t, lo, w in ((1, 0, 256), (0, 256, 128)):
                            qs = slice(t * P, (t + 1) * P)
                            nc.tensor.matmul(bank[:, lo:lo + w], q_two[:, qt_, b, qs], k_two[:, kt_, b, 0:w], start=True, stop=False)
                            ins = nc.tensor.matmul(bank[:, lo:lo + w], q_two[half, qt_, b, qs], k_lo[half, kt_, 0:w],
                                                   start=False, stop=not fox)
                            if fox:
                                hf = i - first
                                rows_ = slice(64 * b, 64 * b + 48)
                                pick, minus = pick_r[rows_, 0, hf:hf + 1], pick_r[rows_, 1, hf:hf + 1]
                                nc.tensor.matmul(bank[:, lo:lo + w], pick.to_broadcast([48, P]), cum_r[rows_, 0:w],
                                                 start=False, stop=False)
                                ins = nc.tensor.matmul(bank[:, lo:lo + w], cum_r[rows_, qs],
                                                       minus.to_broadcast([48, w]), start=False, stop=True)
                        ins.then_inc(scores_done, 1)
                    if between:
                        between(i)
                    j = i - TURN_LAG
                    if first <= j < last:
                        pe.wait_ge(probs_scaled, j + 1)
                        if j >= 2:
                            pe.wait_ge(probsT_ready, j - 1)
                        for c, src in enumerate((256, 0, 128)):
                            ins = nc.tensor.transpose(ps[4 + j % 2][:, c * P:(c + 1) * P], prob[:, j % 4, src:src + P], ident)
                        ins.then_inc(probsT_done, 1)
                    j = i - PV_LAG
                    if j >= first:
                        closes = j + 1 == last or heads[j + 1][7] != heads[j][7]
                        v0, feat, ob, opens = heads[j][4], heads[j][7], heads[j][8], heads[j][9]
                        if j == first:
                            pe.wait_ge(values_taken, values)
                        c0 = feat % 2 * T
                        bank = ps[feat // 2]
                        if first == EVEN[0] and j >= HEADS and (j - HEADS) % 4 == 0:
                            if j == HEADS:
                                pe.wait_ge(cprobsT_sb, 4)
                            for half in range(2):
                                hh = 2 * (feat - 4) + half
                                nc.tensor.matmul(bank[64 * half:64 * half + 64, c0:c0 + T], vcmp[0:15, hh // 4, :], pcT[hh // 2][0:15, hh % 2, :],
                                                 start=True, stop=False)
                        pe.wait_ge(probsT_ready, j + 1)
                        three(bank[:, c0:c0 + T], standing(kind, 0, 0, v0), standing(kind, 1, 0, v0), probT_hi[:, j % 2, 0:T],
                              probT_lo[:, j % 2, 0:T], opens, False)
                        ins = three(bank[:, c0 + P:c0 + T], standing(kind, 0, 1, v0), standing(kind, 1, 1, v0),
                                    probT_hi[:, j % 2, T:SW], probT_lo[:, j % 2, T:SW], False, closes)
                        ins.then_inc(pv_done, 1)

            NORM_SCALED = {n: 2 * i + 2 for i, n in enumerate(["mix0", "mlp0", "mix1", "mlp1", "gf1", "gmix", "gf2"])}

            pe.wait_ge(pick_landed, 16 * N_PAR_LOADS)
            pe.wait_ge(pool_step, 2)
            nc.tensor.matmul(ps[0][0:16, 0:REL], relt[:, :], rpick, start=True, stop=True).then_inc(rel_rows, 1)
            for n in range(N_CMP):
                for t in range(TT):
                    k = (2 * n + t) * P
                    pick = cpick[:, k:k + P]
                    ins = nc.tensor.matmul(ps[2][:, 16 * n + 8 * t:16 * n + 8 * t + 8], pick, relt[:, 8:16], start=True, stop=True)
            ins.then_inc(cbias_done, 1)
            pe.wait_ge(par_landed, 16)
            norm_turn("mix0")
            features_phase("qk_moba", 4, TURN["mix0"])
            features_phase("q_nsa", 4)
            pe.wait_ge(rel_rows_sb, 1)
            pe.wait_ge(cbias_taken, 1)
            rows_phase("v_even", V1W)
            u0 = FIRST["cmp"]
            for j in range(4):
                v, half = j // 2, j % 2
                u = u0 + j
                pe.wait_ge(lo_ready, u + 1)
                pe.wait_ge(blocks_ready, v + 1)
                pe.wait_ge(feat_taken, 8)
                wh = w_hi[:, u % RING, :].rearrange("p (k c) -> p k c", k=8)
                wl = w_lo[:, u % RING, :].rearrange("p (k c) -> p k c", k=8)
                for k in range(8):
                    ins = three(ps[4 + v][0:30, 0:256], blk_hi[:, v, 8 * half + k, :], blk_lo[:, v, 8 * half + k, :],
                                wh[:, k, :], wl[:, k, :], half == 0 and k == 0, half == 1 and k == 7)
                ins.then_inc(unit_used, 1)
            for v in range(2):
                pe.wait_ge(hidden_rows, v + 1)
                for ht in range(2):
                    ins = nc.tensor.transpose(ps[6][:, 64 * v + 32 * ht:64 * v + 32 * ht + 30], hid30[0:30, v, ht * P:(ht + 1) * P],
                                              ident[0:30, 0:30])
            ins.then_inc(hidden_turned, 1)
            pe.wait_ge(hidc_ready, 1)

            def compressed(i):
                if i == 0:
                    for half in range(2):
                        for g in range(2):
                            for ht in range(2):
                                nc.tensor.matmul(ps[2][64 * half:64 * half + 64, 16 * g:16 * g + 15], cw2[:, 0, ht, :],
                                                 hidc[:, 0, ht, 15 * g:15 * g + 15], start=(ht == 0), stop=(ht == 1))
                    for g in range(2):
                        for ht in range(2):
                            ins = nc.tensor.matmul(ps[3][0:15, 64 * g:64 * g + 64], hidc[:, 1, ht, 15 * g:15 * g + 15], cw2[:, 1, ht, :],
                                                   start=(ht == 0), stop=(ht == 1))
                    ins.then_inc(ckv_done, 1)
                if i == 1:
                    pe.wait_ge(ckv_taken, 3)
                    for t in range(TT):
                        for hh in range(HEADS):
                            k, g = 8 * t + hh, hh // 4
                            q_ = q_two[:, 4 + hh % 4, g, t * P:(t + 1) * P]
                            nc.tensor.matmul(ps[2][:, 16 * k:16 * k + 16], q_, kc_hi[:, g, :], start=True, stop=False)
                            ins = nc.tensor.matmul(ps[2][:, 16 * k:16 * k + 16], q_, kc_lo[:, g, :], start=False, stop=True)
                    ins.then_inc(cscores, 1)
                if 4 <= i < 8:
                    c = i - 4
                    pe.wait_ge(cscaled, 1)
                    if c >= 2:
                        pe.wait_ge(cprobsT_sb, c - 1)
                    for k in range(4):
                        hh, t = 2 * c + k // 2, k % 2
                        ins = nc.tensor.transpose(ps[2 + c % 2][0:15, k * P:(k + 1) * P], pc[:, 8 * t + hh, 0:15], ident)
                    ins.then_inc(cprobsT, 1)

            pe.wait_ge(values_taken, 4)
            attend(*EVEN, values=4, kind="even", between=compressed)
            rows_phase("out_even", wait_split=TURN["even_out"])

            def mlp(name):
                u0, f0, x0 = FIRST[name], feat_before[name], hid_before[name]
                feature_unit(u0, u0 % RING, 4, TURN[name])

                def down(u, slot, hs, x, start, stop):
                    pe.wait_ge(hid_ready, x * 3 + 3)
                    row_unit(u, slot, lambda k: hid_hi[:, hs, k * T:(k + 1) * T], lambda k: hid_lo[:, hs, k * T:(k + 1) * T],
                             D, start, stop)

                def pair_(i, j, start):
                    a = u0 + 1 + 2 * j
                    e = (lambda k, c: c) if i is None else (lambda k, c: i * k + c)
                    feature_unit(e(6, a), a % RING, 4 + (j + 1) % 3)
                    down(e(6, a + 1), (a + 1) % RING, j % 3, e(3, x0 + j), start, False)

                for j in range(3):
                    pair_(None, j, j == 0)
                with pe.Fori(1, (FF1 - 1) // 3) as i:
                    for j in range(3):
                        pair_(i, j, False)
                u = u0 + 2 * FF1 - 1
                down(u, u % RING, (FF1 - 1) % 3, x0 + FF1 - 1, False, True)

            def glu(name):
                u0, f0, x0 = FIRST[name], feat_before[name], hid_before[name]
                feature_unit(u0, u0 % RING, 4, TURN["gf1" if name == "glu0" else "gf2"])
                feature_unit(u0 + 1, (u0 + 1) % RING, 5)

                def down(u, slot, hs, x, start, stop):
                    pe.wait_ge(hid_ready, x * 3 + 3)
                    row_unit(u, slot, lambda k: hid_hi[:, hs, k * T:(k + 1) * T], lambda k: hid_lo[:, hs, k * T:(k + 1) * T],
                             D, start, stop)

                def triple(i, j, start):
                    a = u0 + 2 + 3 * j
                    e = (lambda k, c: c) if i is None else (lambda k, c: i * k + c)
                    b = 4 + 2 * ((j + 1) % 2)
                    feature_unit(e(6, a), a % RING, b)
                    feature_unit(e(6, a + 1), (a + 1) % RING, b + 1)
                    down(e(6, a + 2), (a + 2) % RING, j % 2, e(2, x0 + j), start, False)

                for j in range(2):
                    triple(None, j, j == 0)
                with pe.Fori(1, (FF2 - 1) // 2) as i:
                    for j in range(2):
                        triple(i, j, False)
                u = u0 + 3 * FF2 - 1
                down(u, u % RING, (FF2 - 1) % 2, x0 + FF2 - 1, False, True)

            norm_turn("mlp0")
            mlp("mlp0")
            norm_turn("mix1")
            pe.wait_ge(act_split, TURN["mix1"] + 4)
            pe.wait_ge(wf_ready, 2)
            for k in range(KT):
                ins = three(ps[0][0:16, 0:T], wf_hi[:, k, :], wf_lo[:, k, :], a_hi[:, k, :], a_lo[:, k, :], k == 0, k == KT - 1)
            ins.then_inc(fz_done, 1)
            features_phase("qk_fox", 8)
            pe.wait_ge(fz_taken, 1)
            rows_phase("v_fox")
            pe.wait_ge(feat_taken, feat_before["qk_fox"] + 8)
            pe.wait_ge(cum_ready, 10)
            attend(*FOX, values=8, kind="fox")
            rows_phase("out_fox", wait_split=TURN["fox_out"])
            pe.wait_ge(ada_step, ADA_STEPS)
            for v in (0, 1, 3, 4, 6, 7):
                for k in range(KT * v, KT * v + KT):
                    ins = nc.tensor.matmul(ps[7][:, k:k + 1], acc_ada[:, k * P:(k + 1) * P], ones[:, 0:1], start=True, stop=True)
            ins.then_inc(mod_done, 1)
            pe.wait_ge(mod_taken, 1)
            norm_turn("mlp1")
            mlp("mlp1")
            for j, v in enumerate((2, 5, 8)):
                for n in range(2):
                    if j == 2:
                        pe.wait_ge(gate_taken, n + 1)
                    nc.tensor.matmul(ps[4 + 2 * (j % 2) + n][:, :], ones[:, :], acc_ada[:, v * D + 512 * n:v * D + 512 * n + 512],
                                     start=True, stop=True).then_inc(gate_done, 1)
            pe.wait_ge(gate_taken, 6)
            norm_turn("gf1")
            glu("glu0")
            norm_turn("gmix")
            features_phase("qk_dil", 4, TURN["gmix"])
            rows_phase("uv_dil")
            pe.wait_ge(feat_taken, feat_before["qk_dil"] + 4)
            pe.wait_ge(dil_landed, 32)
            pe.wait_ge(pooled_taken, 2)
            for g in range(4):
                for k in range(TT):
                    ins = nc.tensor.matmul(ps[6 + g // 2][:, (g % 2) * T:(g % 2 + 1) * T], u_rows[:, k, g * P:(g + 1) * P],
                                           poolm[:, g, k, :], start=(k == 0), stop=(k == 1))
                if g % 2:
                    ins.then_inc(pooled_done, 1)
            for g in range(4):
                pe.wait_ge(pooled_taken, g // 2 + 3)
                ins = nc.tensor.matmul(ps[4 + g // 2][:, (g % 2) * T:(g % 2 + 1) * T], w_pool[:, g, :], pooledT[:, g, :],
                                       start=True, stop=True)
                if g % 2:
                    ins.then_inc(bank_turned, 1)
            pe.wait_ge(pooled_taken, 6)
            attend(*DIL, values=10, kind="dil")
            rows_phase("out_dil", wait_split=TURN["dil_out"])
            norm_turn("gf2")
            glu("glu1")




def rel_buckets(d):
    n = np.maximum(d, 0)
    nf = np.maximum(n, 1).astype(np.float32)
    large = 16 + (np.log(nf / np.float32(16)) / np.float32(np.log(64.0)) * np.float32(16)).astype(np.int32)
    return np.where(n < 16, n, np.minimum(large, 31))


def shape_constants():
    f = np.float32

    def pick(d):
        m = np.zeros((33, d.size), f)
        b = rel_buckets(d)
        m[b, np.arange(d.size)] = -1.0
        m[0:32, d < 0] = 0.0
        m[32, d < 0] = BIG
        return m

    rel_pick = pick(255 - np.arange(REL))
    q = np.arange(P)
    cmp_pick = np.concatenate(
        [pick(t * P + q - (16 * n + 31)) for n in range(N_CMP) for t in range(TT)], axis=1)
    dist = P + q[:, None] - np.arange(T)[None, :]
    fox_mask = np.where(dist < 0, BIG, 0.0).astype(f)
    count = (dist <= 128).astype(f) + (dist % 4 == 0) + (dist % 16 == 0)
    ok = (dist >= 0) & (count > 0)
    logs = np.log(np.where(ok, count, 1.0))
    dil = np.stack([np.where(ok, dist * 2.0 ** -(hh + 1) - logs, BIG) for hh in range(HEADS)], axis=1).astype(f)
    tt = np.arange(T)
    pool = np.zeros((P, 4, TT, T), f)
    for g, w in enumerate((2, 4, 8, 16)):
        m = ((tt[:, None] <= tt[None, :]) & (tt[:, None] > tt[None, :] - w)) / np.minimum(tt[None, :] + 1, w)
        m = (m - np.eye(T)).astype(f)
        pool[:, g] = m.reshape(TT, P, T).transpose(1, 0, 2)
    row_ok = (np.arange(T) >= 31).astype(f).reshape(TT, P).T
    return rel_pick, cmp_pick, fox_mask, dil, pool, row_ok


def lay_out(a):
    def feats(w):
        n = w.shape[1] // T
        return w.reshape(KT, P, n, T).transpose(2, 1, 0, 3).reshape(n, P, UNIT)

    def rows(w):
        n, width = w.shape[0] // T, w.shape[1]
        u = w.reshape(n, 2, P, width).transpose(0, 2, 1, 3).reshape(n, P, 2 * width)
        if 2 * width < UNIT:
            u = np.concatenate([u, np.zeros((n, P, UNIT - 2 * width), u.dtype)], axis=2)
        return u

    def mlp(w1, w2):
        first, second = feats(w1), rows(w2)
        order = [first[0:1]]
        for j in range(FF1 - 1):
            order += [first[j + 1:j + 2], second[j:j + 1]]
        return order + [second[FF1 - 1:]]

    def glu(wg, wu, wd):
        g, u, d = feats(wg), feats(wu), rows(wd)
        order = [g[0:1], u[0:1]]
        for j in range(FF2 - 1):
            order += [g[j + 1:j + 2], u[j + 1:j + 2], d[j:j + 1]]
        return order + [d[FF2 - 1:]]

    w = a["even_w_in"][0]
    nq = w[:, 1536:2048].reshape(D, 2, 4, HD).transpose(0, 2, 1, 3).reshape(D, 512)
    c = {n: w[:, 2048 + 128 * i:2176 + 128 * i] for i, n in enumerate(("kc", "vc", "ks", "vs", "kw", "vw"))}
    parts = [feats(w[:, 0:1024])]
    parts += [feats(np.concatenate([nq, c["ks"], c["kw"], c["kc"], c["vc"]], axis=1))]
    parts += [rows(np.concatenate([w[:, 1024:1536], c["vs"], c["vw"], w[:, 2816:2840]], axis=1))]
    parts += [feats(a[n][0].reshape(2, 1024, 256).transpose(1, 0, 2).reshape(1024, 512)) for n in ("cmp_k_w1", "cmp_v_w1")]
    parts += [rows(a["even_w_out"][0])]
    parts += mlp(a["mlp_w1"][0], a["mlp_w2"][0])
    wo = a["odd_w_in"][0]
    parts += [feats(wo[:, 0:2048]), rows(wo[:, 2048:3072]), rows(a["odd_w_out"][0])]
    parts += mlp(a["mlp_w1"][1], a["mlp_w2"][1])
    parts += glu(a["w1_gate_2"][0], a["w1_up_2"][0], a["w1_down_2"][0])
    w2 = a["w_in_2"][0]
    parts += [feats(w2[:, 512:1536]), rows(np.concatenate([w2[:, 0:512], w2[:, 1536:2048]], axis=1)), rows(a["w_out_2"][0])]
    parts += glu(a["w2_gate_2"][0], a["w2_up_2"][0], a["w2_down_2"][0])
    stream = np.concatenate(parts, axis=0)
    assert stream.shape == (N_UNITS, P, UNIT)
    n = ADA_W // ADA_PIECE
    ada = a["w_ada_2"][0].reshape(KT, P, n, ADA_PIECE).transpose(2, 0, 1, 3)[::-1].reshape(n * KT, P, ADA_PIECE)

    def col(v):
        return v.reshape(-1, P).T

    rel_pick, cmp_pick, fox_mask, dil, pool, row_ok = shape_constants()
    w2s = np.stack([a[n][0].reshape(2, P, HD) for n in ("cmp_k_w2", "cmp_v_w2")]).transpose(2, 0, 1, 3).reshape(P, 256)
    cols = np.concatenate([
        w2s, col(a["mix_norm"][0]), col(a["mlp_norm"][0]), col(a["mix_norm"][1]), col(a["mlp_norm"][1]),
        col(a["g_ffn1_2"][0]), col(a["g_mix_2"][0]), col(a["g_ffn2_2"][0]), col(a["pool_scale_2"][0]),
        col(a["cmp_pos_k"][0].reshape(-1)), col(a["cmp_pos_v"][0].reshape(-1)), col(a["c_2"][0]), row_ok,
        a["w_pool_2"][0].transpose(1, 0, 2).reshape(P, 512),
        wo[:, 3072:3088].reshape(KT, P, 16).transpose(1, 0, 2).reshape(P, 128), np.eye(P, dtype=np.float32)], axis=1)
    assert cols.shape == (P, N_COLS)
    return {
        "stream": stream, "ada": ada, "cols": cols, "x": a["x"][0], "rel_table": a["rel_bias"],
        "rel_pick": rel_pick, "cmp_pick": cmp_pick, "fox_mask": fox_mask, "dil_bias": dil, "pool_mat": pool,
        "b_ada": a["b_ada_2"], "b_forget": a["odd_b_forget"][0].reshape(16, 1),
        "final_norm": a["final_norm"], "g_final": a["g_final_2"],
    }


def kernel(**inputs):
    import concourse.bacc as bacc
    from concourse.bass_utils import run_bass_kernel_spmd

    arrays = {k: np.ascontiguousarray(v) for k, v in lay_out({k: np.asarray(v) for k, v in inputs.items()}).items()}
    nc = bacc.Bacc("TRN2", target_bir_lowering=False, num_devices=1)
    args = {k: nc.dram_tensor("in_" + k, v.shape, mybir.dt.from_np(v.dtype), kind="ExternalInput").ap() for k, v in arrays.items()}
    out = nc.dram_tensor("out", (T, D), F32, kind="ExternalOutput").ap()
    build(nc, out=out, **args)
    r = run_bass_kernel_spmd(nc, [{"in_" + k: v for k, v in arrays.items()}], core_ids=[0])
    return r.results[0]["out"].reshape(1, T, D)
```

```python
from contextlib import ExitStack

import numpy as np

import concourse.bass as bass
from concourse import mybir

F32 = mybir.dt.float32
F32R = mybir.dt.float32r
ALU = mybir.AluOpType
ACT = mybir.ActivationFunctionType
AX_X = mybir.AxisListType.X

P = 128
T = 256
TT = T // P
D = 1024
KT = D // P
HD = 64
HEADS = 8
UNIT = 2048
RING = 3
FF1 = 4096 // T
FF2 = 2816 // T
N_CMP = 15
V1W = 792
BIG = 1e30
SW = 384
REL = 2 * P + T - 1

PHASES = [
    ("qk_moba", 4), ("q_nsa", 4), ("v_even", 4), ("cmp", 4), ("out_even", 4), ("mlp0", 2 * FF1),
    ("qk_fox", 8), ("v_fox", 4), ("out_fox", 4), ("mlp1", 2 * FF1),
    ("glu0", 3 * FF2), ("qk_dil", 4), ("uv_dil", 4), ("out_dil", 4), ("glu1", 3 * FF2),
]
FIRST = {}
N_UNITS = 0
for _name, _n in PHASES:
    FIRST[_name] = N_UNITS
    N_UNITS += _n
ADA_PIECE = 512
ADA_W = 9 * D

COLS = {}
N_COLS = 0
for _name, _n in [("cmp_w2", 256), ("mix0", 8), ("mlp0", 8), ("mix1", 8), ("mlp1", 8), ("gf1", 8), ("gmix", 8), ("gf2", 8),
                  ("pool_scale", 4), ("pos", 32), ("c", 8), ("row_ok", 2),
                  ("w_pool", 512), ("w_forget", 128), ("ident", 128)]:
    COLS[_name] = N_COLS
    N_COLS += _n

PAIR = 3 * HD
NSA_V = 4 * PAIR
VW = {"even": NSA_V + HD + 4 * 2 * HD, "fox": 8 * PAIR, "dil": 4 * PAIR}

ADA_SHIFT, ADA_SCALE, ADA_GATE = 0, 1, 2
SET_CMP, SET_MOBA, SET_SLC, SET_WIN, SET_FOX0, SET_FOX1, SET_DIL = range(7)


def build(nc, stream, ada, cols, x, rel_table, rel_pick, cmp_pick, fox_mask, dil_bias, pool_mat,
          b_ada, b_forget, final_norm, g_final, out):
    ctx = ExitStack()
    with ctx:
        base = [-(-nc.sbuf_base // 64) * 64]

        def place(name, shape, dt=F32, at=None):
            size = -(-int(np.prod(shape[1:])) * 4 // 64) * 64
            if at is None:
                at = base[0]
                base[0] += size
            t = nc.alloc_sbuf_tensor_at(name, list(shape), dt, offset=at)
            return t

        def sem(name):
            return ctx.enter_context(nc.semaphore(name))

        raw = place("raw", [P, RING, UNIT])
        w_hi = place("w_hi", [P, RING, UNIT], F32R)
        w_lo = place("w_lo", [P, RING, UNIT], F32R)
        V_at = base[0]
        a_hi = place("a_hi", [P, KT, T], F32R)
        a_lo = place("a_lo", [P, KT, T], F32R)
        tok_at = base[0]
        tok = place("tok", [P, TT, D])
        V_all = place("V_all", [P, 2 * TT * VW["fox"]], F32R, at=V_at)

        h = place("h", [P, TT, D])
        work_at = base[0]
        work = place("work", [P, 3072])
        probT_hi = place("probT_hi", [P, 2, SW], F32R, at=work_at + 6 * SW * 4)
        probT_lo_at = base[0]
        probT_lo = place("probT_lo", [P, 2, SW], F32R)
        qkv_at = base[0]
        q_two = place("q_two", [P, 8, 2, T], F32R)
        k_two = place("k_two", [P, 8, 2, T], F32R)
        k_lo = place("k_lo", [P, 8, T], F32R)
        pooled_y = place("pooled_y", [P, 2, 2 * T], at=qkv_at + 4 * 2 * T * 4)
        hid_hi = place("hid_hi", [P, 3, 2 * T], F32R, at=qkv_at)
        hid_lo = place("hid_lo", [P, 3, 2 * T], F32R, at=qkv_at + 3 * 2 * T * 4)
        blk_hi = place("blk_hi", [P, 2, 16, 30], F32R, at=work_at + 2048 * 4)
        blk_lo = place("blk_lo", [P, 2, 16, 30], F32R, at=qkv_at + (8 + 6) * 2 * T * 4)
        acc_ada = place("acc_ada", [P, ADA_W])
        ada_at = base[0]
        ada_raw = place("ada_raw", [P, 2, ADA_PIECE])
        row = place("row", [P, D], at=ada_at)
        fmask_at = base[0]
        fmask = place("fmask", [P, T])
        par_at = base[0]
        par = place("par", [P, N_COLS])
        cmp_bias = place("cmp_bias", [P, 16, 16], at=fmask_at)
        kc = place("kc", [P, 2, 2, 16], F32R)
        vcmp = place("vcmp", [16, 2, HD], at=V_at + 4 * VW["even"] * 4)
        hidc = place("hidc", [P, 2, 2, 32], at=probT_lo_at)
        ones = place("ones", [P, P])
        low = place("low", [P, 7 * 16])
        den = place("den", [P, 7 * 16])
        wgt = place("wgt", [P, 7 * 16])
        gates_at = base[0]
        inv_gates = place("inv_gates", [P, TT, 24])
        gates_e = place("gates_e", [P, TT, 24], at=probT_lo_at + 512)
        stat = place("stat", [P, 16, 2])
        modc = place("modc", [P, 9 * KT])
        gainc = place("gainc", [P, 3 * KT])
        silu_c = place("silu_c", [P, KT])
        wf_hi = place("wf_hi", [P, KT, 16], F32R, at=probT_lo_at)
        wf_lo = place("wf_lo", [P, KT, 16], F32R, at=probT_lo_at + KT * 16 * 4)
        fz = place("fz", [16, 4, T], at=tok_at)
        cum = place("cum", [16, T], at=tok_at + 4 * T * 4)
        cum_r = place("cum_r", [112, T], F32R, at=par_at + COLS["cmp_w2"] * 4)
        pick_r = place("pick_r", [112, 2, 16], F32R, at=gates_at)
        bfor = stat[0:16, 8, 0:1]
        relt = place("relt", [33, 16], at=qkv_at + (8 + 7) * 2 * T * 4)
        assert base[0] <= nc.sbuf_usable_end, (base[0], nc.sbuf_usable_end)
        rel_bias = acc_ada[:, 0:16 * T].rearrange("p (a b) -> p a b", a=16)
        dil_b = acc_ada[:, 0:2 * D].rearrange("p (a b) -> p a b", a=8)
        poolm = acc_ada[:, 3 * D:5 * D].rearrange("p (g k t) -> p g k t", g=4, k=2)
        rpick = work[0:33, 0:REL]
        rrow = work[0:16, 1024:1024 + REL]
        cpick = acc_ada[0:33, 16 * T:16 * T + N_CMP * P]
        u_rows = tok[:, 0, :].rearrange("p (t c) -> p t c", t=TT)
        pooledT = tok[:, 1, :].rearrange("p (g t) -> p g t", g=4)
        logit = work[:, 0:2 * SW].rearrange("p (b c) -> p b c", b=2)
        prob = work[:, 2 * SW:6 * SW].rearrange("p (b c) -> p b c", b=4)
        hid_act = work[:, 0:1536].rearrange("p (b c) -> p b c", b=3)
        hid_f = work[:, 1536:2048]
        shifted = work[:, 0:1024].rearrange("p (b c) -> p b c", b=2)
        pair = work[:, 0:1024].rearrange("p (v g t) -> p v g t", v=2, g=2)
        blk = work[:, 1024:1984].rearrange("p (v j n) -> p v j n", v=2, j=16)
        hid30 = place("hid30", [30, 2, 256], at=qkv_at + (8 + 6) * 2 * T * 4)
        pcT = [place(f"pcT{c}", [16, 2, T], at=at_) for c, at_ in enumerate((
            qkv_at + (8 + 6) * 2 * T * 4, qkv_at + (8 + 7) * 2 * T * 4, qkv_at + (16 * 2 + 6) * T * 4,
            V_at + 4 * VW["even"] * 4 + 2 * HD * 4))]
        assert 4 * VW["even"] + 2 * HD + 2 * T <= 3 * TT * D
        pc = cmp_bias

        def pc_(name, n, k=0):
            return par[:, COLS[name] + k:COLS[name] + k + n]

        ident = pc_("ident", P)
        cw2 = pc_("cmp_w2", 256).rearrange("p (v t d) -> p v t d", v=2, t=2)
        w_pool = pc_("w_pool", 512).rearrange("p (g d) -> p g d", g=4)
        wf = pc_("w_forget", 128).rearrange("p (k h) -> p k h", k=KT)

        ps = [ctx.enter_context(nc.psum_tensor(f"bank{i}", [P, 512], F32)) for i in range(8)]
        rel_dram = nc.dram_tensor("rel_scratch", (16, P, REL + 1), F32)

        par_landed = sem("par_landed")
        x_landed = [sem("x_landed0"), sem("x_landed1")]
        pick_landed = sem("pick_landed")
        cpick_landed = sem("cpick_landed")
        mask_landed = sem("mask_landed")
        feat_hi = sem("feat_hi")
        val_hi = sem("val_hi")
        probsT_hi = sem("probsT_hi")
        raw_landed = [sem(f"raw_landed{i}") for i in range(RING)]
        hi_ready = sem("hi_ready")
        lo_ready = sem("lo_ready")
        unit_used = sem("unit_used")
        feat_taken = sem("feat_taken")
        values_taken = sem("values_taken")
        hid_ready = sem("hid_ready")
        h_ready = sem("h_ready")
        sumsq = sem("sumsq")
        mean_ready = sem("mean_ready")
        root_ready = sem("root_ready")
        sums_done = sem("sums_done")
        rows_scaled = sem("rows_scaled")
        bank_turned = sem("bank_turned")
        act_high = sem("act_high")
        act_split = sem("act_split")
        dve_step = sem("dve_step")
        act_step = sem("act_step")
        pool_step = sem("pool_step")
        rel_rows = sem("rel_rows")
        rel_rows_sb = sem("rel_rows_sb")
        rel_stored = sem("rel_stored")
        rel_landed = sem("rel_landed")
        cbias_done = sem("cbias_done")
        cbias_taken = sem("cbias_taken")
        blocks_ready = sem("blocks_ready")
        hidden_rows = sem("hidden_rows")
        hidden_turned = sem("hidden_turned")
        hidc_ready = sem("hidc_ready")
        ckv_done = sem("ckv_done")
        ckv_taken = sem("ckv_taken")
        cscores = sem("cscores")
        cshifted = sem("cshifted")
        cprobs = sem("cprobs")
        cscaled = sem("cscaled")
        cprobsT = sem("cprobsT")
        cprobsT_sb = sem("cprobsT_sb")
        gates_exp = sem("gates_exp")
        scores_done = sem("scores_done")
        logits_ready = sem("logits_ready")
        probs_ready = sem("probs_ready")
        probsT_done = sem("probsT_done")
        probsT_ready = sem("probsT_ready")
        weight_ready = sem("weight_ready")
        probs_scaled = sem("probs_scaled")
        pv_done = sem("pv_done")
        wf_ready = sem("wf_ready")
        fz_done = sem("fz_done")
        fz_taken = sem("fz_taken")
        fz_exp = sem("fz_exp")
        cum_ready = sem("cum_ready")
        ada_landed = [sem("ada_landed0"), sem("ada_landed1")]
        bada_landed = sem("bada_landed")
        silu_ready = sem("silu_ready")
        ada_step = sem("ada_step")
        ADA_STEPS = 2 * KT * (ADA_W // ADA_PIECE)
        mod_done = sem("mod_done")
        mod_taken = sem("mod_taken")
        gate_done = sem("gate_done")
        gate_taken = sem("gate_taken")
        gain_ready = sem("gain_ready")
        dil_landed = sem("dil_landed")
        row_landed = sem("row_landed")
        pooled_done = sem("pooled_done")
        pooled_taken = sem("pooled_taken")
        out_ready = sem("out_ready")
        out_stored = sem("out_stored")

        heads = []

        def head(s, hh, qt, kt, b, v0, bias, gate, feat, opens):
            heads.append((16 * s + hh, qt, kt, b, v0, bias, gate, feat, hh % 2, opens))

        def pair_col(hh):
            return PAIR * (hh // 2) + HD * (hh % 2)

        def v_cols(kind, part, t, c0, counts):
            at = (part * TT + t) * VW[kind] + c0
            return bass.AP(V_all, at, [list(V_all[:, 0:1].ap[0])] + [list(c) for c in counts])

        def value_moves(kind):
            moves = []
            for t in range(TT):
                if kind != "dil":
                    moves.append((t, 2 * t, 512, 0, [[PAIR, 4], [2 * HD, 2], [1, HD]], "p (a b c) -> p a b c", dict(b=2, c=HD)))
                if kind == "even":
                    moves.append((t, 2 * t + 1, 256, NSA_V + HD, [[2 * HD, 4], [1, HD]], "p (a c) -> p a c", dict(c=HD)))
                else:
                    moves.append((t, 2 * t + 1, 512, 0 if kind == "dil" else 4 * PAIR, [[PAIR, 4], [2 * HD, 2], [1, HD]],
                                  "p (a b c) -> p a b c", dict(b=2, c=HD)))
            return moves

        for hh in range(HEADS):
            head(SET_MOBA, hh, hh // 2, hh // 2, hh % 2, pair_col(hh), rel_bias[:, hh, :], None, hh // 2, hh % 2 == 0)
        for hh in range(HEADS):
            g = hh // 4
            for s, kt_, v, br in ((SET_SLC, 4, g, 1), (SET_WIN, 5, 2 + g, 2)):
                head(s, hh, 4 + hh % 4, kt_, g, NSA_V + HD + 2 * HD * v - HD * (hh % 2), rel_bias[:, 8 + hh, :], inv_gates[:, :, 3 * hh + br],
                     4 + hh // 2, False)
        for hh in range(2 * HEADS):
            head(SET_FOX0 + hh // 8, hh % 8, hh // 2, hh // 2, hh % 2, pair_col(hh), fmask[:, :], None, hh // 2, hh % 2 == 0)
        for hh in range(HEADS):
            head(SET_DIL, hh, hh // 2, hh // 2, hh % 2, pair_col(hh), dil_b[:, hh, :], None, 4 + hh // 2, hh % 2 == 0)
        EVEN = (0, 24)
        FOX = (24, 40)
        DIL = (40, 48)
        SCALE_LAG, TURN_LAG, ROUND_LAG, PV_LAG = 1, 3, 4, 5

        TURN = {n: 4 * i for i, n in enumerate(
            ["mix0", "even_out", "mlp0", "mix1", "fox_out", "mlp1", "gf1", "gmix", "dil_out", "gf2"])}
        BANK = {"mix0": 0, "mlp0": 4, "mix1": 8, "mlp1": 12, "gf1": 16, "gmix": 20, "pooled": 24, "gf2": 26}
        NORM = {n: 2 * i for i, n in enumerate(
            ["mix0", "mlp0", "mix1", "mlp1", "final", "gf1", "gmix", "gf2", "last"])}
        EPS = {n: (1e-5 if n in ("mix0", "mlp0", "mix1", "mlp1", "final") else 1e-6) for n in NORM}
        SUMS = {n: 3 * i for i, n in enumerate(["out_even", "mlp0", "out_fox", "mlp1", "glu0", "out_dil", "glu1"])}

        feat_before = {}
        n = 0
        for name, k in (("qk_moba", 4), ("q_nsa", 4), ("mlp0", FF1), ("qk_fox", 8), ("mlp1", FF1),
                        ("glu0", FF2), ("qk_dil", 4), ("glu1", FF2)):
            feat_before[name] = n
            n += k
        MOD_BANK = (6, 7, 0)
        DIL_MOD = 9
        V_PHASE = {"even": "v_even", "fox": "v_fox", "dil": "uv_dil"}
        V_BEFORE = {"even": 0, "fox": 4, "dil": 8}
        hid_before = {"mlp0": 0, "mlp1": FF1, "glu0": 2 * FF1, "glu1": 2 * FF1 + FF2}

        block = ctx.enter_context(nc.Block())

        @block.sync
        def _(sp):
            for t in range(TT):
                sp.dma_start(h[:, t, :], x[t * P:(t + 1) * P, :]).then_inc(x_landed[t], 16)
            sp.dma_start(par[:, :], cols[:, :]).then_inc(par_landed, 16)
            for u in range(RING):
                sp.dma_start(raw[:, u, :], stream[u]).then_inc(raw_landed[u], 16)
            with sp.Fori(1, N_UNITS // RING) as i:
                for s in range(RING):
                    sp.wait_ge(lo_ready, i * RING + (s - RING + 1))
                    sp.dma_start(raw[:, s, :], stream[i * RING + s]).then_inc(raw_landed[s], 16)
            for u in range(N_UNITS - N_UNITS % RING, N_UNITS):
                sp.wait_ge(lo_ready, u - RING + 1)
                sp.dma_start(raw[:, u % RING, :], stream[u]).then_inc(raw_landed[u % RING], 16)
            for t in range(TT):
                sp.wait_ge(out_ready, t + 1)
                sp.dma_start(out[t * P:(t + 1) * P, :], tok[:, t, :]).then_inc(out_stored, 16)
            sp.wait_ge(out_stored, 16 * TT)

        @block.gpsimd
        def _(pool):
            pool.memset(ones[:, :], 1.0).then_inc(pool_step, 1)
            pool.wait_ge(pool_step, 1)
            pool.memset(relt[32:33, :], 1.0).then_inc(pool_step, 1)
            for s in range(2):
                pool.dma_start(ada_raw[:, s, :], ada[s]).then_inc(ada_landed[s], 16)
            pool.wait_ge(cbias_taken, 1)
            pool.wait_ge(pool_step, 2)
            pool.memset(acc_ada[:, 4 * D:9 * D], 0.0).then_inc(pool_step, 1)
            pool.wait_ge(pool_step, 3)
            pool.dma_start(acc_ada[0:1, 4 * D:9 * D], b_ada[:, 4 * D:9 * D]).then_inc(bada_landed, 16)
            pool.wait_ge(bada_landed, 16)
            pool.wait_ge(silu_ready, 1)
            n_ada = ADA_W // ADA_PIECE * KT
            for nb in range(ADA_W // ADA_PIECE):
                c0 = ADA_W - ADA_PIECE * (nb + 1)
                if c0 == 4 * D - ADA_PIECE:
                    pool.wait_ge(logits_ready, EVEN[1])
                    pool.memset(acc_ada[:, 0:4 * D], 0.0).then_inc(pool_step, 1)
                    pool.wait_ge(pool_step, 4)
                    pool.dma_start(acc_ada[0:1, 0:4 * D], b_ada[:, 0:4 * D]).then_inc(bada_landed, 16)
                    pool.wait_ge(bada_landed, 32)
                for k in range(KT):
                    v = KT * nb + k
                    s = v % 2
                    part = ada_raw[:, s, :]
                    pool.wait_ge(ada_landed[s], 16 * (v // 2 + 1))
                    pool.tensor_scalar(part, part, silu_c[:, k:k + 1], 1.0, ALU.mult, ALU.mult).then_inc(ada_step, 1)
                    pool.wait_ge(ada_step, 2 * v + 1)
                    acc = acc_ada[:, c0:c0 + ADA_PIECE]
                    pool.tensor_tensor(acc, acc, part, ALU.add).then_inc(ada_step, 1)
                    pool.wait_ge(ada_step, 2 * v + 2)
                    if v + 2 < n_ada:
                        pool.dma_start(ada_raw[:, s, :], ada[v + 2]).then_inc(ada_landed[s], 16)

        @block.scalar
        def _(act):
            steps = [0]

            def chain(ins):
                steps[0] += 1
                ins.then_inc(act_step, 1)
                act.wait_ge(act_step, steps[0])

            def round_high(u, slot, landed):
                act.wait_ge(raw_landed[slot], landed)
                if not isinstance(u, int) or u >= RING:
                    act.wait_ge(unit_used, u - (RING - 1))
                nc.scalar.activation(w_hi[:, slot, :], raw[:, slot, :], ACT.Copy).then_inc(hi_ready, 1)

            sent = [0]

            def advance(upto):
                while sent[0] < min(upto, N_UNITS):
                    u = sent[0]
                    round_high(u, u % RING, 16 * (u // RING + 1))
                    sent[0] += 1

            def round_in_loop(i, step, u0):
                round_high(i * step + u0, u0 % RING, i * (16 * step // RING) + 16 * (u0 // RING + 1))

            def norm(name):
                n = NORM[name]
                nc.scalar.activation(stat[:, 10, :], stat[:, 9, :], ACT.Sqrt)
                for t in range(TT):
                    for k in range(2):
                        if name == "mix0":
                            act.wait_ge(x_landed[t], 16)
                        else:
                            act.wait_ge(h_ready, 2 * (n - 2) + 2 * t + k + 1)
                        half = slice(512 * k, 512 * k + 512)
                        nc.scalar.activation(tok[:, t, half], h[:, t, half], ACT.Square, scale=1.0 / 32,
                                             accum_out=stat[:, k, t:t + 1]).then_inc(sumsq, 1)
                    act.wait_ge(mean_ready, n + t + 1)
                    nc.scalar.activation(stat[:, 3, t:t + 1], stat[:, 2, t:t + 1], ACT.Sqrt).then_inc(root_ready, 1)

            def turn(name, gain, shift=None):
                n, m = BANK[name], TURN[name]
                for c in range(4):
                    act.wait_ge(bank_turned, n + c + 1)
                    if shift is not None and c >= 2:
                        act.wait_ge(act_split, m + c - 1)
                    for k in range(2):
                        kt = 2 * c + k
                        src = ps[4 + c][:, k * T:(k + 1) * T]
                        if shift is None:
                            ins = nc.scalar.activation(a_hi[:, kt, :], src, ACT.Identity,
                                                       scale=gain[:, kt:kt + 1])
                        else:
                            ins = nc.scalar.activation(shifted[:, c % 2, k * T:(k + 1) * T], src, ACT.Identity,
                                                       bias=shift[:, kt:kt + 1], scale=gain[:, kt:kt + 1])
                    ins.then_inc(act_high, 1)

            def outputs(n_heads, pooled=False):
                act.wait_ge(pv_done, n_heads)
                for c in range(4):
                    src = pooled_y[:, c, :] if pooled and c < 2 else ps[c][:, :]
                    nc.scalar.activation(a_hi[:, 2 * c:2 * c + 2, :], src, ACT.Copy).then_inc(act_high, 1)

            def stack(j, tile, scale, keys):
                for b in range(2):
                    src = ps[4 + j % 4][64 * b:64 * b + 64, :].rearrange("p (a b) -> p a b", a=2)
                    two = k_two if keys else q_two
                    for half in ((b, 1 - b) if keys else (b,)):
                        ins = nc.scalar.activation(two[64 * half:64 * half + 64, tile:tile + 2, b, :], src, ACT.Copy, scale=scale)
                ins.then_inc(feat_hi, 1)

            def features(name, n, after={}):
                u0 = FIRST[name]
                for j in range(2 * n):
                    advance(u0 + j + RING)
                    act.wait_ge(unit_used, u0 + j + 1)
                    stack(j, 2 * (j % n), -0.125 if j < n else 1.0, j >= n)
                    if j in after:
                        after[j]()

            def values(kind):
                last = FIRST[V_PHASE[kind]] + 4
                advance(last + 2)
                for t, bank, w, c0, counts, form, sizes in value_moves(kind):
                    act.wait_ge(unit_used, last)
                    nc.scalar.activation(v_cols(kind, 0, t, c0, counts), ps[bank][:, 0:w].rearrange(form, **sizes),
                                         ACT.Copy).then_inc(val_hi, 1)

            def take_gate(j, banks):
                v = 3 * j + ADA_GATE
                for n in range(2):
                    act.wait_ge(gate_done, 2 * j + n + 1)
                    nc.scalar.activation(acc_ada[:, v * D + 512 * n:v * D + 512 * n + 512], ps[banks[n]][:, :],
                                         ACT.Copy, scale=(1.0 if j == 1 else 0.5)).then_inc(gate_taken, 1)

            def soft(first, last, between=None):
                for i in range(first, last + ROUND_LAG):
                    j = i - ROUND_LAG
                    if j >= first:
                        act.wait_ge(probsT_done, j + 1)
                        if j >= 2:
                            act.wait_ge(pv_done, j - 1)
                        nc.scalar.activation(probT_hi[:, j % 2, :], ps[4 + j % 2][:, 0:SW], ACT.Copy).then_inc(probsT_hi, 1)
                    if i < last:
                        k = heads[i][0]
                        act.wait_ge(logits_ready, i + 1)
                        if i >= 4:
                            act.wait_ge(probsT_done, i - 3)
                        for t, lo, hi in ((1, 0, 256), (0, 256, 384)):
                            kk = k + 8 * t
                            ins = nc.scalar.activation(prob[:, i % 4, lo:hi], logit[:, i % 2, lo:hi], ACT.Exp, scale=-1.0,
                                                       bias=low[:, kk:kk + 1], accum_out=den[:, kk:kk + 1])
                        ins.then_inc(probs_ready, 1)
                    if between:
                        between(i)
            def mlp(name):
                u0 = FIRST[name]
                f0 = FIRST[name]
                advance(u0 + RING)
                act.wait_ge(unit_used, u0 + 1)
                nc.scalar.activation(hid_act[:, 0, :], ps[4][:, :], ACT.Relu).then_inc(feat_taken, 1)
                with act.Fori(0, (FF1 - 1) // 3) as i:
                    for j in range(3):
                        a = u0 + 1 + 2 * j
                        round_in_loop(i, 6, a + 2)
                        act.wait_ge(unit_used, i * 6 + (a + 1))
                        nc.scalar.activation(hid_act[:, (j + 1) % 3, :], ps[4 + (j + 1) % 3][:, :], ACT.Relu).then_inc(feat_taken, 1)
                        round_in_loop(i, 6, a + 3)
                sent[0] = u0 + 2 * FF1 - 1 + 2
                assert f0 == u0

            def glu(name):
                u0 = FIRST[name]
                last = name == "glu1"
                advance(u0 + RING)
                advance(u0 + RING + 1)
                act.wait_ge(unit_used, u0 + 2)
                nc.scalar.activation(hid_act[:, 0, :], ps[4][:, :], ACT.Silu).then_inc(feat_taken, 1)

                def block_(i, j):
                    a = u0 + 2 + 3 * j
                    if i is None:
                        advance(a + 3)
                    else:
                        round_in_loop(i, 6, a + 2)
                    slot = (j + 1) % 2
                    if i is None:
                        act.wait_ge(unit_used, a + 2)
                    else:
                        act.wait_ge(unit_used, i * 6 + (a + 1))
                    nc.scalar.activation(hid_act[:, slot, :], ps[4 + 2 * slot][:, :], ACT.Silu).then_inc(feat_taken, 1)
                    for k in (3, 4):
                        if i is None:
                            advance(a + k + 1)
                        else:
                            round_in_loop(i, 6, a + k)

                n_loop = (FF2 - 1) // 2 - (1 if last else 0)
                with act.Fori(0, n_loop) as i:
                    block_(i, 0)
                    block_(i, 1)
                sent[0] = u0 + 2 + 6 * n_loop + 2
                if last:
                    block_(None, 2 * n_loop)
                    block_(None, 2 * n_loop + 1)

            for dst, src in ((relt[0:32, :], rel_table), (rpick, rel_pick)):
                act.dma_start(dst, src).then_inc(pick_landed, 16)
            for dst, src in ((cpick, cmp_pick), (bfor[:, :], b_forget)):
                act.dma_start(dst, src).then_inc(cpick_landed, 16)
            act.wait_ge(dve_step, 1)
            norm("mix0")
            act.wait_ge(rel_rows, 1)
            nc.scalar.activation(rrow, ps[0][0:16, 0:REL], ACT.Copy).then_inc(rel_rows_sb, 1)
            act.wait_ge(rel_rows_sb, 1)
            act.dma_start(rel_dram[:, :, 0:REL], rrow.unsqueeze(1).to_broadcast([16, P, REL])).then_inc(rel_stored, 16)
            advance(2)
            act.wait_ge(par_landed, 16)
            turn("mix0", gain=pc_("mix0", KT))
            nc.scalar.activation(silu_c[:, :], pc_("c", KT), ACT.Silu).then_inc(silu_ready, 1)
            features("qk_moba", 2)
            act.wait_ge(rel_stored, 16)
            for hh in range(16):
                band = bass.AP(rel_dram, hh * P * (REL + 1) + P - 1, [[REL, P], [1, T]])
                act.dma_start(rel_bias[:, hh, :], band).then_inc(rel_landed, 16)
            u0 = FIRST["q_nsa"]
            for j in range(3):
                advance(u0 + j + RING)
                act.wait_ge(unit_used, u0 + j + 1)
                stack(j, 4 + 2 * (j % 2), -0.125 if j < 2 else 1.0, j == 2)
            advance(u0 + 3 + RING)
            act.wait_ge(unit_used, u0 + 4)
            for v in range(2):
                for g in range(2):
                    src = ps[7][64 * g:64 * g + 64, v * T:(v + 1) * T]
                    nc.scalar.activation(pair[0:64, v, g, :], src, ACT.Copy)
                    ins = nc.scalar.activation(pair[64:128, v, g, 0:T - 1], src[:, 1:T], ACT.Copy)
            ins.then_inc(feat_taken, 1)
            advance(FIRST["v_even"] + 4 + 2)
            act.wait_ge(unit_used, FIRST["v_even"] + 4)
            for t in range(TT):
                ins = nc.scalar.activation(gates_e[:, t, :], ps[2 * t + 1][:, 256:280], ACT.Exp, scale=-1.0)
            ins.then_inc(gates_exp, 1)
            values("even")
            advance(FIRST["cmp"] + 4 + 2)
            for v in range(2):
                act.wait_ge(unit_used, FIRST["cmp"] + 2 * v + 2)
                nc.scalar.activation(hid30[0:30, v, :], ps[4 + v][0:30, 0:256], ACT.Silu).then_inc(hidden_rows, 1)
            act.wait_ge(hidden_turned, 1)
            nc.scalar.activation(hidc[:, :, :, 0:30], ps[6][:, 0:128].rearrange("p (v h n) -> p v h n", v=2, h=2)[:, :, :, 0:30],
                                 ACT.Copy).then_inc(hidc_ready, 1)

            def compressed(i):
                if i == 0:
                    act.wait_ge(ckv_done, 1)
                    nc.scalar.activation(kc[:, :, 0, 0:15], ps[2][:, 0:32].rearrange("p (g n) -> p g n", g=2)[:, :, 0:15],
                                         ACT.Copy).then_inc(ckv_taken, 1)
                    nc.scalar.activation(vcmp[0:15, :, :], ps[3][0:15, 0:128], ACT.Copy).then_inc(ckv_taken, 1)
                if i == 2:
                    act.wait_ge(cshifted, 1)
                    nc.scalar.activation(pc[:, :, 0:15], pc[:, :, 0:15], ACT.Exp, scale=-1.0).then_inc(cprobs, 1)
                if 6 <= i < 10:
                    c = i - 6
                    act.wait_ge(cprobsT, c + 1)
                    nc.scalar.activation(pcT[c][0:15, :, :], ps[2 + c % 2][0:15, :].rearrange("p (a b) -> p a b", a=2),
                                         ACT.Copy).then_inc(cprobsT_sb, 1)

            soft(*EVEN, between=compressed)
            act.dma_start(fmask[:, :], fox_mask).then_inc(mask_landed, 16)
            outputs(EVEN[1])
            advance(FIRST["out_even"] + 4 + 2)
            norm("mlp0")
            turn("mlp0", gain=pc_("mlp0", KT))
            mlp("mlp0")
            advance(FIRST["mlp0"] + 2 * FF1 + 2)
            norm("mix1")
            turn("mix1", gain=pc_("mix1", KT))

            def forget():
                act.wait_ge(fz_taken, 1)
                chain(nc.scalar.activation(fz[:, 2, :], fz[:, 1, :], ACT.Exp))
                nc.scalar.activation(fz[:, 3, :], fz[:, 2, :], ACT.Ln, bias=1.0).then_inc(fz_exp, 1)

            features("qk_fox", 4, after={3: forget})
            values("fox")
            soft(*FOX)
            outputs(FOX[1])
            advance(FIRST["out_fox"] + 4 + 2)
            norm("mlp1")
            turn("mlp1", gain=pc_("mlp1", KT))
            mlp("mlp1")
            act.wait_ge(ada_step, ADA_STEPS)
            act.dma_start(row[:, :], final_norm.partition_broadcast(P)).then_inc(row_landed, 16)
            advance(FIRST["mlp1"] + 2 * FF1 + 2)
            norm("final")
            norm("gf1")
            take_gate(0, (4, 5))
            act.wait_ge(gain_ready, 2)
            act.dma_start(dil_b, dil_bias).then_inc(dil_landed, 16)
            act.dma_start(poolm, pool_mat).then_inc(dil_landed, 16)
            turn("gf1", gain=gainc[:, 0:KT], shift=modc[:, 0:KT])
            act.dma_start(row[:, :], g_final.partition_broadcast(P)).then_inc(row_landed, 16)
            glu("glu0")
            advance(FIRST["glu0"] + 3 * FF2 + 2)
            norm("gmix")
            turn("gmix", gain=gainc[:, KT:2 * KT], shift=modc[:, 3 * KT:4 * KT])
            features("qk_dil", 2)
            advance(FIRST["uv_dil"] + 4 + 2)
            for t in range(TT):
                act.wait_ge(unit_used, FIRST["uv_dil"] + 4)
                nc.scalar.activation(u_rows[:, t, :], ps[2 * t][:, :], ACT.Copy).then_inc(pooled_taken, 1)
            values("dil")

            def pool_and_gates(i):
                i -= DIL[0]
                if i in (0, 1):
                    act.wait_ge(pooled_done, i + 1)
                    nc.scalar.activation(pooledT[:, 2 * i:2 * i + 2, :], ps[i][:, :], ACT.Copy).then_inc(pooled_taken, 1)
                if i in (2, 3):
                    c = i - 2
                    act.wait_ge(bank_turned, BANK["pooled"] + c + 1)
                    for k in range(2):
                        ins = nc.scalar.activation(pooled_y[:, c, k * T:(k + 1) * T], ps[c][:, k * T:(k + 1) * T],
                                                   ACT.Identity, scale=pc_("pool_scale", 1, 2 * c + k))
                    ins.then_inc(pooled_taken, 1)
                if i in (5, 7):
                    take_gate((i - 3) // 2, (0, 1))

            soft(*DIL, between=pool_and_gates)
            act.wait_ge(pooled_taken, 6)
            outputs(DIL[1], pooled=True)
            advance(FIRST["out_dil"] + 4 + 2)
            norm("gf2")
            turn("gf2", gain=gainc[:, 2 * KT:3 * KT], shift=modc[:, 6 * KT:7 * KT])
            glu("glu1")
            norm("last")

        @block.vector
        def _(dve):
            steps = [0]

            def chain(ins):
                steps[0] += 1
                ins.then_inc(dve_step, 1)
                dve.wait_ge(dve_step, steps[0])

            def take_rest(u, slot):
                dve.wait_ge(hi_ready, u + 1)
                nc.vector.tensor_tensor(w_lo[:, slot, :], raw[:, slot, :], w_hi[:, slot, :].bitcast(F32),
                                        ALU.subtract).then_inc(lo_ready, 1)

            sent = [0]

            def advance(upto):
                while sent[0] < min(upto, N_UNITS):
                    take_rest(sent[0], sent[0] % RING)
                    sent[0] += 1

            def norm(name, sums=None, gate=None, gain=None, dst=None, done=None):
                n = NORM[name]

                def add(t, k):
                    if sums is None:
                        return
                    if (t, k) == (1, 1):
                        dve.wait_ge(unit_used, FIRST[sums] + dict(PHASES)[sums])
                    else:
                        dve.wait_ge(sums_done, SUMS[sums] + 2 * t + k + 1)
                    half = slice(512 * k, 512 * k + 512)
                    to = h[:, t, half]
                    if gate is None:
                        nc.vector.tensor_tensor(to, ps[2 * t + k][:, :], to, ALU.add).then_inc(h_ready, 1)
                    else:
                        chain(nc.vector.tensor_tensor(tok[:, t, half], ps[2 * t + k][:, :], gate[:, half], ALU.mult))
                        nc.vector.tensor_tensor(to, to, tok[:, t, half], ALU.add).then_inc(h_ready, 1)

                def mean(t):
                    dve.wait_ge(sumsq, 2 * n + 2 * t + 2)
                    nc.vector.tensor_scalar(stat[:, 2, t:t + 1], stat[:, 0, t:t + 1], stat[:, 1, t:t + 1], EPS[name],
                                            ALU.add, ALU.add).then_inc(mean_ready, 1)

                def root(t):
                    dve.wait_ge(root_ready, n + t + 1)
                    v, y, b = stat[:, 2, t:t + 1], stat[:, 5, t:t + 1], stat[:, 6, t:t + 1]
                    chain(nc.vector.reciprocal(y, stat[:, 3, t:t + 1]))
                    chain(nc.vector.scalar_tensor_tensor(out=b, in0=v, scalar=y, in1=y, op0=ALU.mult, op1=ALU.mult))
                    chain(nc.vector.tensor_scalar(b, b, -0.5, 1.5, ALU.mult, ALU.add))
                    if gain is not None:
                        chain(nc.vector.tensor_tensor(y, y, b, ALU.mult))

                def scale(t):
                    y, b = stat[:, 5, t:t + 1], stat[:, 6, t:t + 1]
                    if gain is None:
                        for k in range(2):
                            half = slice(512 * k, 512 * k + 512)
                            nc.vector.tensor_scalar(tok[:, t, half], h[:, t, half], b, y, ALU.mult, ALU.mult).then_inc(rows_scaled, 1)
                    else:
                        nc.vector.scalar_tensor_tensor(out=dst[:, t, :], in0=h[:, t, :], scalar=y, in1=gain,
                                                       op0=ALU.mult, op1=ALU.mult).then_inc(*done)

                add(0, 0)
                add(0, 1)
                add(1, 0)
                mean(0)
                root(0)
                add(1, 1)
                scale(0)
                mean(1)
                root(1)
                scale(1)

            def turn(name, gain=None):
                n = TURN[name]
                for c in range(4):
                    dve.wait_ge(act_high, n + c + 1)
                    if gain is None:
                        src, tiles = shifted[:, c % 2, :].rearrange("p (a b) -> p a b", a=2), slice(2 * c, 2 * c + 2)
                        chain(nc.vector.tensor_copy(a_hi[:, tiles, :], src))
                        ins = nc.vector.tensor_tensor(a_lo[:, tiles, :], src, a_hi[:, tiles, :].bitcast(F32), ALU.subtract)
                    else:
                        for kt in (2 * c, 2 * c + 1):
                            ins = nc.vector.scalar_tensor_tensor(out=a_lo[:, kt, :], in0=ps[4 + c][:, (kt % 2) * T:(kt % 2 + 1) * T],
                                                                 scalar=gain[:, kt:kt + 1], in1=a_hi[:, kt, :].bitcast(F32),
                                                                 op0=ALU.mult, op1=ALU.subtract)
                    ins.then_inc(act_split, 1)

            def outputs(name, pooled=False):
                n = TURN[name]
                for c in range(4):
                    dve.wait_ge(act_high, n + c + 1)
                    src = pooled_y[:, c, :] if pooled and c < 2 else ps[c][:, :]
                    nc.vector.tensor_tensor(a_lo[:, 2 * c:2 * c + 2, :], src.rearrange("p (a b) -> p a b", a=2),
                                            a_hi[:, 2 * c:2 * c + 2, :].bitcast(F32), ALU.subtract).then_inc(act_split, 1)

            def stack(j, tile, scale, keys):
                for b in range(2):
                    rows_ = slice(64 * b, 64 * b + 64)
                    src = ps[4 + j % 4][rows_, :].rearrange("p (a b) -> p a b", a=2)
                    hi = (k_two if keys else q_two)[rows_, tile:tile + 2, b, :]
                    dst = k_lo[rows_, tile:tile + 2, :] if keys else q_two[64 * (1 - b):64 * (1 - b) + 64, tile:tile + 2, b, :]
                    ins = nc.vector.scalar_tensor_tensor(out=dst, in0=src, scalar=scale, in1=hi.bitcast(F32),
                                                         op0=ALU.mult, op1=ALU.subtract)
                ins.then_inc(feat_taken, 1)

            def features(name, n, after={}):
                u0 = FIRST[name]
                for j in range(2 * n):
                    advance(u0 + j + RING)
                    dve.wait_ge(feat_hi, f_hi[name] + j + 1)
                    stack(j, 2 * (j % n), -0.125 if j < n else 1.0, j >= n)
                    if j in after:
                        after[j]()

            f_hi = {"qk_moba": 0, "q_nsa": 4, "qk_fox": 7, "qk_dil": 15}

            def values(kind):
                last = FIRST[V_PHASE[kind]] + 4
                advance(last + 2)
                dve.wait_ge(unit_used, last)
                for part in range(2):
                    for t in range(TT):
                        nc.vector.memset(v_cols(kind, part, t, HD, [[PAIR, 8 if kind == "fox" else 4], [1, HD]]).bitcast(F32), 0.0)
                        if kind == "even":
                            nc.vector.memset(v_cols(kind, part, t, NSA_V, [[2 * HD, 5], [1, HD]]).bitcast(F32), 0.0)
                for k, (t, bank, w, c0, counts, form, sizes) in enumerate(value_moves(kind)):
                    dve.wait_ge(val_hi, V_BEFORE[kind] + k + 1)
                    nc.vector.tensor_tensor(v_cols(kind, 1, t, c0, counts), ps[bank][:, 0:w].rearrange(form, **sizes),
                                            v_cols(kind, 0, t, c0, counts).bitcast(F32), ALU.subtract).then_inc(values_taken, 1)

            def heads_(first, last, between=None):
                for i in range(first, last + ROUND_LAG):
                    if i < last:
                        k, bias = heads[i][0], heads[i][5]
                        dve.wait_ge(scores_done, i + 1)
                        if i >= 2:
                            dve.wait_ge(probs_ready, i - 1)
                        for t, lo, hi in ((1, 0, 256), (0, 256, 384)):
                            kk = k + 8 * t
                            ins = nc.vector.tensor_tensor_reduce(
                                logit[:, i % 2, lo:hi], ps[6 + i % 2][:, lo:hi], bias[:, 256 - (hi - lo):256],
                                1.0, 4 * BIG, ALU.add, ALU.min, low[:, kk:kk + 1])
                        ins.then_inc(logits_ready, 1)
                    j = i - SCALE_LAG
                    if first <= j < last:
                        k, gate = heads[j][0], heads[j][6]
                        w, d = wgt[:, k:k + 9:8], den[:, k:k + 9:8]
                        dve.wait_ge(probs_ready, j + 1)
                        if gate is None:
                            nc.vector.reciprocal(w, d).then_inc(weight_ready, 1)
                        else:
                            chain(nc.vector.tensor_tensor(w, gate, d, ALU.mult))
                            nc.vector.reciprocal(w, w).then_inc(weight_ready, 1)
                    m = i - ROUND_LAG
                    if m >= first:
                        dve.wait_ge(probsT_hi, m + 1)
                        nc.vector.tensor_tensor(probT_lo[:, m % 2, :], ps[4 + m % 2][:, 0:SW], probT_hi[:, m % 2, :].bitcast(F32),
                                                ALU.subtract).then_inc(probsT_ready, 1)
                    if first <= j < last:
                        dve.wait_ge(weight_ready, j + 1)
                        for t, lo, hi in ((1, 0, 256), (0, 256, 384)):
                            kk = heads[j][0] + 8 * t
                            p_ = prob[:, j % 4, lo:hi]
                            ins = nc.vector.tensor_scalar(p_, p_, wgt[:, kk:kk + 1], None, ALU.mult)
                        ins.then_inc(probs_scaled, 1)
                    if between:
                        between(i)

            def modulation(j, name):
                dve.wait_ge(mod_done, j + 1)
                k = 3 * j * KT
                chain(nc.vector.tensor_copy(modc[:, k:k + 2 * KT], ps[MOD_BANK[j]][:, k:k + 2 * KT]))
                g = gainc[:, KT * j:KT * j + KT]
                chain(nc.vector.tensor_scalar(g, modc[:, k + KT:k + 2 * KT], 1.0, None, ALU.add))
                nc.vector.tensor_tensor(g, g, pc_(name, KT), ALU.mult).then_inc(gain_ready, 1)

            def mlp(name):
                u0 = FIRST[name]
                f0, x0 = feat_before[name], hid_before[name]
                advance(u0 + RING)

                def hidden(slot, f, x):
                    dve.wait_ge(feat_taken, f + 1)
                    if not isinstance(x, int) or x > 0:
                        dve.wait_ge(hid_ready, x * 3)
                    src = hid_act[:, slot, :]
                    nc.vector.tensor_tensor(hid_f, src, src, ALU.mult).then_inc(hid_ready, 1)
                    dve.wait_ge(hid_ready, x * 3 + 1)
                    nc.vector.tensor_copy(hid_hi[:, slot, :], hid_f).then_inc(hid_ready, 1)
                    dve.wait_ge(hid_ready, x * 3 + 2)
                    nc.vector.tensor_tensor(hid_lo[:, slot, :], hid_f, hid_hi[:, slot, :].bitcast(F32),
                                            ALU.subtract).then_inc(hid_ready, 1)

                hidden(0, f0, x0)
                with dve.Fori(0, (FF1 - 1) // 3) as i:
                    for j in range(3):
                        a = u0 + 1 + 2 * j
                        take_rest(i * 6 + (a + 2), (a + 2) % RING)
                        hidden((j + 1) % 3, i * 3 + (f0 + j + 1), i * 3 + (x0 + j + 1))
                        take_rest(i * 6 + (a + 3), (a + 3) % RING)
                sent[0] = u0 + 2 * FF1 - 1 + 2

            def glu(name):
                u0 = FIRST[name]
                f0, x0 = feat_before[name], hid_before[name]
                last = name == "glu1"
                advance(u0 + RING + 1)

                def hidden(slot, f, x, u):
                    dve.wait_ge(unit_used, u + 1)
                    dve.wait_ge(feat_taken, f + 1)
                    dve.wait_ge(hid_ready, x * 3)
                    nc.vector.tensor_tensor(hid_f, hid_act[:, slot, :], ps[5 + 2 * slot][:, :], ALU.mult).then_inc(hid_ready, 1)
                    dve.wait_ge(hid_ready, x * 3 + 1)
                    nc.vector.tensor_copy(hid_hi[:, slot, :], hid_f).then_inc(hid_ready, 1)
                    dve.wait_ge(hid_ready, x * 3 + 2)
                    nc.vector.tensor_tensor(hid_lo[:, slot, :], hid_f, hid_hi[:, slot, :].bitcast(F32),
                                            ALU.subtract).then_inc(hid_ready, 1)

                hidden(0, f0, x0, u0 + 1)

                def block_(i, j):
                    a = u0 + 2 + 3 * j
                    if i is None:
                        advance(a + 3)
                        hidden((j + 1) % 2, f0 + j + 1, x0 + j + 1, a + 1)
                        advance(a + 5)
                    else:
                        take_rest(i * 6 + (a + 2), (a + 2) % RING)
                        hidden((j + 1) % 2, i * 2 + (f0 + j + 1), i * 2 + (x0 + j + 1), i * 6 + (a + 1))
                        take_rest(i * 6 + (a + 3), (a + 3) % RING)
                        take_rest(i * 6 + (a + 4), (a + 4) % RING)

                n_loop = (FF2 - 1) // 2 - (1 if last else 0)
                with dve.Fori(0, n_loop) as i:
                    block_(i, 0)
                    block_(i, 1)
                sent[0] = u0 + 2 + 6 * n_loop + 2
                if last:
                    block_(None, 2 * n_loop)
                    block_(None, 2 * n_loop + 1)

            nc.vector.memset(kc[:, :, :, 15:16].bitcast(F32), 0.0)
            chain(nc.vector.memset(stat[:, 9, :], 1.0))
            norm("mix0")
            advance(2)
            dve.wait_ge(cbias_done, 1)
            late = ps[2][:, 0:8 * N_CMP].rearrange("p (n c) -> p c n", n=N_CMP)
            nc.vector.memset(cmp_bias[:, 0:8, 7:15], BIG)
            nc.vector.tensor_copy(cmp_bias[:, 0:8, 0:7], late[:, :, 8:15])
            nc.vector.tensor_copy(cmp_bias[:, 8:16, 0:15], late).then_inc(cbias_taken, 1)
            turn("mix0", gain=pc_("mix0", KT))
            features("qk_moba", 2)
            for j in range(3):
                advance(FIRST["q_nsa"] + j + RING)
                dve.wait_ge(feat_hi, f_hi["q_nsa"] + j + 1)
                stack(j, 4 + 2 * (j % 2), -0.125 if j < 2 else 1.0, j == 2)
            advance(FIRST["q_nsa"] + 3 + RING)
            dve.wait_ge(feat_taken, feat_before["q_nsa"] + 4)
            for v in range(2):
                pos = pc_("pos", 16, 16 * v)
                for g in range(2):
                    src = bass.AP(work, v * 512 + g * T, [list(pair[:, v, g, :].ap[0]), [2, 16], [16, 15]])
                    dst = blk[:, v, :, 15 * g:15 * g + 15]
                    chain(nc.vector.tensor_tensor(dst, src, pos.unsqueeze(2).to_broadcast([P, 16, 15]), ALU.add))
                chain(nc.vector.tensor_copy(blk_hi[:, v], blk[:, v]))
                nc.vector.tensor_tensor(blk_lo[:, v], blk[:, v], blk_hi[:, v].bitcast(F32), ALU.subtract).then_inc(blocks_ready, 1)
            values("even")
            dve.wait_ge(gates_exp, 1)
            nc.vector.tensor_scalar(inv_gates[:, :, :], gates_e[:, :, :], 1.0, None, ALU.add).then_inc(dve_step, 1)
            steps[0] += 1
            advance(FIRST["cmp"] + 4 + 2)

            def compressed(i):
                if i == 0:
                    dve.wait_ge(ckv_taken, 2)
                    nc.vector.tensor_tensor(kc[:, :, 1, 0:15], ps[2][:, 0:32].rearrange("p (g n) -> p g n", g=2)[:, :, 0:15],
                                            kc[:, :, 0, 0:15].bitcast(F32), ALU.subtract).then_inc(ckv_taken, 1)
                if i == 1:
                    dve.wait_ge(cscores, 1)
                    s4 = ps[2][:, :].rearrange("p (a c b) -> p a c b", a=16, c=2)
                    for part in range(2):
                        chain(nc.vector.tensor_tensor(pc[:, :, 0:15], s4[:, :, part, 0:15], pc[:, :, 0:15], ALU.add))
                    chain(nc.vector.tensor_reduce(low[:, 0:16], pc[:, :, 0:15], AX_X, ALU.min))
                    nc.vector.tensor_tensor(pc[:, :, 0:15], pc[:, :, 0:15], low[:, 0:16].unsqueeze(2).to_broadcast([P, 16, 15]),
                                            ALU.subtract).then_inc(cshifted, 1)
                if i == 3:
                    dve.wait_ge(cprobs, 1)
                    chain(nc.vector.tensor_reduce(den[:, 0:16], pc[:, :, 0:15], AX_X, ALU.add))
                    w0 = wgt[:, 0:16].rearrange("p (t h) -> p t h", t=2)
                    d0 = den[:, 0:16].rearrange("p (t h) -> p t h", t=2)
                    chain(nc.vector.tensor_tensor(w0, inv_gates[:, :, :].rearrange("p t (h b) -> p t h b", b=3)[:, :, :, 0], d0, ALU.mult))
                    chain(nc.vector.reciprocal(w0, w0))
                    for t in range(TT):
                        nc.vector.tensor_scalar(w0[:, t, :], w0[:, t, :], pc_("row_ok", 1, t), None, ALU.mult).then_inc(dve_step, 1)
                    steps[0] += 2
                    dve.wait_ge(dve_step, steps[0])
                    nc.vector.tensor_tensor(pc[:, :, 0:15], pc[:, :, 0:15], wgt[:, 0:16].unsqueeze(2).to_broadcast([P, 16, 15]),
                                            ALU.mult).then_inc(cscaled, 1)

            dve.wait_ge(rel_landed, 16 * 16)
            heads_(*EVEN, between=compressed)
            outputs("even_out")
            advance(FIRST["out_even"] + 4 + 1)
            norm("mlp0", sums="out_even")
            turn("mlp0", gain=pc_("mlp0", KT))
            mlp("mlp0")
            norm("mix1", sums="mlp0")
            turn("mix1", gain=pc_("mix1", KT))
            nc.vector.tensor_copy(wf_hi[:, :, :], wf).then_inc(wf_ready, 1)
            dve.wait_ge(wf_ready, 1)
            nc.vector.tensor_tensor(wf_lo[:, :, :], wf, wf_hi[:, :, :].bitcast(F32), ALU.subtract).then_inc(wf_ready, 1)

            def forget_logits():
                dve.wait_ge(fz_done, 1)
                chain(nc.vector.tensor_scalar(fz[:, 0, :], ps[0][0:16, 0:T], bfor[:, 0:1], None, ALU.add))
                chain(nc.vector.tensor_scalar(fz[:, 1, :], fz[:, 0, :], -1.0, None, ALU.mult))
                nc.vector.tensor_tensor(fz[:, 1, :], fz[:, 1, :], fz[:, 0, :], ALU.min).then_inc(fz_taken, 1)

            def forget_sums():
                dve.wait_ge(fz_exp, 1)
                chain(nc.vector.tensor_scalar(fz[:, 0, :], fz[:, 0, :], 0.0, None, ALU.min))
                chain(nc.vector.tensor_tensor(fz[:, 0, :], fz[:, 0, :], fz[:, 3, :], ALU.subtract))
                chain(nc.vector.memset(fz[:, 1, :], 1.0))
                chain(nc.vector.tensor_tensor_scan(cum[:, :], fz[:, 1, :], fz[:, 0, :], 0.0, ALU.mult, ALU.add))
                chain(nc.vector.memset(cum_r[:, :].bitcast(F32), 0.0))
                chain(nc.vector.memset(pick_r[:, :, :].bitcast(F32), 0.0))
                for r in (0, 64):
                    chain(nc.vector.tensor_copy(cum_r[r:r + 16, :], cum[:, :]))
                    nc.vector.tensor_tensor(cum_r[r + 32:r + 48, :], cum[:, :], cum_r[0:16, :].bitcast(F32), ALU.subtract).then_inc(cum_ready, 1)
                    for part in (0, 32):
                        for k, sign in enumerate((1.0, -1.0)):
                            nc.vector.tensor_scalar(pick_r[r + part:r + part + 16, k, :], ident[0:16, 0:16], sign, None,
                                                    ALU.mult).then_inc(cum_ready, 1)

            features("qk_fox", 4, after={2: forget_logits, 4: forget_sums})
            values("fox")
            dve.wait_ge(mask_landed, 16)
            heads_(*FOX)
            outputs("fox_out")
            advance(FIRST["out_fox"] + 4 + 1)
            norm("mlp1", sums="out_fox")
            turn("mlp1", gain=pc_("mlp1", KT))
            mlp("mlp1")
            dve.wait_ge(row_landed, 16)
            norm("final", sums="mlp1", gain=row[:, :], dst=h, done=(h_ready, 2))
            norm("gf1")
            for j, name in enumerate(("gf1", "gmix")):
                modulation(j, name)
            turn("gf1")
            glu("glu0")
            dve.wait_ge(gate_taken, 2)
            norm("gmix", sums="glu0", gate=acc_ada[:, 2 * D:3 * D])
            turn("gmix")
            features("qk_dil", 2)
            values("dil")
            dve.wait_ge(dil_landed, 32)
            heads_(*DIL, between=lambda i: modulation(2, "gf2") if i == DIL[0] + DIL_MOD else None)
            outputs("dil_out", pooled=True)
            advance(FIRST["out_dil"] + 4 + 1)
            dve.wait_ge(gate_taken, 6)
            norm("gf2", sums="out_dil", gate=acc_ada[:, 5 * D:6 * D])
            turn("gf2")
            glu("glu1")
            dve.wait_ge(row_landed, 32)
            norm("last", sums="glu1", gate=acc_ada[:, 8 * D:9 * D], gain=row[:, :], dst=tok, done=(out_ready, 1))

        @block.tensor
        def _(pe):
            def three(dst, l_hi, l_lo, r_hi, r_lo, start, stop):
                nc.tensor.matmul(dst, l_hi, r_lo, start=start, stop=False)
                nc.tensor.matmul(dst, l_lo, r_hi, start=False, stop=False)
                return nc.tensor.matmul(dst, l_hi, r_hi, start=False, stop=stop)

            def feature_unit(u, slot, bank, wait_split=None):
                pe.wait_ge(lo_ready, u + 1)
                wh = w_hi[:, slot, :].rearrange("p (k c) -> p k c", k=KT)
                wl = w_lo[:, slot, :].rearrange("p (k c) -> p k c", k=KT)
                for nt in range(2):
                    for k in range(KT):
                        if wait_split is not None and nt == 0 and k % 2 == 0:
                            pe.wait_ge(act_split, wait_split + k // 2 + 1)
                        cols_ = slice(nt * P, nt * P + P)
                        ins = three(ps[bank][:, nt * T:(nt + 1) * T], wh[:, k, cols_], wl[:, k, cols_],
                                    a_hi[:, k, :], a_lo[:, k, :], k == 0, k == KT - 1)
                ins.then_inc(unit_used, 1)

            def row_unit(u, slot, l_hi, l_lo, width, start, stop, sums=False):
                pe.wait_ge(lo_ready, u + 1)
                wh = w_hi[:, slot, 0:2 * width].rearrange("p (k c) -> p k c", k=2)
                wl = w_lo[:, slot, 0:2 * width].rearrange("p (k c) -> p k c", k=2)
                banks = [(t, n) for t in range(TT) for n in range(2)]
                order = [(k, t, n) for t, n in banks for k in range(2)] if sums else [(k, t, n) for k in range(2) for t, n in banks]
                for k, t, n in order:
                    w = min(512, width - 512 * n)
                    sl = slice(512 * n, 512 * n + w)
                    ins = three(ps[2 * t + n][:, 0:w], l_hi(k)[:, t * P:(t + 1) * P], l_lo(k)[:, t * P:(t + 1) * P],
                                wh[:, k, sl], wl[:, k, sl], start and k == 0, stop and k == 1)
                    if sums and k == 1 and (t, n) != (1, 1):
                        ins.then_inc(sums_done, 1)
                ins.then_inc(unit_used, 1)

            def rows_phase(name, width=D, wait_split=None):
                u0 = FIRST[name]
                for j in range(4):
                    if wait_split is not None and j == 0:
                        pe.wait_ge(act_split, wait_split + 4)
                    row_unit(u0 + j, (u0 + j) % RING, lambda k: a_hi[:, 2 * j + k, :], lambda k: a_lo[:, 2 * j + k, :],
                             width, j == 0, j == 3, sums=name.startswith("out") and j == 3)

            def features_phase(name, n, wait_split=None, after={}):
                u0, f0 = FIRST[name], feat_before[name]
                for j in range(n):
                    if j >= 4 or name == "q_nsa":
                        pe.wait_ge(feat_taken, f0 + j - 3)
                    feature_unit(u0 + j, (u0 + j) % RING, 4 + j % 4, wait_split if j == 0 else None)
                    if j in after:
                        after[j]()

            def norm_turn(name):
                n = 4 * TURNED.index(name)
                for t in range(TT):
                    for c in range(4):
                        if c % 2 == 0:
                            pe.wait_ge(rows_scaled, n + 2 * t + c // 2 + 1)
                        for k in range(2):
                            kt = 2 * c + k
                            ins = nc.tensor.transpose(ps[4 + c][:, (2 * k + t) * P:(2 * k + t + 1) * P],
                                                      tok[:, t, kt * P:(kt + 1) * P], ident)
                        if t == TT - 1:
                            ins.then_inc(bank_turned, 1)

            def modulation(j):
                for k in range(3 * j * KT, (3 * j + 2) * KT):
                    ins = nc.tensor.matmul(ps[MOD_BANK[j]][:, k:k + 1], acc_ada[:, k * P:(k + 1) * P], ones[:, 0:1], start=True, stop=True)
                ins.then_inc(mod_done, 1)

            def gate_rows(j, banks):
                v = 3 * j + ADA_GATE
                for n in range(2):
                    nc.tensor.matmul(ps[banks[n]][:, :], ones[:, :], acc_ada[:, v * D + 512 * n:v * D + 512 * n + 512],
                                     start=True, stop=True).then_inc(gate_done, 1)

            def standing(kind, part, t, v0):
                return v_cols(kind, part, t, v0, [[1, P]])

            WARM = (20, 20)

            def keep_clock(n):
                for _ in range(n):
                    nc.tensor.matmul(ps[5][:, 0:T], q_two[:, 0, 0, 0:P], k_two[:, 0, 0, :], start=True, stop=True)

            def attend(first, last, values, kind, between=None):
                fox = kind == "fox"
                for i in range(first, last + PV_LAG):
                    if i < last:
                        _, qt_, kt_, b = heads[i][:4]
                        if kind != "dil" and first + 1 <= i < first + TURN_LAG:
                            keep_clock(WARM[i - first - 1])
                        if i >= 2:
                            pe.wait_ge(logits_ready, i - 1)
                        bank = ps[6 + i % 2]
                        half = slice(64 * b, 64 * b + 64)
                        for t, lo, w in ((1, 0, 256), (0, 256, 128)):
                            qs = slice(t * P, (t + 1) * P)
                            nc.tensor.matmul(bank[:, lo:lo + w], q_two[:, qt_, b, qs], k_two[:, kt_, b, 0:w], start=True, stop=False)
                            ins = nc.tensor.matmul(bank[:, lo:lo + w], q_two[half, qt_, b, qs], k_lo[half, kt_, 0:w],
                                                   start=False, stop=not fox)
                            if fox:
                                hf = i - first
                                rows_ = slice(64 * b, 64 * b + 48)
                                pick, minus = pick_r[rows_, 0, hf:hf + 1], pick_r[rows_, 1, hf:hf + 1]
                                nc.tensor.matmul(bank[:, lo:lo + w], pick.to_broadcast([48, P]), cum_r[rows_, 0:w],
                                                 start=False, stop=False)
                                ins = nc.tensor.matmul(bank[:, lo:lo + w], cum_r[rows_, qs],
                                                       minus.to_broadcast([48, w]), start=False, stop=True)
                        ins.then_inc(scores_done, 1)
                    if between:
                        between(i)
                    j = i - TURN_LAG
                    if first <= j < last:
                        pe.wait_ge(probs_scaled, j + 1)
                        if j >= 2:
                            pe.wait_ge(probsT_ready, j - 1)
                        for c, src in enumerate((256, 0, 128)):
                            ins = nc.tensor.transpose(ps[4 + j % 2][:, c * P:(c + 1) * P], prob[:, j % 4, src:src + P], ident)
                        ins.then_inc(probsT_done, 1)
                    j = i - PV_LAG
                    if j >= first:
                        closes = j + 1 == last or heads[j + 1][7] != heads[j][7]
                        v0, feat, ob, opens = heads[j][4], heads[j][7], heads[j][8], heads[j][9]
                        if j == first:
                            pe.wait_ge(values_taken, values)
                        c0 = feat % 2 * T
                        bank = ps[feat // 2]
                        if first == EVEN[0] and j >= HEADS and (j - HEADS) % 4 == 0:
                            if j == HEADS:
                                pe.wait_ge(cprobsT_sb, 4)
                            for half in range(2):
                                hh = 2 * (feat - 4) + half
                                nc.tensor.matmul(bank[64 * half:64 * half + 64, c0:c0 + T], vcmp[0:15, hh // 4, :], pcT[hh // 2][0:15, hh % 2, :],
                                                 start=True, stop=False)
                        pe.wait_ge(probsT_ready, j + 1)
                        three(bank[:, c0:c0 + T], standing(kind, 0, 0, v0), standing(kind, 1, 0, v0), probT_hi[:, j % 2, 0:T],
                              probT_lo[:, j % 2, 0:T], opens, False)
                        ins = three(bank[:, c0 + P:c0 + T], standing(kind, 0, 1, v0), standing(kind, 1, 1, v0),
                                    probT_hi[:, j % 2, T:SW], probT_lo[:, j % 2, T:SW], False, closes)
                        ins.then_inc(pv_done, 1)

            TURNED = ["mix0", "mlp0", "mix1", "mlp1", "gf1", "gmix", "gf2"]

            pe.wait_ge(pick_landed, 32)
            pe.wait_ge(pool_step, 2)
            nc.tensor.matmul(ps[0][0:16, 0:REL], relt[:, :], rpick, start=True, stop=True).then_inc(rel_rows, 1)
            pe.wait_ge(cpick_landed, 32)
            for n in range(N_CMP):
                ins = nc.tensor.matmul(ps[2][:, 8 * n:8 * n + 8], cpick[:, n * P:(n + 1) * P], relt[:, 8:16], start=True, stop=True)
            ins.then_inc(cbias_done, 1)
            pe.wait_ge(par_landed, 16)
            norm_turn("mix0")
            features_phase("qk_moba", 4, TURN["mix0"])
            features_phase("q_nsa", 4)
            pe.wait_ge(rel_rows_sb, 1)
            pe.wait_ge(cbias_taken, 1)
            rows_phase("v_even", V1W)
            u0 = FIRST["cmp"]
            for j in range(4):
                v, half = j // 2, j % 2
                u = u0 + j
                pe.wait_ge(lo_ready, u + 1)
                pe.wait_ge(blocks_ready, v + 1)
                pe.wait_ge(feat_taken, 8)
                wh = w_hi[:, u % RING, :].rearrange("p (k c) -> p k c", k=8)
                wl = w_lo[:, u % RING, :].rearrange("p (k c) -> p k c", k=8)
                for k in range(8):
                    ins = three(ps[4 + v][0:30, 0:256], blk_hi[:, v, 8 * half + k, :], blk_lo[:, v, 8 * half + k, :],
                                wh[:, k, :], wl[:, k, :], half == 0 and k == 0, half == 1 and k == 7)
                ins.then_inc(unit_used, 1)
            for v in range(2):
                pe.wait_ge(hidden_rows, v + 1)
                for ht in range(2):
                    ins = nc.tensor.transpose(ps[6][:, 64 * v + 32 * ht:64 * v + 32 * ht + 30], hid30[0:30, v, ht * P:(ht + 1) * P],
                                              ident[0:30, 0:30])
            ins.then_inc(hidden_turned, 1)
            pe.wait_ge(hidc_ready, 1)

            def compressed(i):
                if i == 0:
                    for half in range(2):
                        for g in range(2):
                            for ht in range(2):
                                nc.tensor.matmul(ps[2][64 * half:64 * half + 64, 16 * g:16 * g + 15], cw2[:, 0, ht, :],
                                                 hidc[:, 0, ht, 15 * g:15 * g + 15], start=(ht == 0), stop=(ht == 1))
                    for g in range(2):
                        for ht in range(2):
                            ins = nc.tensor.matmul(ps[3][0:15, 64 * g:64 * g + 64], hidc[:, 1, ht, 15 * g:15 * g + 15], cw2[:, 1, ht, :],
                                                   start=(ht == 0), stop=(ht == 1))
                    ins.then_inc(ckv_done, 1)
                if i == 1:
                    pe.wait_ge(ckv_taken, 3)
                    for t in range(TT):
                        for hh in range(HEADS):
                            k, g = 8 * t + hh, hh // 4
                            q_ = q_two[:, 4 + hh % 4, g, t * P:(t + 1) * P]
                            ins = nc.tensor.matmul(ps[2][:, 32 * k:32 * k + 32], q_, kc[:, g, :, :].rearrange("p a b -> p (a b)"),
                                                   start=True, stop=True)
                    ins.then_inc(cscores, 1)
                if 6 <= i < 10:
                    c = i - 6
                    pe.wait_ge(cscaled, 1)
                    if c >= 2:
                        pe.wait_ge(cprobsT_sb, c - 1)
                    for k in range(4):
                        hh, t = 2 * c + k // 2, k % 2
                        ins = nc.tensor.transpose(ps[2 + c % 2][0:15, k * P:(k + 1) * P], pc[:, 8 * t + hh, 0:15], ident)
                    ins.then_inc(cprobsT, 1)

            pe.wait_ge(values_taken, 4)
            attend(*EVEN, values=4, kind="even", between=compressed)
            rows_phase("out_even", wait_split=TURN["even_out"])

            def mlp(name):
                u0, f0, x0 = FIRST[name], feat_before[name], hid_before[name]
                feature_unit(u0, u0 % RING, 4, TURN[name])

                def down(u, slot, hs, x, start, stop, sums=False):
                    pe.wait_ge(hid_ready, x * 3 + 3)
                    row_unit(u, slot, lambda k: hid_hi[:, hs, k * T:(k + 1) * T], lambda k: hid_lo[:, hs, k * T:(k + 1) * T],
                             D, start, stop, sums)

                def pair_(i, j, start):
                    a = u0 + 1 + 2 * j
                    e = (lambda k, c: c) if i is None else (lambda k, c: i * k + c)
                    feature_unit(e(6, a), a % RING, 4 + (j + 1) % 3)
                    down(e(6, a + 1), (a + 1) % RING, j % 3, e(3, x0 + j), start, False)

                for j in range(3):
                    pair_(None, j, j == 0)
                with pe.Fori(1, (FF1 - 1) // 3) as i:
                    for j in range(3):
                        pair_(i, j, False)
                u = u0 + 2 * FF1 - 1
                down(u, u % RING, (FF1 - 1) % 3, x0 + FF1 - 1, False, True, sums=True)

            def glu(name):
                u0, f0, x0 = FIRST[name], feat_before[name], hid_before[name]
                feature_unit(u0, u0 % RING, 4, TURN["gf1" if name == "glu0" else "gf2"])
                feature_unit(u0 + 1, (u0 + 1) % RING, 5)

                def down(u, slot, hs, x, start, stop, sums=False):
                    pe.wait_ge(hid_ready, x * 3 + 3)
                    row_unit(u, slot, lambda k: hid_hi[:, hs, k * T:(k + 1) * T], lambda k: hid_lo[:, hs, k * T:(k + 1) * T],
                             D, start, stop, sums)

                def triple(i, j, start):
                    a = u0 + 2 + 3 * j
                    e = (lambda k, c: c) if i is None else (lambda k, c: i * k + c)
                    b = 4 + 2 * ((j + 1) % 2)
                    feature_unit(e(6, a), a % RING, b)
                    feature_unit(e(6, a + 1), (a + 1) % RING, b + 1)
                    down(e(6, a + 2), (a + 2) % RING, j % 2, e(2, x0 + j), start, False)

                for j in range(2):
                    triple(None, j, j == 0)
                with pe.Fori(1, (FF2 - 1) // 2) as i:
                    for j in range(2):
                        triple(i, j, False)
                u = u0 + 3 * FF2 - 1
                down(u, u % RING, (FF2 - 1) % 2, x0 + FF2 - 1, False, True, sums=True)

            norm_turn("mlp0")
            mlp("mlp0")
            norm_turn("mix1")

            def forget():
                pe.wait_ge(wf_ready, 2)
                for k in range(KT):
                    ins = three(ps[0][0:16, 0:T], wf_hi[:, k, :], wf_lo[:, k, :], a_hi[:, k, :], a_lo[:, k, :], k == 0, k == KT - 1)
                ins.then_inc(fz_done, 1)

            features_phase("qk_fox", 8, TURN["mix1"], after={1: forget})
            pe.wait_ge(fz_taken, 1)
            rows_phase("v_fox")
            pe.wait_ge(feat_taken, feat_before["qk_fox"] + 8)
            pe.wait_ge(cum_ready, 10)
            attend(*FOX, values=8, kind="fox")
            rows_phase("out_fox", wait_split=TURN["fox_out"])
            norm_turn("mlp1")
            mlp("mlp1")
            pe.wait_ge(ada_step, ADA_STEPS)
            modulation(0)
            modulation(1)
            gate_rows(0, (4, 5))
            pe.wait_ge(gate_taken, 2)
            pe.wait_ge(gain_ready, 2)
            norm_turn("gf1")
            glu("glu0")
            norm_turn("gmix")
            features_phase("qk_dil", 4, TURN["gmix"])
            rows_phase("uv_dil")
            pe.wait_ge(feat_taken, feat_before["qk_dil"] + 4)

            def pool_and_modulation(i):
                i -= DIL[0]
                if i == 0:
                    pe.wait_ge(dil_landed, 32)
                    pe.wait_ge(pooled_taken, 2)
                    pe.wait_ge(values_taken, 10)
                if i in (0, 1):
                    for g in (2 * i, 2 * i + 1):
                        for k in range(TT):
                            ins = nc.tensor.matmul(ps[i][:, (g % 2) * T:(g % 2 + 1) * T], u_rows[:, k, g * P:(g + 1) * P],
                                                   poolm[:, g, k, :], start=(k == 0), stop=(k == 1))
                    ins.then_inc(pooled_done, 1)
                if i in (2, 3):
                    c = i - 2
                    pe.wait_ge(pooled_taken, c + 3)
                    for g in (2 * c, 2 * c + 1):
                        ins = nc.tensor.matmul(ps[c][:, (g % 2) * T:(g % 2 + 1) * T], w_pool[:, g, :], pooledT[:, g, :],
                                               start=True, stop=True)
                    ins.then_inc(bank_turned, 1)
                if i == 4:
                    pe.wait_ge(pooled_taken, 6)
                    gate_rows(1, (0, 1))
                if i == 6:
                    pe.wait_ge(gate_taken, 4)
                    gate_rows(2, (0, 1))
                if i == 7:
                    pe.wait_ge(gate_taken, 5)
                    modulation(2)

            attend(*DIL, values=10, kind="dil", between=pool_and_modulation)
            rows_phase("out_dil", wait_split=TURN["dil_out"])
            norm_turn("gf2")
            glu("glu1")




def rel_buckets(d):
    n = np.maximum(d, 0)
    nf = np.maximum(n, 1).astype(np.float32)
    large = 16 + (np.log(nf / np.float32(16)) / np.float32(np.log(64.0)) * np.float32(16)).astype(np.int32)
    return np.where(n < 16, n, np.minimum(large, 31))


def shape_constants():
    f = np.float32

    def pick(d):
        m = np.zeros((33, d.size), f)
        b = rel_buckets(d)
        m[b, np.arange(d.size)] = -1.0
        m[0:32, d < 0] = 0.0
        m[32, d < 0] = BIG
        return m

    rel_pick = pick(255 - np.arange(REL))
    q = np.arange(P)
    cmp_pick = np.concatenate([pick(P + q - (16 * n + 31)) for n in range(N_CMP)], axis=1)
    dist = P + q[:, None] - np.arange(T)[None, :]
    fox_mask = np.where(dist < 0, BIG, 0.0).astype(f)
    count = (dist <= 128).astype(f) + (dist % 4 == 0) + (dist % 16 == 0)
    ok = (dist >= 0) & (count > 0)
    logs = np.log(np.where(ok, count, 1.0))
    dil = np.stack([np.where(ok, dist * 2.0 ** -(hh + 1) - logs, BIG) for hh in range(HEADS)], axis=1).astype(f)
    tt = np.arange(T)
    pool = np.zeros((P, 4, TT, T), f)
    for g, w in enumerate((2, 4, 8, 16)):
        m = ((tt[:, None] <= tt[None, :]) & (tt[:, None] > tt[None, :] - w)) / np.minimum(tt[None, :] + 1, w)
        m = (m - np.eye(T)).astype(f)
        pool[:, g] = m.reshape(TT, P, T).transpose(1, 0, 2)
    row_ok = (np.arange(T) >= 31).astype(f).reshape(TT, P).T
    return rel_pick, cmp_pick, fox_mask, dil, pool, row_ok


def lay_out(a):
    def feats(w):
        n = w.shape[1] // T
        return w.reshape(KT, P, n, T).transpose(2, 1, 0, 3).reshape(n, P, UNIT)

    def rows(w):
        n, width = w.shape[0] // T, w.shape[1]
        u = w.reshape(n, 2, P, width).transpose(0, 2, 1, 3).reshape(n, P, 2 * width)
        if 2 * width < UNIT:
            u = np.concatenate([u, np.zeros((n, P, UNIT - 2 * width), u.dtype)], axis=2)
        return u

    def mlp(w1, w2):
        first, second = feats(w1), rows(w2)
        order = [first[0:1]]
        for j in range(FF1 - 1):
            order += [first[j + 1:j + 2], second[j:j + 1]]
        return order + [second[FF1 - 1:]]

    def glu(wg, wu, wd):
        g, u, d = feats(wg), feats(wu), rows(wd)
        order = [g[0:1], u[0:1]]
        for j in range(FF2 - 1):
            order += [g[j + 1:j + 2], u[j + 1:j + 2], d[j:j + 1]]
        return order + [d[FF2 - 1:]]

    w = a["even_w_in"][0]
    nq = w[:, 1536:2048].reshape(D, 2, 4, HD).transpose(0, 2, 1, 3).reshape(D, 512)
    c = {n: w[:, 2048 + 128 * i:2176 + 128 * i] for i, n in enumerate(("kc", "vc", "ks", "vs", "kw", "vw"))}
    parts = [feats(w[:, 0:1024])]
    parts += [feats(np.concatenate([nq, c["ks"], c["kw"], c["kc"], c["vc"]], axis=1))]
    parts += [rows(np.concatenate([w[:, 1024:1536], c["vs"], c["vw"], w[:, 2816:2840]], axis=1))]
    parts += [feats(a[n][0].reshape(2, 1024, 256).transpose(1, 0, 2).reshape(1024, 512)) for n in ("cmp_k_w1", "cmp_v_w1")]
    parts += [rows(a["even_w_out"][0])]
    parts += mlp(a["mlp_w1"][0], a["mlp_w2"][0])
    wo = a["odd_w_in"][0]
    parts += [feats(wo[:, 0:2048]), rows(wo[:, 2048:3072]), rows(a["odd_w_out"][0])]
    parts += mlp(a["mlp_w1"][1], a["mlp_w2"][1])
    parts += glu(a["w1_gate_2"][0], a["w1_up_2"][0], a["w1_down_2"][0])
    w2 = a["w_in_2"][0]
    parts += [feats(w2[:, 512:1536]), rows(np.concatenate([w2[:, 0:512], w2[:, 1536:2048]], axis=1)), rows(a["w_out_2"][0])]
    parts += glu(a["w2_gate_2"][0], a["w2_up_2"][0], a["w2_down_2"][0])
    stream = np.concatenate(parts, axis=0)
    assert stream.shape == (N_UNITS, P, UNIT)
    n = ADA_W // ADA_PIECE
    ada = a["w_ada_2"][0].reshape(KT, P, n, ADA_PIECE).transpose(2, 0, 1, 3)[::-1].reshape(n * KT, P, ADA_PIECE)

    def col(v):
        return v.reshape(-1, P).T

    rel_pick, cmp_pick, fox_mask, dil, pool, row_ok = shape_constants()
    w2s = np.stack([a[n][0].reshape(2, P, HD) for n in ("cmp_k_w2", "cmp_v_w2")]).transpose(2, 0, 1, 3).reshape(P, 256)
    cols = np.concatenate([
        w2s, col(a["mix_norm"][0]), col(a["mlp_norm"][0]), col(a["mix_norm"][1]), col(a["mlp_norm"][1]),
        col(a["g_ffn1_2"][0]), col(a["g_mix_2"][0]), col(a["g_ffn2_2"][0]), col(a["pool_scale_2"][0]),
        col(a["cmp_pos_k"][0].reshape(-1)), col(a["cmp_pos_v"][0].reshape(-1)), col(a["c_2"][0]), row_ok,
        a["w_pool_2"][0].transpose(1, 0, 2).reshape(P, 512),
        wo[:, 3072:3088].reshape(KT, P, 16).transpose(1, 0, 2).reshape(P, 128), np.eye(P, dtype=np.float32)], axis=1)
    assert cols.shape == (P, N_COLS)
    return {
        "stream": stream, "ada": ada, "cols": cols, "x": a["x"][0], "rel_table": a["rel_bias"],
        "rel_pick": rel_pick, "cmp_pick": cmp_pick, "fox_mask": fox_mask, "dil_bias": dil, "pool_mat": pool,
        "b_ada": a["b_ada_2"], "b_forget": a["odd_b_forget"][0].reshape(16, 1),
        "final_norm": a["final_norm"], "g_final": a["g_final_2"],
    }


def kernel(**inputs):
    import concourse.bacc as bacc
    from concourse.bass_utils import run_bass_kernel_spmd

    arrays = {k: np.ascontiguousarray(v) for k, v in lay_out({k: np.asarray(v) for k, v in inputs.items()}).items()}
    nc = bacc.Bacc("TRN2", target_bir_lowering=False, num_devices=1)
    args = {k: nc.dram_tensor("in_" + k, v.shape, mybir.dt.from_np(v.dtype), kind="ExternalInput").ap() for k, v in arrays.items()}
    out = nc.dram_tensor("out", (T, D), F32, kind="ExternalOutput").ap()
    build(nc, out=out, **args)
    r = run_bass_kernel_spmd(nc, [{"in_" + k: v for k, v in arrays.items()}], core_ids=[0])
    return r.results[0]["out"].reshape(1, T, D)
```
